# Optimizing a Trainium2 kernel written in Bass

```python
import math
import jax, jax.numpy as jnp
from jax import lax
import numpy as np

D_MODEL = 1024
BATCH = 1
SEQ = 1024
DEPTH = 2
DEC_BATCH = 8
DEC_SEQ = 1
PAST_LEN = 4096
PAGE_SIZE = 128

HEAD_DIM = 64
N_A_LAYERS = (DEPTH + 1) // 2
N_C_LAYERS = DEPTH // 2
A_HEADS = 8
A_KV = 2
A_REP = A_HEADS // A_KV
A_Q = A_HEADS * HEAD_DIM
A_KVW = A_KV * HEAD_DIM
A_GATE = 3 * A_HEADS
CMP_LEN = 32
CMP_STRIDE = 16
SEL_BLOCK = 64
SEL_TOPK = 16
WIN_A = 512
NSA_QBLK = 64
FORCE_BONUS = 1000.0
B_WIDTH = D_MODEL // 2
B_GROUP = 16
B_GROUPS = B_WIDTH // B_GROUP
B_STATE = 64
DT_MIN = 1e-3
DT_MAX = 1e-1
IN_A = A_Q + 6 * A_KVW + A_GATE + B_WIDTH
C_HEADS = D_MODEL // HEAD_DIM
C_KV = 2
C_REP = C_HEADS // C_KV
WIN_C = 128
IN_C = (C_HEADS + 2 * C_KV) * HEAD_DIM
NUM_BUCKETS = 32
MAX_DISTANCE = 128
BIAS_HEADS = D_MODEL // HEAD_DIM
D_FF = 2816
CONV_W = 3
EPS = 1e-6

kernel_name = 'hybrid_nsa_s5_swa_convffn_step'

def rms_norm(x, g):
    xf = x.astype(jnp.float32)
    y = xf * lax.rsqrt(jnp.mean(xf * xf, axis=-1, keepdims=True) + EPS)
    return (y * g.astype(jnp.float32)).astype(x.dtype)

def rel_bucket(dist):
    n = jnp.maximum(dist, 0)
    exact = NUM_BUCKETS // 2
    nf = jnp.maximum(n, exact).astype(jnp.float32)
    large = exact + (jnp.log(nf / exact) / math.log(MAX_DISTANCE / exact) * (NUM_BUCKETS - exact)).astype(jnp.int32)
    return jnp.where(n < exact, n, jnp.minimum(large, NUM_BUCKETS - 1))

def masked_softmax(s, mask):
    s = jnp.where(mask, s.astype(jnp.float32), -jnp.inf)
    m = jnp.max(s, axis=-1, keepdims=True)
    m = jnp.where(jnp.isfinite(m), m, 0.0)
    e = jnp.exp(s - m)
    d = jnp.sum(e, axis=-1, keepdims=True)
    return e / jnp.where(d > 0, d, 1.0)

def compress(rows, pos, w1, w2):
    b, t, g, dh = rows.shape
    r = CMP_LEN // CMP_STRIDE
    nch = t // CMP_STRIDE
    chunks = rows[:, :nch * CMP_STRIDE].reshape(b, nch, CMP_STRIDE, g, dh)
    w1b = w1.reshape(r, CMP_STRIDE, dh, w1.shape[-1])
    nc = nch - r + 1
    hid = jnp.einsum('ld,ldh->h', pos, w1.reshape(CMP_LEN, dh, w1.shape[-1]))
    for j in range(r):
        hid = hid + jnp.einsum('bnsgd,sdh->bngh', chunks[:, j:j + nc], w1b[j])
    return jnp.einsum('bngh,hd->bngd', jax.nn.gelu(hid), w2)

def compressed_kv(k_rows, v_rows, cmp_pos, cmp_w1, cmp_w2, k_gain):
    kc = rms_norm(compress(k_rows, cmp_pos[0], cmp_w1[0], cmp_w2[0]), k_gain)
    vc = compress(v_rows, cmp_pos[1], cmp_w1[1], cmp_w2[1])
    c_end = jnp.arange(kc.shape[1]) * CMP_STRIDE + (CMP_LEN - 1)
    return kc, vc, c_end

def nsa_attend(q, q_pos, kc, vc, c_end, n_sel, gather_sel, kw, vw, w_pos, gates, tab):
    scale = HEAD_DIM ** -0.5
    g_n = q.shape[2]
    s_c = jnp.einsum('bqgrd,bngd->bgrqn', q, kc) * scale
    p_c = masked_softmax(s_c, c_end[None, :] <= q_pos[:, None])
    o_c = jnp.einsum('bgrqn,bngd->bqgrd', p_c.astype(vc.dtype), vc)
    s_start = jnp.arange(n_sel) * SEL_BLOCK
    c_start = c_end - (CMP_LEN - 1)
    cover = ((c_start[:, None] < s_start[None, :] + SEL_BLOCK) & (c_end[:, None] >= s_start[None, :])).astype(jnp.float32)
    imp = jnp.einsum('bgrqn,ns->bgqs', p_c, cover)
    qblk = q_pos[:, None] // SEL_BLOCK
    sblk = jnp.arange(n_sel)[None, :]
    forced = ((sblk == 0) | (sblk == qblk) | (sblk == qblk - 1)).astype(jnp.float32)
    score = jnp.where(sblk <= qblk, imp + FORCE_BONUS * forced, -jnp.inf)
    _, idx = lax.top_k(score, min(SEL_TOPK, n_sel))
    k_sel, v_sel = gather_sel(idx)
    kpos = idx[..., None] * SEL_BLOCK + jnp.arange(SEL_BLOCK)
    dist = q_pos[:, None, None] - kpos
    tab_g = jnp.transpose(tab, (1, 0, 2))
    gi = jnp.arange(g_n)[None, :, None, None, None]
    bias = jnp.moveaxis(tab_g[gi, rel_bucket(dist)], -1, 3)
    s_s = jnp.einsum('bqgrd,bgqkjd->bgqrkj', q, k_sel) * scale + bias
    shp = s_s.shape
    mask = jnp.broadcast_to((dist >= 0)[:, :, :, None], shp)
    p_s = masked_softmax(s_s.reshape(shp[:4] + (-1,)), mask.reshape(shp[:4] + (-1,))).reshape(shp)
    o_s = jnp.einsum('bgqrkj,bgqkjd->bqgrd', p_s.astype(v_sel.dtype), v_sel)
    wd = q_pos[:, None] - w_pos[None, :]
    wmask = (wd >= 0) & (wd < WIN_A) & (w_pos[None, :] >= 0)
    wbias = jnp.transpose(tab[rel_bucket(wd)], (2, 3, 0, 1))
    s_w = jnp.einsum('bqgrd,bwgd->bgrqw', q, kw) * scale + wbias
    p_w = masked_softmax(s_w, wmask)
    o_w = jnp.einsum('bgrqw,bwgd->bqgrd', p_w.astype(vw.dtype), vw)
    return gates[..., 0:1] * o_c + gates[..., 1:2] * o_s + gates[..., 2:3] * o_w

def nsa_prompt(q, gates, kc_rows, vc_rows, ks, vs, kw, vw, cmp_pos, cmp_w1, cmp_w2, k_gain, tab):
    b, t = q.shape[:2]
    kc, vc, c_end = compressed_kv(kc_rows, vc_rows, cmp_pos, cmp_w1, cmp_w2, k_gain)
    n_sel = t // SEL_BLOCK
    ks_b = ks.reshape(b, n_sel, SEL_BLOCK, A_KV, HEAD_DIM).transpose(0, 3, 1, 2, 4)
    vs_b = vs.reshape(b, n_sel, SEL_BLOCK, A_KV, HEAD_DIM).transpose(0, 3, 1, 2, 4)
    bi = jnp.arange(b)[:, None, None, None]
    gi = jnp.arange(A_KV)[None, :, None, None]

    def gather_sel(idx):
        return ks_b[bi, gi, idx], vs_b[bi, gi, idx]

    pad = ((0, 0), (WIN_A, 0), (0, 0), (0, 0))
    kw_p, vw_p = jnp.pad(kw, pad), jnp.pad(vw, pad)

    def chunk(start):
        q_pos = start + jnp.arange(NSA_QBLK)
        qc = lax.dynamic_slice_in_dim(q, start, NSA_QBLK, axis=1)
        gc = lax.dynamic_slice_in_dim(gates, start, NSA_QBLK, axis=1)
        kwc = lax.dynamic_slice_in_dim(kw_p, start, NSA_QBLK + WIN_A, axis=1)
        vwc = lax.dynamic_slice_in_dim(vw_p, start, NSA_QBLK + WIN_A, axis=1)
        w_pos = start - WIN_A + jnp.arange(NSA_QBLK + WIN_A)
        return nsa_attend(qc, q_pos, kc, vc, c_end, n_sel, gather_sel, kwc, vwc, w_pos, gc, tab)

    out = lax.map(chunk, jnp.arange(t // NSA_QBLK) * NSA_QBLK)
    return jnp.moveaxis(out, 0, 1).reshape(b, t, A_KV, A_REP, HEAD_DIM)

def nsa_sample(q, gates, new_c, new_s, win_all, past, pool_cmp, pool_sel, page_table,
               cmp_pos, cmp_w1, cmp_w2, k_gain, tab):
    db, s = q.shape[:2]
    past_c = pool_cmp[page_table].reshape(db, past, 2, A_KV, HEAD_DIM)
    rows_c = jnp.concatenate([past_c, new_c], axis=1)
    kc, vc, c_end = compressed_kv(rows_c[:, :, 0], rows_c[:, :, 1], cmp_pos, cmp_w1, cmp_w2, k_gain)
    q_pos = past + jnp.arange(s)
    n_past_blk = past // SEL_BLOCK
    n_new_blk = -(-s // SEL_BLOCK)
    n_sel = n_past_blk + n_new_blk
    bpp = PAGE_SIZE // SEL_BLOCK
    pool_b = pool_sel.reshape(pool_sel.shape[0], bpp, SEL_BLOCK, 2, A_KV, HEAD_DIM)
    new_b = jnp.pad(new_s, ((0, 0), (0, n_new_blk * SEL_BLOCK - s), (0, 0), (0, 0), (0, 0)))
    new_b = new_b.reshape(db, n_new_blk, SEL_BLOCK, 2, A_KV, HEAD_DIM)
    bi = jnp.arange(db)[:, None, None, None]
    gi = jnp.arange(A_KV)[None, :, None, None]

    def gather_sel(idx):
        pidx = jnp.clip(idx, 0, n_past_blk - 1)
        phys = page_table[bi, pidx // bpp]
        from_pool = pool_b[phys, pidx % bpp, :, :, gi]
        from_new = new_b[bi, jnp.clip(idx - n_past_blk, 0, n_new_blk - 1), :, :, gi]
        kv = jnp.where((idx < n_past_blk)[..., None, None, None], from_pool, from_new)
        return kv[..., 0, :], kv[..., 1, :]

    w_len = win_all.shape[1]
    w_pos = past + s - w_len + jnp.arange(w_len)
    return nsa_attend(q, q_pos, kc, vc, c_end, n_sel, gather_sel, win_all[:, :, 0], win_all[:, :, 1],
                      w_pos, gates, tab)

def _ssm_combine(e1, e2):
    a1r, a1i, b1r, b1i = e1
    a2r, a2i, b2r, b2i = e2
    return (a2r * a1r - a2i * a1i, a2r * a1i + a2i * a1r,
            a2r * b1r - a2i * b1i + b2r, a2r * b1i + a2i * b1r + b2i)

def s5_mix(u, h_re, h_im, a_re, a_im, log_dt, b_re, b_im, c_re, c_im, d, w_glu, b_glu):
    bsz, t, _ = u.shape
    f32 = jnp.float32
    uf = u.astype(f32)
    ug = uf.reshape(bsz, t, B_GROUPS, B_GROUP)
    dt = jnp.exp(log_dt.astype(f32))[:, None]
    ar, ai = a_re.astype(f32), a_im.astype(f32)
    mag = jnp.exp(ar * dt)
    abr, abi = mag * jnp.cos(ai * dt), mag * jnp.sin(ai * dt)
    den = ar * ar + ai * ai
    wr = ((abr - 1.0) * ar + abi * ai) / den
    wi = (abi * ar - (abr - 1.0) * ai) / den
    bu_r = jnp.einsum('gpc,btgc->btgp', b_re.astype(f32), ug)
    bu_i = jnp.einsum('gpc,btgc->btgp', b_im.astype(f32), ug)
    x_r = wr * bu_r - wi * bu_i
    x_i = wr * bu_i + wi * bu_r
    hr, hi = h_re.astype(f32), h_im.astype(f32)
    x_r = x_r.at[:, 0].add(abr * hr - abi * hi)
    x_i = x_i.at[:, 0].add(abr * hi + abi * hr)
    a_r = jnp.broadcast_to(abr, x_r.shape)
    a_i = jnp.broadcast_to(abi, x_i.shape)
    _, _, s_r, s_i = lax.associative_scan(_ssm_combine, (a_r, a_i, x_r, x_i), axis=1)
    y = jnp.einsum('gcp,btgp->btgc', c_re.astype(f32), s_r) - jnp.einsum('gcp,btgp->btgc', c_im.astype(f32), s_i)
    y = y.reshape(bsz, t, B_WIDTH) + d.astype(f32) * uf
    z = jax.nn.gelu(y)
    out = z * jax.nn.sigmoid(z @ w_glu.astype(f32) + b_glu.astype(f32))
    return out.astype(u.dtype), s_r[:, -1], s_i[:, -1]

def nsa_s5_inputs(xn, w_in, q_gain, k_gain):
    b, t, _ = xn.shape
    sizes = [A_Q] + [A_KVW] * 6 + [A_GATE, B_WIDTH]
    cuts = [int(c) for c in np.cumsum(sizes)[:-1]]
    q, kc, vc, ks, vs, kw, vw, gl, u = jnp.split(xn @ w_in, cuts, axis=-1)
    heads = lambda z: z.reshape(b, t, A_KV, HEAD_DIM)
    q = rms_norm(q.reshape(b, t, A_KV, A_REP, HEAD_DIM), q_gain)
    gates = jax.nn.sigmoid(gl).reshape(b, t, A_KV, A_REP, 3)
    return (q, rms_norm(heads(kc), k_gain), heads(vc), rms_norm(heads(ks), k_gain), heads(vs),
            rms_norm(heads(kw), k_gain), heads(vw), gates, u)

def swa_inputs(xn, w_in, q_gain, k_gain):
    b, t, _ = xn.shape
    q, k, v = jnp.split(xn @ w_in, [C_HEADS * HEAD_DIM, (C_HEADS + C_KV) * HEAD_DIM], axis=-1)
    q = rms_norm(q.reshape(b, t, C_KV, C_REP, HEAD_DIM), q_gain)
    k = rms_norm(k.reshape(b, t, C_KV, HEAD_DIM), k_gain)
    return q, k, v.reshape(b, t, C_KV, HEAD_DIM)

def swa_attend(q, q_pos, k, v, k_pos, sinks, tab):
    dist = q_pos[:, :, None] - k_pos[:, None, :]
    mask = (dist >= 0) & (dist < WIN_C) & (k_pos[:, None, :] >= 0)
    bias = jnp.transpose(tab[rel_bucket(dist)], (3, 4, 0, 1, 2))
    s = jnp.einsum('bnqgrd,bnkgd->bgrnqk', q, k).astype(jnp.float32) * (HEAD_DIM ** -0.5) + bias
    s = jnp.where(mask, s, -jnp.inf)
    sink = sinks.astype(jnp.float32).reshape(C_KV, C_REP)[:, :, None, None, None]
    m = jnp.maximum(jnp.max(s, axis=-1, keepdims=True), sink)
    e = jnp.exp(s - m)
    p = e / (jnp.sum(e, axis=-1, keepdims=True) + jnp.exp(sink - m))
    return jnp.einsum('bgrnqk,bnkgd->bnqgrd', p.astype(v.dtype), v)

def swa_prompt_attend(q, k, v, sinks, tab):
    b, t = q.shape[:2]
    nb = t // WIN_C
    qb = q.reshape(b, nb, WIN_C, C_KV, C_REP, HEAD_DIM)

    def band(x):
        xb = x.reshape(b, nb, WIN_C, C_KV, HEAD_DIM)
        prev = jnp.pad(xb[:, :-1], ((0, 0), (1, 0), (0, 0), (0, 0), (0, 0)))
        return jnp.concatenate([prev, xb], axis=2)

    q_pos = jnp.arange(t).reshape(nb, WIN_C)
    k_pos = (jnp.arange(nb)[:, None] - 1) * WIN_C + jnp.arange(2 * WIN_C)[None, :]
    o = swa_attend(qb, q_pos, band(k), band(v), k_pos, sinks, tab)
    return o.reshape(b, t, C_HEADS * HEAD_DIM)

def conv_ffn(xn, prev, w_up, w_gate, conv_w, conv_b, w_down):
    h = xn @ w_up
    g = xn @ w_gate
    hp = jnp.concatenate([prev.astype(h.dtype), h], axis=1)
    hc = lax.conv_general_dilated(hp, conv_w.astype(hp.dtype)[:, None, :], window_strides=(1,), padding='VALID',
                                  dimension_numbers=('NWC', 'WIO', 'NWC'), feature_group_count=D_FF) + conv_b
    return (jax.nn.gelu(hc) * g) @ w_down, hp[:, -(CONV_W - 1):]

def setup_inputs(seed: int = 0) -> dict:
    key = jax.random.key(seed)
    keys = iter(jax.random.split(key, 64))
    nrm = lambda shape, scale: jax.random.normal(next(keys), shape, jnp.float32) * scale
    n_pages = PAST_LEN // PAGE_SIZE
    n_used = DEC_BATCH * n_pages
    n_pool = n_used + max(1, n_used // 4)
    wa_buf = min(WIN_A, PAST_LEN)
    wc_buf = min(WIN_C, PAST_LEN)
    page_table = jax.random.permutation(next(keys), n_pool)[:n_used].reshape(DEC_BATCH, n_pages).astype(jnp.int32)
    inp = {}
    inp['x_prompt'] = nrm((BATCH, SEQ, D_MODEL), 1.0)
    inp['x_sample'] = nrm((DEC_BATCH, DEC_SEQ, D_MODEL), 1.0)
    inp['cache_nsa_cmp'] = nrm((N_A_LAYERS, n_pool, PAGE_SIZE, 2, A_KV, HEAD_DIM), 1.0)
    inp['cache_nsa_sel'] = nrm((N_A_LAYERS, n_pool, PAGE_SIZE, 2, A_KV, HEAD_DIM), 1.0)
    inp['cache_nsa_win'] = nrm((N_A_LAYERS, DEC_BATCH, wa_buf, 2, A_KV, HEAD_DIM), 1.0)
    inp['state_s5_re'] = nrm((N_A_LAYERS, DEC_BATCH, B_GROUPS, B_STATE), 0.1)
    inp['state_s5_im'] = nrm((N_A_LAYERS, DEC_BATCH, B_GROUPS, B_STATE), 0.1)
    inp['cache_swa'] = nrm((N_C_LAYERS, DEC_BATCH, wc_buf, 2, C_KV, HEAD_DIM), 1.0)
    inp['state_ffn_conv'] = nrm((DEPTH, DEC_BATCH, CONV_W - 1, D_FF), 1.0)
    inp['page_table'] = page_table
    inp['rel_bias'] = nrm((NUM_BUCKETS, BIAS_HEADS), 0.5)
    inp['norm_mix'] = 1.0 + nrm((DEPTH, D_MODEL), 0.02)
    inp['norm_ffn'] = 1.0 + nrm((DEPTH, D_MODEL), 0.02)
    inp['a_w_in'] = nrm((N_A_LAYERS, D_MODEL, IN_A), D_MODEL ** -0.5)
    inp['a_w_out'] = nrm((N_A_LAYERS, A_Q + B_WIDTH, D_MODEL), (A_Q + B_WIDTH) ** -0.5)
    inp['nsa_q_gain'] = 1.0 + nrm((N_A_LAYERS, HEAD_DIM), 0.02)
    inp['nsa_k_gain'] = 1.0 + nrm((N_A_LAYERS, HEAD_DIM), 0.02)
    inp['nsa_cmp_pos'] = nrm((N_A_LAYERS, 2, CMP_LEN, HEAD_DIM), 0.1)
    inp['nsa_cmp_w1'] = nrm((N_A_LAYERS, 2, CMP_LEN * HEAD_DIM, HEAD_DIM), (CMP_LEN * HEAD_DIM) ** -0.5)
    inp['nsa_cmp_w2'] = nrm((N_A_LAYERS, 2, HEAD_DIM, HEAD_DIM), HEAD_DIM ** -0.5)
    inp['s5_a_re'] = -0.5 + nrm((N_A_LAYERS, B_GROUPS, B_STATE), 0.01)
    inp['s5_a_im'] = math.pi * jnp.arange(B_STATE, dtype=jnp.float32) + nrm((N_A_LAYERS, B_GROUPS, B_STATE), 0.01)
    inp['s5_log_dt'] = jax.random.uniform(next(keys), (N_A_LAYERS, B_GROUPS), jnp.float32, math.log(DT_MIN), math.log(DT_MAX))
    inp['s5_b_re'] = nrm((N_A_LAYERS, B_GROUPS, B_STATE, B_GROUP), B_GROUP ** -0.5)
    inp['s5_b_im'] = nrm((N_A_LAYERS, B_GROUPS, B_STATE, B_GROUP), B_GROUP ** -0.5)
    inp['s5_c_re'] = nrm((N_A_LAYERS, B_GROUPS, B_GROUP, B_STATE), B_STATE ** -0.5)
    inp['s5_c_im'] = nrm((N_A_LAYERS, B_GROUPS, B_GROUP, B_STATE), B_STATE ** -0.5)
    inp['s5_d'] = nrm((N_A_LAYERS, B_WIDTH), 1.0)
    inp['s5_w_glu'] = nrm((N_A_LAYERS, B_WIDTH, B_WIDTH), B_WIDTH ** -0.5)
    inp['s5_b_glu'] = nrm((N_A_LAYERS, B_WIDTH), 0.02)
    inp['c_w_in'] = nrm((N_C_LAYERS, D_MODEL, IN_C), D_MODEL ** -0.5)
    inp['c_w_out'] = nrm((N_C_LAYERS, C_HEADS * HEAD_DIM, D_MODEL), (C_HEADS * HEAD_DIM) ** -0.5)
    inp['c_q_gain'] = 1.0 + nrm((N_C_LAYERS, HEAD_DIM), 0.02)
    inp['c_k_gain'] = 1.0 + nrm((N_C_LAYERS, HEAD_DIM), 0.02)
    inp['c_sinks'] = nrm((N_C_LAYERS, C_HEADS), 0.5)
    inp['ffn_w_up'] = nrm((DEPTH, D_MODEL, D_FF), D_MODEL ** -0.5)
    inp['ffn_w_gate'] = nrm((DEPTH, D_MODEL, D_FF), D_MODEL ** -0.5)
    inp['ffn_conv_w'] = nrm((DEPTH, CONV_W, D_FF), CONV_W ** -0.5)
    inp['ffn_conv_b'] = nrm((DEPTH, D_FF), 0.02)
    inp['ffn_w_down'] = nrm((DEPTH, D_FF, D_MODEL), D_FF ** -0.5)
    return inp

def reference(x_prompt, x_sample, cache_nsa_cmp, cache_nsa_sel, cache_nsa_win, state_s5_re, state_s5_im,
              cache_swa, state_ffn_conv, page_table, rel_bias, norm_mix, norm_ffn, a_w_in, a_w_out,
              nsa_q_gain, nsa_k_gain, nsa_cmp_pos, nsa_cmp_w1, nsa_cmp_w2, s5_a_re, s5_a_im, s5_log_dt,
              s5_b_re, s5_b_im, s5_c_re, s5_c_im, s5_d, s5_w_glu, s5_b_glu, c_w_in, c_w_out, c_q_gain,
              c_k_gain, c_sinks, ffn_w_up, ffn_w_gate, ffn_conv_w, ffn_conv_b, ffn_w_down):
    bp, tp, _ = x_prompt.shape
    bs, ts, _ = x_sample.shape
    past = page_table.shape[1] * PAGE_SIZE
    tab_a = rel_bias[:, :A_HEADS].reshape(NUM_BUCKETS, A_KV, A_REP)
    tab_c = rel_bias[:, :C_HEADS].reshape(NUM_BUCKETS, C_KV, C_REP)
    hp, hs = x_prompt, x_sample
    cmp_p, cmp_s, sel_p, sel_s, win_p, win_s = [], [], [], [], [], []
    s5r_p, s5i_p, s5r_s, s5i_s = [], [], [], []
    swa_p, swa_s, conv_p, conv_s = [], [], [], []
    for layer in range(DEPTH):
        i = layer // 2
        xp = rms_norm(hp, norm_mix[layer])
        xs = rms_norm(hs, norm_mix[layer])
        if layer % 2 == 0:
            qp, kcp, vcp, ksp, vsp, kwp, vwp, gp, up = nsa_s5_inputs(xp, a_w_in[i], nsa_q_gain[i], nsa_k_gain[i])
            qs, kcs, vcs, kss, vss, kws, vws, gs, us = nsa_s5_inputs(xs, a_w_in[i], nsa_q_gain[i], nsa_k_gain[i])
            cmp_args = (nsa_cmp_pos[i], nsa_cmp_w1[i], nsa_cmp_w2[i], nsa_k_gain[i], tab_a)
            o_ap = nsa_prompt(qp, gp, kcp, vcp, ksp, vsp, kwp, vwp, *cmp_args)
            new_c = jnp.stack([kcs, vcs], axis=2)
            new_sel = jnp.stack([kss, vss], axis=2)
            win_all = jnp.concatenate([cache_nsa_win[i].astype(kws.dtype), jnp.stack([kws, vws], axis=2)], axis=1)
            o_as = nsa_sample(qs, gs, new_c, new_sel, win_all, past, cache_nsa_cmp[i], cache_nsa_sel[i],
                              page_table, *cmp_args)
            s5_args = (s5_a_re[i], s5_a_im[i], s5_log_dt[i], s5_b_re[i], s5_b_im[i], s5_c_re[i], s5_c_im[i],
                       s5_d[i], s5_w_glu[i], s5_b_glu[i])
            h0 = jnp.zeros((bp, B_GROUPS, B_STATE), jnp.float32)
            o_bp, hr_p, hi_p = s5_mix(up, h0, h0, *s5_args)
            o_bs, hr_s, hi_s = s5_mix(us, state_s5_re[i], state_s5_im[i], *s5_args)
            hp = hp + jnp.concatenate([o_ap.reshape(bp, tp, A_Q), o_bp], axis=-1) @ a_w_out[i]
            hs = hs + jnp.concatenate([o_as.reshape(bs, ts, A_Q), o_bs], axis=-1) @ a_w_out[i]
            cmp_p.append(jnp.stack([kcp, vcp], axis=2))
            cmp_s.append(new_c)
            sel_p.append(jnp.stack([ksp, vsp], axis=2))
            sel_s.append(new_sel)
            win_p.append(jnp.stack([kwp, vwp], axis=2)[:, -min(WIN_A, tp):])
            win_s.append(win_all[:, -min(WIN_A, win_all.shape[1]):])
            s5r_p.append(hr_p)
            s5i_p.append(hi_p)
            s5r_s.append(hr_s)
            s5i_s.append(hi_s)
        else:
            qp, kp, vp = swa_inputs(xp, c_w_in[i], c_q_gain[i], c_k_gain[i])
            qs, k_s, v_s = swa_inputs(xs, c_w_in[i], c_q_gain[i], c_k_gain[i])
            o_cp = swa_prompt_attend(qp, kp, vp, c_sinks[i], tab_c)
            kv_all = jnp.concatenate([cache_swa[i].astype(k_s.dtype), jnp.stack([k_s, v_s], axis=2)], axis=1)
            kv_len = kv_all.shape[1]
            q_pos = (past + jnp.arange(ts))[None, :]
            k_pos = (past + ts - kv_len + jnp.arange(kv_len))[None, :]
            o_cs = swa_attend(qs[:, None], q_pos, kv_all[:, None, :, 0], kv_all[:, None, :, 1], k_pos,
                              c_sinks[i], tab_c).reshape(bs, ts, C_HEADS * HEAD_DIM)
            hp = hp + o_cp @ c_w_out[i]
            hs = hs + o_cs @ c_w_out[i]
            swa_p.append(jnp.stack([kp, vp], axis=2)[:, -min(WIN_C, tp):])
            swa_s.append(kv_all[:, -min(WIN_C, kv_len):])
        f_args = (ffn_w_up[layer], ffn_w_gate[layer], ffn_conv_w[layer], ffn_conv_b[layer], ffn_w_down[layer])
        yp, cp = conv_ffn(rms_norm(hp, norm_ffn[layer]), jnp.zeros((bp, CONV_W - 1, D_FF), hp.dtype), *f_args)
        ys, cs = conv_ffn(rms_norm(hs, norm_ffn[layer]), state_ffn_conv[layer], *f_args)
        hp = hp + yp
        hs = hs + ys
        conv_p.append(cp)
        conv_s.append(cs)
    y_prompt, y_sample = hp, hs
    nsa_cmp_prompt, nsa_cmp_sample = jnp.stack(cmp_p), jnp.stack(cmp_s)
    nsa_sel_prompt, nsa_sel_sample = jnp.stack(sel_p), jnp.stack(sel_s)
    nsa_win_prompt, nsa_win_sample = jnp.stack(win_p), jnp.stack(win_s)
    s5_re_prompt, s5_im_prompt = jnp.stack(s5r_p), jnp.stack(s5i_p)
    s5_re_sample, s5_im_sample = jnp.stack(s5r_s), jnp.stack(s5i_s)
    swa_prompt, swa_sample = jnp.stack(swa_p), jnp.stack(swa_s)
    ffn_conv_prompt, ffn_conv_sample = jnp.stack(conv_p), jnp.stack(conv_s)
    return (y_prompt, y_sample, nsa_cmp_prompt, nsa_cmp_sample, nsa_sel_prompt, nsa_sel_sample,
            nsa_win_prompt, nsa_win_sample, s5_re_prompt, s5_im_prompt, s5_re_sample, s5_im_sample,
            swa_prompt, swa_sample, ffn_conv_prompt, ffn_conv_sample)


_drawn_inputs = setup_inputs


def setup_inputs(seed=0):
    import zlib

    import numpy as np

    out = dict(_drawn_inputs(seed))
    spreads = {}
    factors = {'norm_mix': 2.762,
     'nsa_q_gain': 8.0,
     'nsa_k_gain': 3.145,
     's5_a_re': 17.437,
     's5_b_glu': 8.0,
     'c_q_gain': 8.0,
     'c_k_gain': 3.771,
     'c_sinks': 50.713,
     'ffn_conv_b': 3.767}
    for name, (base, spread) in spreads.items():
        noise = np.random.default_rng([zlib.crc32(name.encode()), seed]).standard_normal(out[name].shape)
        drawn = base * np.exp(spread * noise) if base else spread * noise
        out[name] = __import__('jax').numpy.asarray(drawn.astype(out[name].dtype))
    for name, factor in factors.items():
        out[name] = (out[name] * factor).astype(out[name].dtype)
    return out
```

```python
from contextlib import ExitStack

import numpy as np

import concourse.bass as bass
from concourse import mybir

F32 = mybir.dt.float32
U32 = mybir.dt.uint32
I32 = mybir.dt.int32
ALU = mybir.AluOpType
ACT = mybir.ActivationFunctionType
AX = mybir.AxisListType.X

P = 128
D = 1024
KD = D // P
T = 1024
TT = T // P
NB = 8
TA = T + NB
NCH = 3
CH = TA // NCH
HD = 64
AH, G = 8, 2
CHD = 16
DFF = 2816
KF = DFF // P
PAST = 4096
PAGE = 128
NPAGE = PAST // PAGE
EPS = 1e-6
NEG = -1e30
FLOOR = -1e29
GRP, CG, NS = 32, 16, 64
L = 8
NC = T // L
QG = 8
NCK = T // 16 - 1
NCS = PAST // 16 - 1

C_MIX, C_FFN, C_D, C_BGLU, C_CB, C_GAIN, C_POS, C_CW = 0, 16, 32, 36, 40, 84, 88, 120
N_COLA = 120
N_CW = 3 * KF
O_TOEP, O_WIN, O_SWA, O_SEL = 0, 384, 896, 1024
N_OH = 1024 + 129


class Chain:

    def __init__(self, eng, sem):
        self.eng, self.sem, self.n = eng, sem, 0

    def __call__(self, ins):
        self.n += 1
        ins.then_inc(self.sem, 1)
        self.eng.wait_ge(self.sem, self.n)


class Core:

    def __init__(self, nc, ctx, ins, outs):
        self.nc, self.ctx, self.i, self.o = nc, ctx, ins, outs
        self.n, self.live = 0, []

    def sem(self, name):
        self.n += 1
        self.live.append(self.nc.alloc_semaphore(name=f"{name}_{self.n}"))
        return self.live[-1]

    def recycle(self):
        self.nc.clear_and_free_semaphores(self.live)
        self.nc.all_engine_barrier()
        self.live = []

    def sb(self, st, name, shape, dt=F32):
        self.n += 1
        return st.enter_context(self.nc.sbuf_tensor(f"{name}_{self.n}", shape, dt))


def bc(ap, dims):
    return bass.AP(ap.tensor, ap.offset, [list(ap.ap[0])] + [list(d) for d in dims])


def stage_setup(k):
    nc = k.nc
    with ExitStack() as st:
        rows = k.sb(st, "rows", [P, 3, P])
        xt = k.sb(st, "xt", [P, TT, D])
        xs = k.sb(st, "xs", [NB, D])
        oh = k.sb(st, "oh", [33, N_OH])
        tabs = k.sb(st, "tabs", [33, NB, AH])
        tabc = k.sb(st, "tabc", [33, NB, CHD])
        toep = k.sb(st, "toep", [P, 2, 384])
        s_zero, s_ident, s_tab1, s_rows, s_x, s_tab = (k.sem(n) for n in (
            "consts_zeroed", "ident_made", "tab_ones", "rows_in", "x_in", "tab_in"))
        s_tr, s_trc, s_rep, s_bias, s_biasc = (k.sem(n) for n in (
            "transposed", "transposed_out", "tab_repeated", "bias_made", "bias_out"))
        s_te, s_tw, s_bc, s_tb = (k.sem(n) for n in (
            "toep_made", "toep_written", "bcast_in", "toep_psum"))
        s_head = k.sem("headones_zeroed")
        s_trc = [s_trc, k.sem("transposed_out_act")]
        s_tw = [s_tw, k.sem("toep_written_odd")]
        i = k.i
        row_loads = [
            (rows[0:16, 0, :], i["norm_mix"].rearrange("l (a b) -> (l a) b", b=P)),
            (rows[16:32, 0, :], i["norm_ffn"].rearrange("l (a b) -> (l a) b", b=P)),
            (rows[32:36, 0, :], i["s5_d"].rearrange("l (a b) -> (l a) b", b=P)),
            (rows[36:40, 0, :], i["s5_b_glu"].rearrange("l (a b) -> (l a) b", b=P)),
            (rows[40:84, 0, :], i["ffn_conv_b"].rearrange("l (a b) -> (l a) b", b=P)),
            (rows[88:120, 0, :], i["nsa_cmp_pos"].rearrange("l k (a s) d -> (l k a) (s d)", s=2)),
            (rows[0:66, 1, :], i["ffn_conv_w"][0].rearrange("w (a b) -> (w a) b", b=P)),
            (rows[0:66, 2, :], i["ffn_conv_w"][1].rearrange("w (a b) -> (w a) b", b=P)),
        ]
        for n, name in enumerate(("nsa_q_gain", "nsa_k_gain", "c_q_gain", "c_k_gain")):
            for half in range(2):
                row_loads.append((rows[84 + n:85 + n, 0, half * HD:half * HD + HD], i[name]))
        n_jobs = 2 * KD + 1 + 3

        with nc.Block() as block:
            def copy_job(eng, j):
                src = k.ps[:, j % 4, :]
                copy = eng.tensor_copy if eng is nc.vector else eng.copy
                if j < 2 * KD:
                    copy(k.hT[:, j // 2, (j % 2) * 512:(j % 2) * 512 + 512], src).then_inc(s_trc[j % 2], 1)
                elif j == 2 * KD:
                    copy(k.hT[:, :, T:TA], src[:, 0:KD * NB].rearrange("p (f b) -> p f b", b=NB)).then_inc(s_trc[j % 2], 1)
                elif j == 2 * KD + 1:
                    copy(k.cols[:, 0:N_COLA], src[:, 0:N_COLA]).then_inc(s_trc[j % 2], 1)
                else:
                    c0 = C_CW + (j - 2 * KD - 2) * N_CW
                    copy(k.cols[:, c0:c0 + N_CW], src[:, 0:N_CW]).then_inc(s_trc[j % 2], 1)

            @block.gpsimd
            def _(pool):
                pool.memset(k.ident[:, :], 0.0).then_inc(s_zero, 1)
                pool.memset(k.ones[:, :], 1.0).then_inc(s_zero, 1)
                pool.memset(k.tab[:, :], 1.0).then_inc(s_tab1, 1)
                pool.wait_ge(s_zero, 2)
                pool.wait_ge(s_tab1, 1)
                pool.affine_select(out=k.ident[:, :], in_=k.ident[:, :], compare_op=ALU.not_equal, fill=1.0,
                                   base=0, pattern=[[-1, P]], channel_multiplier=1).then_inc(s_ident, 1)

            @block.sync
            def _(sp):
                for t in range(TT):
                    sp.dma_start(xt[:, t, :], i["x_prompt"][0, t * P:(t + 1) * P, :]).then_inc(s_x, 16)
                sp.dma_start(xs[:, :], i["x_sample"].rearrange("b s d -> (b s) d")).then_inc(s_x, 16)
                for h in range(CHD):
                    sp.wait_ge(s_te, h + 1)
                    sp.dma_start(k.d_toep[h], toep[:, h % 2, :]).then_inc(s_tw[h % 2], 16)
                for parity in range(2):
                    sp.wait_ge(s_tw[parity], 16 * CHD // 2)

            @block.scalar
            def _(act):
                act.wait_ge(s_tab1, 1)
                act.dma_start(k.tab[0:32, :], i["rel_bias"]).then_inc(s_tab, 16)
                act.dma_start(oh[:, :], i["bucket_onehot"]).then_inc(s_tab, 16)
                for dst, src in row_loads:
                    act.dma_start(dst, src).then_inc(s_rows, 16)
                act.dma_start(k.sink[:, 0, :], i["c_sinks"].broadcast_to([P, CHD])).then_inc(s_bc, 16)
                act.dma_start(k.sink[:, 1, :], i["rel_bias"][31:32, :].broadcast_to([P, CHD])).then_inc(s_bc, 16)
                act.wait_ge(s_bc, 32)
                for j in range(1, n_jobs, 2):
                    act.wait_ge(s_tr, j + 1)
                    copy_job(act, j)

            @block.vector
            def _(dve):
                dve.memset(k.headones[:, :], 0.0).then_inc(s_head, 1)
                dve.wait_ge(s_head, 1)
                dve.memset(k.headones[0:64, 0:64], 1.0)
                dve.memset(k.headones[64:128, 64:128], 1.0)
                dve.wait_ge(s_tab, 32)
                for b in range(NB):
                    dve.tensor_copy(tabs[:, b, :], k.tab[:, 0:AH]).then_inc(s_rep, 1)
                    dve.tensor_copy(tabc[:, b, :], k.tab[:, :]).then_inc(s_rep, 1)
                for j in range(0, n_jobs, 2):
                    dve.wait_ge(s_tr, j + 1)
                    copy_job(dve, j)
                for h in range(CHD):
                    dve.wait_ge(s_tb, h + 1)
                    if h >= 2:
                        dve.wait_ge(s_tw[h % 2], 16 * (h // 2))
                    dve.tensor_copy(toep[:, h % 2, :], k.ps[:, 4 + h % 2, 0:384]).then_inc(s_te, 1)
                dve.wait_ge(s_bias, 1)
                dve.tensor_copy(k.b_win[:, :], k.ps[0:64, 6, :])
                dve.wait_ge(s_bias, 2)
                dve.tensor_copy(k.b_swa[:, :], k.ps[:, 7, 0:P])
                dve.tensor_copy(k.b_sel[:, :], k.ps[0:64, 7, P:P + 129]).then_inc(s_biasc, 1)

            @block.tensor
            def _(pe):
                pe.wait_ge(s_ident, 1)
                pe.wait_ge(s_x, 16 * (TT + 1))
                for j in range(n_jobs):
                    if j >= 4:
                        pe.wait_ge(s_trc[j % 2], (j - 4) // 2 + 1)
                    bank = k.ps[:, j % 4, :]
                    if j < 2 * KD:
                        f = j // 2
                        for t in range(4):
                            ins = pe.transpose(bank[:, t * P:(t + 1) * P],
                                               xt[:, (j % 2) * 4 + t, f * P:(f + 1) * P], k.ident[:, :])
                    elif j == 2 * KD:
                        for f in range(KD):
                            ins = pe.transpose(bank[:, f * NB:(f + 1) * NB], xs[:, f * P:(f + 1) * P],
                                               k.ident[0:NB, 0:NB])
                    else:
                        if j == 2 * KD + 1:
                            pe.wait_ge(s_rows, 16 * len(row_loads))
                        n, w = j - 2 * KD - 1, (N_COLA, N_CW, N_CW)[j - 2 * KD - 1]
                        ins = pe.transpose(bank[:, 0:w], rows[0:w, n, :], k.ident[0:w, 0:w])
                    ins.then_inc(s_tr, 1)
                pe.wait_ge(s_tab, 32)
                pe.wait_ge(s_rep, 2 * NB)
                for h in range(CHD):
                    if h >= 2:
                        pe.wait_ge(s_te, h - 1)
                    pe.matmul(k.ps[:, 4 + h % 2, 0:384], k.tab[:, h:h + 1].to_broadcast([33, P]),
                              oh[:, O_TOEP:O_TOEP + 384], start=True, stop=True).then_inc(s_tb, 1)
                pe.matmul(k.ps[0:64, 6, :], tabs[:, :, :], oh[:, O_WIN:O_WIN + 512],
                          start=True, stop=True).then_inc(s_bias, 1)
                pe.matmul(k.ps[:, 7, 0:P], tabc[:, :, :], oh[:, O_SWA:O_SWA + P], start=True, stop=True)
                pe.matmul(k.ps[0:64, 7, P:P + 129], tabs[:, :, :], oh[:, O_SEL:O_SEL + 129],
                          start=True, stop=True).then_inc(s_bias, 1)


def stage_norm(k, xn, gain_col):
    nc = k.nc
    with ExitStack() as st:
        sq = k.sb(st, "sq", [P, 4, CH])
        root = k.sb(st, "root", [P, 2, CH])
        s_sq, s_used, s_root, s_rec, s_done = (k.sem(n) for n in (
            "squared", "square_used", "rooted", "reciprocal_ready", "normed"))
        with nc.Block() as block:
            @block.scalar
            def _(act):
                for c in range(NCH):
                    for f in range(KD):
                        j = c * KD + f
                        if j >= 4:
                            act.wait_ge(s_used, j - 3)
                        act.activation(sq[:, j % 4, :], k.hT[:, f, c * CH:(c + 1) * CH], ACT.Square).then_inc(s_sq, 1)
                    act.wait_ge(s_used, (c + 1) * KD)
                    if c >= 2:
                        act.wait_ge(s_done, c - 1)
                    act.activation(root[:, c % 2, :], k.ps[:, c, 0:CH], ACT.Sqrt, bias=k.eps[:, :],
                                   scale=1.0 / D).then_inc(s_root, 1)

            @block.tensor
            def _(pe):
                for c in range(NCH):
                    for f in range(KD):
                        pe.wait_ge(s_sq, c * KD + f + 1)
                        pe.matmul(k.ps[:, c, 0:CH], k.ones[:, :], sq[:, (c * KD + f) % 4, :], start=(f == 0),
                                  stop=(f == KD - 1)).then_inc(s_used, 1)

            @block.vector
            def _(dve):
                for c in range(NCH):
                    dve.wait_ge(s_root, c + 1)
                    dve.reciprocal(root[:, c % 2, :], root[:, c % 2, :]).then_inc(s_rec, 1)
                    dve.wait_ge(s_rec, c + 1)
                    for f in range(KD):
                        ins = dve.scalar_tensor_tensor(
                            out=xn[:, f, c * CH:(c + 1) * CH], in0=k.hT[:, f, c * CH:(c + 1) * CH],
                            scalar=k.cols[:, gain_col + f:gain_col + f + 1], in1=root[:, c % 2, :],
                            op0=ALU.mult, op1=ALU.mult)
                    ins.then_inc(s_done, 1)


def stage_linear(k, w, kt, tiles, rhs, put, scalar_engine):
    nc = k.nc
    slots = 3 if kt > KD else 4
    with ExitStack() as st:
        ring = k.sb(st, "wring", [P, slots, kt, P])
        s_w = [k.sem(f"weights_in{n}") for n in range(slots)]
        s_prod, s_out = (k.sem(n) for n in ("product_ready", "product_out"))
        with nc.Block() as block:
            @block.sync
            def _(sp):
                for m, (c0, width) in enumerate(tiles):
                    if m >= slots:
                        sp.wait_ge(s_prod, NCH * (m - slots + 1))
                    sp.dma_start(ring[:, m % slots, :, 0:width],
                                 w[:, c0:c0 + width].rearrange("(a p) n -> p a n", p=P)).then_inc(s_w[m % slots], 16)

            @block.tensor
            def _(pe):
                for m, (c0, width) in enumerate(tiles):
                    pe.wait_ge(s_w[m % slots], 16 * (m // slots + 1))
                    for c in range(NCH):
                        j = m * NCH + c
                        if j >= 8:
                            pe.wait_ge(s_out, j - 7)
                        for a in range(kt):
                            ins = pe.matmul(k.ps[0:width, j % 8, 0:CH], ring[:, m % slots, a, 0:width],
                                            rhs(a, c), start=(a == 0), stop=(a == kt - 1))
                        ins.then_inc(s_prod, 1)

            def take(eng):
                for m, (c0, width) in enumerate(tiles):
                    for c in range(NCH):
                        j = m * NCH + c
                        eng.wait_ge(s_prod, j + 1)
                        put(m, c, k.ps[0:width, j % 8, 0:CH]).then_inc(s_out, 1)

            if scalar_engine:
                block.scalar(take)
            else:
                block.vector(take)


def stage_head_norm(k, tiles):
    nc = k.nc
    jobs = []
    for t, g, f in tiles:
        cols = t.shape[-1]
        step = min(cols, CH if cols == TA else 512)
        jobs += [(t[:, c:c + step], g, f, step) for c in range(0, cols, step)]
    n = len(jobs)
    with ExitStack() as st:
        sq = k.sb(st, "hsq", [P, 4, 512])
        root = k.sb(st, "hroot", [P, 4, 512])
        gain = k.sb(st, "hgain", [P, 2])
        s_sq, s_sum, s_root, s_rec, s_gain, s_done = (k.sem(x) for x in (
            "head_squared", "head_summed", "head_rooted", "head_reciprocal", "gain_scaled", "head_normed"))
        with nc.Block() as block:
            @block.scalar
            def _(act):
                for j in range(n + 2):
                    if j < n:
                        t, _, _, w = jobs[j]
                        if j >= 4:
                            act.wait_ge(s_sum, j - 3)
                        act.activation(sq[:, j % 4, 0:w], t, ACT.Square).then_inc(s_sq, 1)
                    if j >= 2:
                        act.wait_ge(s_sum, j - 1)
                        if j >= 6:
                            act.wait_ge(s_done, j - 5)
                        w = jobs[j - 2][3]
                        act.activation(root[:, (j - 2) % 4, 0:w], k.ps[:, (j - 2) % 4, 0:w], ACT.Sqrt,
                                       bias=k.eps[:, :], scale=1.0 / HD).then_inc(s_root, 1)

            @block.tensor
            def _(pe):
                for j in range(n):
                    pe.wait_ge(s_sq, j + 1)
                    if j >= 4:
                        pe.wait_ge(s_root, j - 3)
                    w = jobs[j][3]
                    pe.matmul(k.ps[:, j % 4, 0:w], k.headones[:, :], sq[:, j % 4, 0:w], start=True,
                              stop=True).then_inc(s_sum, 1)

            @block.vector
            def _(dve):
                g0 = tiles[0][1]
                dve.tensor_scalar(gain[:, :], k.cols[:, g0:g0 + 2], HD ** -0.5, None, ALU.mult).then_inc(s_gain, 1)
                dve.wait_ge(s_gain, 1)
                for j, (t, g, scaled, w) in enumerate(jobs):
                    dve.wait_ge(s_root, j + 1)
                    dve.reciprocal(root[:, j % 4, 0:w], root[:, j % 4, 0:w]).then_inc(s_rec, 1)
                    dve.wait_ge(s_rec, j + 1)
                    dve.scalar_tensor_tensor(
                        out=t, in0=t,
                        scalar=gain[:, 0:1] if scaled else k.cols[:, g:g + 1], in1=root[:, j % 4, 0:w],
                        op0=ALU.mult, op1=ALU.mult).then_inc(s_done, 1)


def stage_rows(k, kv, tok, stok, stores):
    nc = k.nc
    n_kv = len(kv)
    jobs = [(n, h) for n in range(n_kv) for h in range(2)] + [(n, 2) for n in range(n_kv)]
    with ExitStack() as st:
        s_tr, s_out, s_store = (k.sem(x) for x in ("rows_transposed", "rows_out", "rows_stored"))
        with nc.Block() as block:
            def take(eng, par):
                for j, (n, h) in enumerate(jobs):
                    if j % 2 != par:
                        continue
                    eng.wait_ge(s_tr, j + 1)
                    src = k.ps[:, j % 8, :]
                    copy = eng.copy if par else eng.tensor_copy
                    if h < 2:
                        copy(tok[:, 4 * h:4 * h + 4, n, :], src.rearrange("p (t f) -> p t f", t=4)).then_inc(s_out[par], 1)
                    else:
                        copy(stok[:, n, :], src[0:NB, 0:P]).then_inc(s_out[par], 1)

            s_out = [s_out, k.sem("rows_out_act")]

            @block.vector
            def _(dve):
                take(dve, 0)

            @block.scalar
            def _(act):
                take(act, 1)

            @block.tensor
            def _(pe):
                for j, (n, h) in enumerate(jobs):
                    if j >= 8:
                        pe.wait_ge(s_out[j % 2], (j - 8) // 2 + 1)
                    if h < 2:
                        for t in range(4):
                            c0 = (4 * h + t) * P
                            ins = pe.transpose(k.ps[:, j % 8, t * P:(t + 1) * P], kv[n][:, c0:c0 + P], k.ident[:, :])
                    else:
                        ins = pe.transpose(k.ps[0:NB, j % 8, 0:P], kv[n][:, T:TA], k.ident[:, :])
                    ins.then_inc(s_tr, 1)

            @block.sync
            def _(sp):
                sp.wait_ge(s_out[0], (len(jobs) + 1) // 2)
                sp.wait_ge(s_out[1], len(jobs) // 2)
                for dst, src in stores:
                    sp.dma_start(dst, src).then_inc(s_store, 16)
                sp.wait_ge(s_store, 16 * len(stores))


def stage_finish(k):
    nc = k.nc
    jobs = [(t, h) for t in range(TT + 1) for h in range(2)]
    with ExitStack() as st:
        out = k.sb(st, "yrows", [P, 3, D])
        s_tr, s_c0, s_c1, s_y = (k.sem(x) for x in ("y_transposed", "y_out_dve", "y_out_act", "y_stored0"))
        s_y = [s_y, k.sem("y_stored1"), k.sem("y_stored2")]
        with nc.Block() as block:
            def take(eng, par, sem):
                for t in range(TT + 1):
                    j = 2 * t + par
                    eng.wait_ge(s_tr, j + 1)
                    if t >= 3:
                        eng.wait_ge(s_y[t % 3], 16 * (t // 3))
                    n = P if t < TT else NB
                    copy = eng.copy if par else eng.tensor_copy
                    copy(out[0:n, t % 3, par * 512:par * 512 + 512], k.ps[0:n, j % 8, :]).then_inc(sem, 1)

            @block.vector
            def _(dve):
                take(dve, 0, s_c0)

            @block.scalar
            def _(act):
                take(act, 1, s_c1)

            @block.tensor
            def _(pe):
                for j, (t, h) in enumerate(jobs):
                    if j >= 8:
                        pe.wait_ge((s_c0, s_c1)[h], (j - 8) // 2 + 1)
                    n = P if t < TT else NB
                    for f in range(4):
                        ins = pe.transpose(k.ps[0:n, j % 8, f * P:(f + 1) * P],
                                           k.hT[:, 4 * h + f, t * P:t * P + n], k.ident[:, :])
                    ins.then_inc(s_tr, 1)

            @block.sync
            def _(sp):
                for t in range(TT + 1):
                    sp.wait_ge(s_c0, t + 1)
                    sp.wait_ge(s_c1, t + 1)
                    if t < TT:
                        sp.dma_start(k.o["y_prompt"][0, t * P:(t + 1) * P, :], out[:, t % 3, :]).then_inc(s_y[t % 3], 16)
                    else:
                        sp.dma_start(k.o["y_sample"].rearrange("b s d -> (b s) d"), out[0:NB, t % 3, :]).then_inc(s_y[t % 3], 16)
                for n in range(3):
                    sp.wait_ge(s_y[n], 16 * 3)


def stage_attend(k, qT, n_heads, branches, oT, gates):
    nc = k.nc
    per_group = n_heads // G
    tasks = [(i, h, b) for i in range(TT) for h in range(n_heads) for b in range(len(branches))]
    n = len(tasks)
    swa = branches[0]["kind"] == "swa"

    def last_of_tile(t):
        return t >= 0 and (t + 1) % (n_heads * len(branches)) == 0

    def key_tiles(t):
        i, _, b = tasks[t]
        br = branches[b]
        return [0] if br["kind"] == "cmp" else list(range(br["first"](i), i + 1))

    def width(t):
        return NCK if branches[tasks[t][2]]["kind"] == "cmp" else P * len(key_tiles(t))

    steps, groups = [], []
    for t in range(n + 3):
        mine = []
        if 0 <= t - 1 < n:
            m = len(key_tiles(t - 1))
            for g0 in range(0, m, 4):
                mine.append((t - 1, g0, min(4, m - g0)))
        out = []
        if last_of_tile(t - 3):
            out = [(None, tasks[t - 3][0], g0) for g0 in range(0, n_heads // 2, 4)]
        steps.append((list(range(len(groups), len(groups) + len(mine))),
                      list(range(len(groups) + len(mine), len(groups) + len(mine) + len(out)))))
        groups += mine + out

    with ExitStack() as st:
        btab = k.sb(st, "btab", [P, n_heads, 2 * P])
        pbuf = k.sb(st, "probs", [P, 2, 2 * 512])
        pt = k.sb(st, "probsT", [P, 2, TT, P])
        acc = k.sb(st, "acc", [P, 2, n_heads, HD])
        negm = k.sb(st, "negmax", [P, 4])
        sums = k.sb(st, "sums", [P, 4])
        fac = k.sb(st, "factors", [P, 4, 2])
        esink = k.sb(st, "esink", [P, 4])
        nsink = k.sb(st, "nsink", [P, CHD])
        psink = k.sb(st, "psink", [P, CHD])
        farmask = k.sb(st, "farmask", [P, P])
        cmask = k.sb(st, "cmask", [P, TT, 64])
        s_btab, s_mask0, s_mask, s_sc, s_max, s_exp, s_tr, s_pv, s_o, s_dve, s_sink, s_accT = (k.sem(x) for x in (
            "btab_in", "mask_zeroed", "masks_made", "scores_ready", "max_ready", "probs_ready", "probsT_psum",
            "values_done", "head_out", "dve_step", "sink_ready", "esink_ready"))
        s_pt = [k.sem("probsT_act"), k.sem("probsT_dve")]

        def scores(t):
            w = width(t)
            return k.ps[:, 2 * (t % 2):2 * (t % 2) + 2, :].rearrange("p a b -> p (a b)")[:, 0:w]

        with nc.Block() as block:
            @block.sync
            def _(sp):
                for h in range(n_heads):
                    src = bass.AP(k.d_toep.tensor, h * P * 384 + P - 1, [[383, P], [1, 2 * P]])
                    sp.dma_start(btab[:, h, :], src).then_inc(s_btab, 16)
                sp.wait_ge(s_btab, 16 * n_heads)

            @block.gpsimd
            def _(pool):
                pool.memset(farmask[:, :], 0.0).then_inc(s_mask0, 1)
                pool.memset(cmask[:, :, :], 0.0).then_inc(s_mask0, 1)
                pool.wait_ge(s_mask0, 2)
                pool.affine_select(out=farmask[:, :], in_=farmask[:, :], compare_op=ALU.is_gt, fill=NEG,
                                   base=0, pattern=[[1, P]], channel_multiplier=-1).then_inc(s_mask, 1)
                pool.affine_select(out=cmask[:, :, :], in_=cmask[:, :, :], compare_op=ALU.is_ge, fill=NEG,
                                   base=-31, pattern=[[P, TT], [-16, 64]], channel_multiplier=1).then_inc(s_mask, 1)

            def copy_group(eng, gi):
                t, a, m = groups[gi]
                eng.wait_ge(s_tr, gi + 1)
                bank = k.ps[:, 4 + gi % 2, :]
                copy = eng.copy if gi % 2 == 0 else eng.tensor_copy
                if t is None:
                    dst, src = oT[:, m:m + 4, a * P:(a + 1) * P], bank.rearrange("p (f q) -> p f q", f=4)
                elif width(t) == NCK:
                    dst, src = pt[0:NCK, t % 2, 0, :], bank[0:NCK, 0:P]
                else:
                    dst, src = pt[:, t % 2, a:a + m, :].rearrange("p a b -> p (a b)"), bank[:, 0:m * P]
                if t is not None and t >= 2:
                    eng.wait_ge(s_pv, t - 1)
                copy(dst, src).then_inc(s_pt[gi % 2], 1)

            @block.tensor
            def _(pe):
                for t in range(n + 3):
                    if t < n:
                        i, h, b = tasks[t]
                        br = branches[b]
                        g, base = h // per_group, (h % 2) * HD
                        kt = br["k"] if base == g * HD else br["kx"]
                        if t >= 2:
                            pe.wait_ge(s_exp, t - 1)
                        w, c0 = width(t), key_tiles(t)[0] * P
                        sc = scores(t)
                        for c in range(0, w, 512):
                            m = min(512, w - c)
                            ins = pe.matmul(sc[:, c:c + m], qT[base:base + HD, h // 2, i * P:(i + 1) * P],
                                            kt[base:base + HD, c0 + c:c0 + c + m], start=True, stop=True)
                        ins.then_inc(s_sc, 1)
                    mine, out = steps[t]
                    for gi in mine + out:
                        task, a, m = groups[gi]
                        if gi >= 2:
                            pe.wait_ge(s_pt[gi % 2], (gi - 2) // 2 + 1)
                        bank = k.ps[:, 4 + gi % 2, :]
                        if task is None:
                            pe.wait_ge(s_o, t - 2)
                            for f in range(4):
                                src = acc[:, a % 2, 2 * (m + f):2 * (m + f) + 2, :].rearrange("p h d -> p (h d)")
                                ins = pe.transpose(bank[:, f * P:(f + 1) * P], src, k.ident[:, :])
                        else:
                            pe.wait_ge(s_exp, task + 1)
                            kw = width(task)
                            for x in range(m):
                                lo, hi = (a + x) * P, min((a + x + 1) * P, kw)
                                ins = pe.transpose(bank[0:hi - lo, x * P:(x + 1) * P],
                                                   pbuf[:, task % 2, lo:hi], k.ident[:, :])
                        ins.then_inc(s_tr, 1)
                    if 0 <= t - 2 < n:
                        u = t - 2
                        i, h, b = tasks[u]
                        g = h // per_group
                        for gi, (task, _, _) in enumerate(groups[:steps[t][0][-1] + 1] if steps[t][0] else groups):
                            if task == u:
                                pe.wait_ge(s_pt[gi % 2], gi // 2 + 1)
                        if u >= 2:
                            pe.wait_ge(s_o, u - 1)
                        kts = key_tiles(u)
                        for x, kti in enumerate(kts):
                            rows = NCK if width(u) == NCK else P
                            ins = pe.matmul(k.ps[:, 6 + u % 2, 0:HD], pt[0:rows, u % 2, x, :],
                                            branches[b]["v"](kti, g), start=(x == 0), stop=(x == len(kts) - 1))
                        ins.then_inc(s_pv, 1)

            @block.vector
            def _(dve):
                link = Chain(dve, s_dve)
                dve.wait_ge(s_mask, 2)
                dve.wait_ge(s_btab, 16 * n_heads)
                if swa:
                    link(dve.tensor_tensor(psink[:, :], k.sink[:, 0, :], k.sink[:, 1, :], ALU.subtract))
                    dve.tensor_scalar(nsink[:, :], psink[:, :], -1.0, None, ALU.mult).then_inc(s_sink, 1)
                    for h in range(n_heads):
                        ins = dve.tensor_tensor(btab[:, h, 0:P], btab[:, h, 0:P], farmask[:, :], ALU.add)
                    link(ins)
                    dve.wait_ge(s_sink, 1)
                for t in range(n + 3):
                    if t < n:
                        i, h, b = tasks[t]
                        kind = branches[b]["kind"]
                        sc, w = scores(t), width(t)
                        dve.wait_ge(s_sc, t + 1)
                        if kind == "cmp":
                            link(dve.tensor_tensor(sc, sc, cmask[:, i, 0:NCK], ALU.add))
                        else:
                            near = min(w, 2 * P)
                            link(dve.tensor_tensor(sc[:, w - near:w], sc[:, w - near:w],
                                                   btab[:, h, 2 * P - near:2 * P], ALU.add))
                            if kind == "win" and i >= 4:
                                link(dve.tensor_tensor(sc[:, 0:P], sc[:, 0:P], farmask[:, :], ALU.add))
                        m = negm[:, t % 4:t % 4 + 1]
                        if t >= 4:
                            dve.wait_ge(s_exp, t - 3)
                        if kind == "cmp":
                            link(dve.tensor_reduce(m, sc, AX, ALU.max, negate=True))
                            dve.tensor_scalar(m, m, -FLOOR, None, ALU.min).then_inc(s_max, 1)
                        elif swa:
                            link(dve.tensor_reduce(m, sc, AX, ALU.max, negate=True))
                            dve.tensor_tensor(m, m, nsink[:, h:h + 1], ALU.min).then_inc(s_max, 1)
                        else:
                            dve.tensor_reduce(m, sc, AX, ALU.max, negate=True).then_inc(s_max, 1)
                    for gi in steps[t][0]:
                        if gi % 2 == 1:
                            copy_group(dve, gi)
                    if 0 <= t - 2 < n:
                        u = t - 2
                        i, h, b = tasks[u]
                        f = fac[:, u % 4, :]
                        total = sums[:, u % 4:u % 4 + 1]
                        if swa:
                            dve.wait_ge(s_accT, u + 1)
                            link(dve.tensor_tensor(f[:, 0:1], total, esink[:, u % 4:u % 4 + 1], ALU.add))
                        else:
                            dve.wait_ge(s_exp, u + 1)
                            link(dve.tensor_scalar(f[:, 0:1], total, 1e-30, None, ALU.max))
                        link(dve.reciprocal(f[:, 1:2], f[:, 0:1]))
                        if gates is not None:
                            link(dve.tensor_tensor(f[:, 1:2], f[:, 1:2], gates[:, i, 3 * h + b:3 * h + b + 1], ALU.mult))
                        dve.wait_ge(s_pv, u + 1)
                        dst, src = acc[:, i % 2, h, :], k.ps[:, 6 + u % 2, 0:HD]
                        if h == 0 and b == 0 and i >= 2:
                            gl = max(x for x, gr in enumerate(groups) if gr[0] is None and gr[1] == i - 2)
                            dve.wait_ge(s_tr, gl + 1)
                        if b == 0:
                            dve.tensor_scalar(dst, src, f[:, 1:2], None, ALU.mult).then_inc(s_o, 1)
                        else:
                            dve.wait_ge(s_o, u)
                            dve.scalar_tensor_tensor(out=dst, in0=src, scalar=f[:, 1:2], in1=dst, op0=ALU.mult,
                                                     op1=ALU.add).then_inc(s_o, 1)
                    for gi in steps[t][1]:
                        if gi % 2 == 1:
                            copy_group(dve, gi)

            @block.scalar
            def _(act):
                for t in range(n + 3):
                    if t < n:
                        act.wait_ge(s_max, t + 1)
                        if t >= 2:
                            act.wait_ge(s_tr, max(x for x, gr in enumerate(groups) if gr[0] == t - 2) + 1)
                        if t >= 4:
                            act.wait_ge(s_o, t - 3)
                        c = t % 4
                        act.activation(pbuf[:, t % 2, 0:width(t)], scores(t), ACT.Exp, bias=negm[:, c:c + 1],
                                       accum_out=sums[:, c:c + 1]).then_inc(s_exp, 1)
                        if swa:
                            h = tasks[t][1]
                            if t == 0:
                                act.wait_ge(s_sink, 1)
                            act.activation(esink[:, c:c + 1], psink[:, h:h + 1], ACT.Exp,
                                           bias=negm[:, c:c + 1]).then_inc(s_accT, 1)
                    for gi in steps[t][0] + steps[t][1]:
                        if gi % 2 == 0:
                            copy_group(act, gi)


def stage_swap(k, pairs):
    nc = k.nc
    with nc.Block() as block:
        @block.vector
        def _(dve):
            for dst, src in pairs:
                dve.tensor_copy(dst[0:HD, :], src[HD:P, :])

        @block.scalar
        def _(act):
            for dst, src in pairs:
                act.copy(dst[HD:P, :], src[0:HD, :])


def stage_conv_state(k, layer, stT):
    nc = k.nc
    state, out = k.i["state_ffn_conv"][layer], k.o["ffn_conv_sample"][layer]
    with ExitStack() as st:
        rows = k.sb(st, "state_rows", [2 * NB, DFF])
        s_in, s_pass, s_tr = k.sem("state_in"), k.sem("state_passed"), k.sem("state_transposed")
        with nc.Block() as block:
            @block.sync
            def _(sp):
                sp.dma_start(rows[:, :], state.rearrange("b j f -> (b j) f")).then_inc(s_in, 16)
                sp.dma_start(out[:, 0, :], state[:, 1, :]).then_inc(s_pass, 16)
                sp.wait_ge(s_pass, 16)

            @block.tensor
            def _(pe):
                pe.wait_ge(s_in, 16)
                for f in range(KF):
                    ins = pe.transpose(k.ps[:, 0, f * 16:(f + 1) * 16], rows[:, f * P:(f + 1) * P], k.ident[0:16, 0:16])
                ins.then_inc(s_tr, 1)

            @block.vector
            def _(dve):
                dve.wait_ge(s_tr, 1)
                dve.tensor_copy(stT[:, :, :], k.ps[:, 0, 0:KF * 16].rearrange("p (f c) -> p f c", c=16))


def stage_conv_rows(k, layer, hlast):
    nc = k.nc
    with ExitStack() as st:
        rows = k.sb(st, "last_rows", [10, KF, P])
        s_tr, s_out, s_st = k.sem("last_transposed"), k.sem("last_out"), k.sem("last_stored")
        with nc.Block() as block:
            @block.tensor
            def _(pe):
                for f in range(KF):
                    ins = pe.transpose(k.ps[0:10, f // 4, (f % 4) * P:(f % 4 + 1) * P], hlast[:, f, :], k.ident[:, :])
                    if f % 4 == 3 or f == KF - 1:
                        ins.then_inc(s_tr, 1)

            @block.vector
            def _(dve):
                for b in range(-(-KF // 4)):
                    m = min(4, KF - 4 * b)
                    dve.wait_ge(s_tr, b + 1)
                    dve.tensor_copy(rows[:, 4 * b:4 * b + m, :],
                                    k.ps[0:10, b, 0:m * P].rearrange("r (f c) -> r f c", c=P)).then_inc(s_out, 1)

            @block.sync
            def _(sp):
                sp.wait_ge(s_out, -(-KF // 4))
                sp.dma_start(k.o["ffn_conv_prompt"][layer, 0], rows[0:2, :, :].rearrange("r f c -> r (f c)")).then_inc(s_st, 16)
                sp.dma_start(k.o["ffn_conv_sample"][layer, :, 1, :], rows[2:10, :, :].rearrange("r f c -> r (f c)")).then_inc(s_st, 16)
                sp.wait_ge(s_st, 32)


def stage_ffn_up(k, layer, xn, stT, hid, hlast):
    nc = k.nc
    wu, wg = k.i["ffn_w_up"][layer], k.i["ffn_w_gate"][layer]
    cb, cw = C_CB + layer * KF, C_CW + layer * N_CW
    with ExitStack() as st:
        ring = k.sb(st, "upgate", [P, 2, 2, KD, P])
        hb = k.sb(st, "hbuf", [P, 2, 2 + T + NB])
        z = k.sb(st, "conv", [P, 2, TA])
        s_wu, s_wg = [k.sem("up_in0"), k.sem("up_in1")], [k.sem("gate_in0"), k.sem("gate_in1")]
        s_up, s_gate, s_h, s_conv, s_gelu, s_hid, s_step, s_upd, s_gated = (k.sem(x) for x in (
            "up_ready", "gate_ready", "h_out", "conv_ready", "gelu_ready", "hid_ready", "conv_step",
            "up_used", "gate_used"))
        with nc.Block() as block:
            def weights(f, w):
                return w[:, bass.ds(f * P, P)].rearrange("(a p) n -> p a n", p=P)

            @block.sync
            def _(sp):
                sp.sem_inc(s_upd, 2)
                sp.sem_inc(s_gated, 2)
                with sp.Fori(0, KF // 2) as it:
                    for s in range(2):
                        f = it * 2 + s
                        sp.wait_ge(s_upd, f + 1)
                        sp.dma_start(ring[:, s, 0, :, :], weights(f, wu)).then_inc(s_wu[s], 16)
                        sp.wait_ge(s_gated, f + 1)
                        sp.dma_start(ring[:, s, 1, :, :], weights(f, wg)).then_inc(s_wg[s], 16)

            @block.tensor
            def _(pe):
                pe.sem_inc(s_h, NCH)
                pe.sem_inc(s_hid, NCH)
                with pe.Fori(0, KF // 2) as it:
                    for s in range(2):
                        f = it * 2 + s
                        for which, s_in, s_free, s_done, s_used in (
                                (0, s_wu, s_h, s_up, s_upd), (1, s_wg, s_hid, s_gate, s_gated)):
                            pe.wait_ge(s_in[s], it * 16 + 16)
                            for c in range(NCH):
                                pe.wait_ge(s_free, f * NCH + c + 1)
                                for a in range(KD):
                                    ins = pe.matmul(k.ps[:, 3 * which + c, 0:CH], ring[:, s, which, a, :],
                                                    xn[:, a, c * CH:(c + 1) * CH], start=(a == 0), stop=(a == KD - 1))
                                ins.then_inc(s_done, 1)
                            pe.wait_ge(s_done, f * NCH + NCH)
                            pe.sem_inc(s_used, 1)

            @block.scalar
            def _(act):
                with act.Fori(0, KF // 2) as it:
                    for s in range(2):
                        f = it * 2 + s
                        act.wait_ge(s_conv, f + 1)
                        for c in range(NCH):
                            act.wait_ge(s_up, f * NCH + c + 1)
                            act.copy(hb[:, s, 2 + c * CH:2 + (c + 1) * CH], k.ps[:, c, 0:CH]).then_inc(s_h, 1)
                        act.wait_ge(s_conv, f + 3)
                        act.activation(z[:, s, :], z[:, s, :], ACT.Gelu_apprx_tanh).then_inc(s_gelu, 1)

            @block.vector
            def _(dve):
                dve.memset(hb[:, 0, 0:2], 0.0).then_inc(s_conv, 1)
                dve.memset(hb[:, 1, 0:2], 0.0).then_inc(s_conv, 1)
                with dve.Fori(0, KF // 2) as it:
                    for s in range(2):
                        f = it * 2 + s

                        def tap(j):
                            return k.cols[:, bass.ds(f + (cw + j * KF), 1)]

                        def prev(j):
                            return stT[:, bass.ds(f, 1), j:16:2]

                        hp, hn = hb[:, s, :], hb[:, s, 2 + T:2 + T + NB]
                        zp, zn = z[:, s, 0:T], z[:, s, T:TA]
                        bias = k.cols[:, bass.ds(f + cb, 1)]
                        dve.wait_ge(s_h, f * NCH + 2 * NCH)
                        dve.tensor_copy(hlast[:, bass.ds(f, 1), :], hb[:, s:s + 1, T:T + 10])
                        dve.tensor_scalar(zp, hp[:, 0:T], tap(0), bias, ALU.mult, ALU.add)
                        dve.tensor_scalar(zn, prev(0), tap(0), bias, ALU.mult, ALU.add).then_inc(s_step, 1)
                        dve.wait_ge(s_step, f * 2 + 1)
                        dve.scalar_tensor_tensor(out=zp, in0=hp[:, 1:T + 1], scalar=tap(1), in1=zp, op0=ALU.mult, op1=ALU.add)
                        dve.scalar_tensor_tensor(out=zn, in0=prev(1), scalar=tap(1), in1=zn, op0=ALU.mult,
                                                 op1=ALU.add).then_inc(s_step, 1)
                        dve.wait_ge(s_step, f * 2 + 2)
                        dve.scalar_tensor_tensor(out=zp, in0=hp[:, 2:T + 2], scalar=tap(2), in1=zp, op0=ALU.mult, op1=ALU.add)
                        dve.scalar_tensor_tensor(out=zn, in0=hn, scalar=tap(2), in1=zn, op0=ALU.mult,
                                                 op1=ALU.add).then_inc(s_conv, 1)
                        dve.wait_ge(s_gelu, f + 1)
                        for c in range(NCH):
                            dve.wait_ge(s_gate, f * NCH + c + 1)
                            dve.tensor_tensor(hid[:, bass.ds(f, 1), c * CH:(c + 1) * CH], z[:, s:s + 1, c * CH:(c + 1) * CH],
                                              k.ps[:, 3 + c:4 + c, 0:CH], ALU.mult).then_inc(s_hid, 1)


def stage_residual(k, w, kt, rhs):
    nc = k.nc
    with ExitStack() as st:
        ring = k.sb(st, "rwring", [P, 2, kt, P])
        s_w = [k.sem("rweights_in0"), k.sem("rweights_in1")]
        s_prod, s_out, s_free = k.sem("sum_ready"), k.sem("sum_added"), k.sem("rslot_free")
        with nc.Block() as block:
            @block.sync
            def _(sp):
                sp.sem_inc(s_free, 2)
                with sp.Fori(0, KD // 2) as it:
                    for s in range(2):
                        m = it * 2 + s
                        sp.wait_ge(s_free, m + 1)
                        sp.dma_start(ring[:, s, :, :],
                                     w[:, bass.ds(m * P, P)].rearrange("(a p) n -> p a n", p=P)).then_inc(s_w[s], 16)

            @block.tensor
            def _(pe):
                pe.sem_inc(s_out, 2 * NCH)
                with pe.Fori(0, KD // 2) as it:
                    for s in range(2):
                        m = it * 2 + s
                        pe.wait_ge(s_w[s], it * 16 + 16)
                        for c in range(NCH):
                            pe.wait_ge(s_out, m * NCH + c + 1)
                            for a in range(kt):
                                ins = pe.matmul(k.ps[:, 3 * s + c, 0:CH], ring[:, s, a, :], rhs(a, c),
                                                start=(a == 0), stop=(a == kt - 1))
                            ins.then_inc(s_prod, 1)
                        pe.wait_ge(s_prod, m * NCH + NCH)
                        pe.sem_inc(s_free, 1)

            @block.vector
            def _(dve):
                with dve.Fori(0, KD // 2) as it:
                    for s in range(2):
                        m = it * 2 + s
                        for c in range(NCH):
                            dve.wait_ge(s_prod, m * NCH + c + 1)
                            h = k.hT[:, bass.ds(m, 1), c * CH:(c + 1) * CH]
                            dve.tensor_tensor(h, h, k.ps[:, 3 * s + c:3 * s + c + 1, 0:CH], ALU.add).then_inc(s_out, 1)


def ffn(k, layer):
    i = k.i
    with ExitStack() as st:
        stT = k.sb(st, "stateT", [P, KF, 2 * NB])
        hlast = k.sb(st, "hlast", [P, KF, 10])
        stage_conv_state(k, layer, stT)
        hid = k.sb(st, "hid", [P, KF, TA])
        with ExitStack() as st2:
            xn = k.sb(st2, "xf", [P, KD, TA])
            stage_norm(k, xn, C_FFN + layer * KD)
            stage_ffn_up(k, layer, xn, stT, hid, hlast)
        stage_conv_rows(k, layer, hlast)
        stage_residual(k, i["ffn_w_down"][layer], KF, lambda a, c: hid[:, a, c * CH:(c + 1) * CH])


def layer_c(k):
    nc = k.nc
    i, o = k.i, k.o
    with ExitStack() as st:
        oT = k.sb(st, "oT", [P, KD, TA])
        qT = k.sb(st, "cqT", [P, KD, TA])
        kvT = k.sb(st, "ckvT", [P, 2, TA])
        kx = k.sb(st, "ckx", [P, TA])
        tok = k.sb(st, "ckvrows", [P, TT, 2, P])
        stok = k.sb(st, "ckvrows_s", [NB, 2, P])
        with ExitStack() as st2:
            xn = k.sb(st2, "cxn", [P, KD, TA])
            stage_norm(k, xn, C_MIX + KD)

            def put(m, c, ps):
                dst = qT[:, m, :] if m < KD else kvT[:, m - KD, :]
                return nc.scalar.copy(dst[:, c * CH:(c + 1) * CH], ps)

            stage_linear(k, i["c_w_in"][0], KD, [(m * P, P) for m in range(10)],
                         lambda a, c: xn[:, a, c * CH:(c + 1) * CH], put, True)
        stage_head_norm(k, [(qT[:, n, :], C_GAIN + 2, True) for n in range(KD)] + [(kvT[:, 0, :], C_GAIN + 3, False)])
        swa = o["swa_sample"][0].rearrange("b t k g d -> b t (k g d)")
        stage_rows(k, [kvT[:, n, :] for n in range(2)], tok, stok, [
            (kv_rows(o["swa_prompt"]), tok[:, TT - 1, :, :]),
            (swa[:, 127, :], stok[:, :, :]),
            (swa[:, 0:127, :], i["cache_swa"][0, :, 1:128].rearrange("b t k g d -> b t (k g d)"))])
        stage_swap(k, [(kx, kvT[:, 0, :])])
        branch = dict(kind="swa", k=kvT[:, 0, :], kx=kx, first=lambda q: max(0, q - 1),
                      v=lambda t, g: tok[:, t, 1, g * HD:(g + 1) * HD])
        stage_attend(k, qT, CHD, [branch], oT, None)
        stage_swa_sample(k, qT, stok, oT)
        stage_residual(k, i["c_w_out"][0], KD, lambda a, c: oT[:, a, c * CH:(c + 1) * CH])


def stage_swa_sample(k, qT, stok, oT):
    nc = k.nc
    i = k.i
    cache = i["cache_swa"][0].rearrange("b t k g d -> b t (k g d)")
    new = k.o["swa_sample"][0].rearrange("b t k g d -> b t (k g d)")
    with ExitStack() as st:
        kv = k.sb(st, "swa_rows", [P, NB, 4 * HD])
        qb = k.sb(st, "swa_q", [P, NB, NB * CHD])
        kT = k.sb(st, "swa_kT", [P, NB, P])
        pr = k.sb(st, "swa_p", [P, P])
        pT = k.sb(st, "swa_pT", [P, P])
        sc = k.sb(st, "swa_sc", [P, P])
        sm = k.sb(st, "swa_small", [P, 8])
        s_in, s_q0, s_q, s_tr, s_kT, s_sc, s_dve, s_act, s_pTp, s_pT, s_o, s_sink = (k.sem(x) for x in (
            "swa_in", "swa_q_zeroed", "swa_q_ready", "swa_transposed", "swa_kT_ready", "swa_scores", "swa_dve",
            "swa_exp", "swa_pT_psum", "swa_pT_ready", "swa_values", "swa_sink_in"))
        with nc.Block() as block:
            @block.sync
            def _(sp):
                sp.dma_start(kv[0:127, :, :], cache[:, 1:128, :].rearrange("b t c -> t b c")).then_inc(s_in, 16)
                sp.dma_start(kv[127:128, :, :], new[:, 127:128, :].rearrange("b t c -> t b c")).then_inc(s_in, 16)
                for b in range(NB):
                    sp.dma_start(sm[b * CHD:(b + 1) * CHD, 0:1], i["c_sinks"].rearrange("l h -> h l"),
                                 allow_slow_non_contiguous=True).then_inc(s_sink, 16)
                sp.wait_ge(s_sink, 16 * NB)

            @block.vector
            def _(dve):
                link = Chain(dve, s_dve)
                dve.memset(qb[:, :, :], 0.0).then_inc(s_q0, 1)
                dve.wait_ge(s_q0, 1)
                for h in range(CHD):
                    g, base = h // 8, (h % 2) * HD
                    dst = bass.AP(qb.ap().tensor, qb[g * HD:g * HD + 1, 0, h:h + 1].offset,
                                  [[NB * NB * CHD, HD], [NB * CHD + CHD, NB]])
                    ins = dve.tensor_copy(dst, qT[base:base + HD, h // 2, T:TA])
                ins.then_inc(s_q, 1)
                for b in range(2):
                    dve.wait_ge(s_tr, b + 1)
                    dve.tensor_copy(kT[:, 4 * b:4 * b + 4, :], k.ps[:, b, :].rearrange("p (b c) -> p b c", b=4)).then_inc(s_kT, 1)
                dve.wait_ge(s_sc, 1)
                link(dve.tensor_tensor(sc[:, :], k.ps[:, 2, 0:P], k.b_swa[:, :], ALU.add))
                link(dve.tensor_reduce(sm[:, 1:2], sc[:, :], AX, ALU.max))
                dve.wait_ge(s_sink, 16 * NB)
                link(dve.tensor_tensor(sm[:, 1:2], sm[:, 1:2], sm[:, 0:1], ALU.max))
                link(dve.tensor_scalar(sm[:, 2:3], sm[:, 1:2], -1.0, None, ALU.mult))
                dve.wait_ge(s_act, 2)
                link(dve.tensor_tensor(sm[:, 5:6], sm[:, 3:4], sm[:, 4:5], ALU.add))
                link(dve.reciprocal(sm[:, 6:7], sm[:, 5:6]))
                link(dve.tensor_scalar(pr[:, :], pr[:, :], sm[:, 6:7], None, ALU.mult))
                dve.wait_ge(s_pTp, 1)
                dve.tensor_copy(pT[:, :], k.ps[:, 3, 0:P]).then_inc(s_pT, 1)
                dve.wait_ge(s_o, 1)
                for par in range(2):
                    src = k.ps[0:HD, 4, 0:P].rearrange("p (b f r) -> p f b r", b=NB, r=2)[:, :, :, par]
                    dve.tensor_copy(oT[par * HD:(par + 1) * HD, :, T:TA], src)

            @block.scalar
            def _(act):
                act.wait_ge(s_dve, 4)
                act.activation(pr[:, :], sc[:, :], ACT.Exp, bias=sm[:, 2:3], accum_out=sm[:, 3:4]).then_inc(s_act, 1)
                act.activation(sm[:, 4:5], sm[:, 0:1], ACT.Exp, bias=sm[:, 2:3]).then_inc(s_act, 1)

            @block.tensor
            def _(pe):
                pe.wait_ge(s_in, 32)
                for b in range(NB):
                    ins = pe.transpose(k.ps[:, b // 4, (b % 4) * P:(b % 4 + 1) * P], kv[:, b, 0:P], k.ident[:, :])
                    if b % 4 == 3:
                        ins.then_inc(s_tr, 1)
                pe.wait_ge(s_q, 1)
                pe.wait_ge(s_kT, 2)
                for b in range(NB):
                    ins = pe.matmul(k.ps[:, 2, 0:P], qb[:, b, :], kT[:, b, :], start=(b == 0), stop=(b == NB - 1))
                ins.then_inc(s_sc, 1)
                pe.wait_ge(s_dve, 7)
                pe.transpose(k.ps[:, 3, 0:P], pr[:, :], k.ident[:, :]).then_inc(s_pTp, 1)
                pe.wait_ge(s_pT, 1)
                for b in range(NB):
                    for g in range(G):
                        c0 = b * CHD + g * 8
                        ins = pe.matmul(k.ps[0:HD, 4, c0:c0 + 8], kv[:, b, P + g * HD:P + (g + 1) * HD],
                                        pT[:, c0:c0 + 8], start=True, stop=True)
                ins.then_inc(s_o, 1)


class S5Tensors:

    def __init__(self, k, st):
        new = lambda name, *shape: k.sb(st, "s5_" + name, [P] + list(shape))
        self.angles = k.sem("angles_ready")
        self.c1, self.c2 = new("c1", GRP * CG), new("c2", GRP * CG)
        self.wb1, self.wb2 = new("wb1", GRP, CG), new("wb2", GRP, CG)
        self.h1, self.h2 = new("h1", 256), new("h2", 256)
        self.pr, self.pi = new("pr", L + 1, GRP), new("pi", L + 1, GRP)
        self.mag8 = new("mag8", GRP)
        self.turns = new("turns", 7, 2, GRP)
        self.fin_c, self.fin_s = new("fin_c", GRP), new("fin_s", GRP)
        self.hnew = new("hnew", NB, GRP)
        self.swap = new("swap", P)


def stage_s5_params(k, s):
    nc, i = k.nc, k.i
    with ExitStack() as st:
        ar_rows = k.sb(st, "ar_rows", [GRP, 2, P])
        c_rows = k.sb(st, "c_rows", [P, 2, 4, P])
        h_rows = k.sb(st, "h_rows", [P, 2, 2, P])
        b1 = k.sb(st, "b1", [P, GRP, CG])
        b2 = k.sb(st, "b2", [P, GRP, CG])
        tmp = k.sb(st, "wb_tmp", [P, GRP, CG])
        names = ("logdt dt ar ai x mag th kk r rc c s m den am1 wr wi t1 t2").split()
        v = {n: k.sb(st, "s5_" + n, [P, GRP]) for n in names}
        s_rows, s_b, s_tr, s_dve, s_act, s_sw0, s_sw = (k.sem(x) for x in (
            "s5_rows_in", "s5_b_in", "s5_transposed", "s5_dve", "s5_act", "swap_zeroed", "swap_made"))
        flat = lambda name, pat: i[name][0].rearrange(pat)
        row_loads = []
        for n, name in enumerate(("s5_a_re", "s5_a_im")):
            row_loads += [(ar_rows[:, n, half * NS:(half + 1) * NS], i[name][0]) for half in range(2)]
        for n, name in enumerate(("s5_c_re", "s5_c_im")):
            src = flat(name, "g c p -> (g c) p").rearrange("(a r) p -> r a p", r=P)
            row_loads += [(c_rows[:, 0, :, n * NS:(n + 1) * NS], src), (c_rows[:, 1, :, (1 - n) * NS:(2 - n) * NS], src)]
        for n, name in enumerate(("state_s5_re", "state_s5_im")):
            src = flat(name, "b g p -> (b g) p").rearrange("(a r) p -> r a p", r=P)
            row_loads += [(h_rows[:, 0, :, n * NS:(n + 1) * NS], src), (h_rows[:, 1, :, (1 - n) * NS:(2 - n) * NS], src)]
        with nc.Block() as block:
            @block.sync
            def _(sp):
                for dst, src in row_loads:
                    sp.dma_start(dst, src).then_inc(s_rows, 16)
                sp.dma_start(v["logdt"][:, :], i["s5_log_dt"].broadcast_to([P, GRP])).then_inc(s_b, 16)
                for n, name in enumerate(("s5_b_re", "s5_b_im")):
                    src = flat(name, "g p c -> p g c")
                    sp.dma_start(b1[n * NS:(n + 1) * NS, :, :], src).then_inc(s_b, 16)
                    sp.dma_start(b2[(1 - n) * NS:(2 - n) * NS, :, :], src).then_inc(s_b, 16)
                sp.wait_ge(s_b, 80)

            @block.gpsimd
            def _(pool):
                pool.memset(s.swap[:, :], 0.0).then_inc(s_sw0, 1)
                pool.wait_ge(s_sw0, 1)
                pool.affine_select(out=s.swap[:, :], in_=s.swap[:, :], compare_op=ALU.not_equal, fill=-1.0,
                                   base=-NS, pattern=[[-1, P]], channel_multiplier=1).then_inc(s_sw0, 1)
                pool.wait_ge(s_sw0, 2)
                pool.affine_select(out=s.swap[:, :], in_=s.swap[:, :], compare_op=ALU.not_equal, fill=1.0,
                                   base=NS, pattern=[[-1, P]], channel_multiplier=1).then_inc(s_sw, 1)

            @block.tensor
            def _(pe):
                pe.wait_ge(s_rows, 16 * len(row_loads))
                for n in range(2):
                    pe.transpose(k.ps[:, 0, n * GRP:(n + 1) * GRP], ar_rows[:, n, :], k.ident[0:GRP, 0:GRP])
                    for a in range(4):
                        pe.transpose(k.ps[:, 1 + n, a * P:(a + 1) * P], c_rows[:, n, a, :], k.ident[:, :])
                    for a in range(2):
                        ins = pe.transpose(k.ps[:, 3 + n, a * P:(a + 1) * P], h_rows[:, n, a, :], k.ident[:, :])
                ins.then_inc(s_tr, 1)

            @block.vector
            def _(dve):
                link = Chain(dve, s_dve)
                vv = {n: v[n][:, :] for n in names}
                tt = lambda o, a, b, op: link(dve.tensor_tensor(vv[o], vv[a], vv[b], op))
                ts = lambda o, a, x, op, y=None, op2=ALU.bypass: link(dve.tensor_scalar(vv[o], vv[a], x, y, op, op2))
                dve.wait_ge(s_tr, 1)
                link(dve.tensor_copy(vv["ar"], k.ps[:, 0, 0:GRP]))
                link(dve.tensor_copy(vv["ai"], k.ps[:, 0, GRP:2 * GRP]))
                link(dve.tensor_copy(s.c1[0:NS, :], k.ps[0:NS, 1, :]))
                link(dve.tensor_scalar(s.c1[NS:P, :], k.ps[NS:P, 1, :], -1.0, None, ALU.mult))
                link(dve.tensor_scalar(s.c2[:, :], k.ps[:, 2, :], -1.0, None, ALU.mult))
                link(dve.tensor_copy(s.h1[:, :], k.ps[:, 3, 0:256]))
                link(dve.tensor_scalar(s.h2[0:NS, :], k.ps[0:NS, 4, 0:256], -1.0, None, ALU.mult))
                link(dve.tensor_copy(s.h2[NS:P, :], k.ps[NS:P, 4, 0:256]))
                dve.wait_ge(s_act, 1)
                tt("x", "ar", "dt", ALU.mult)
                tt("th", "ai", "dt", ALU.mult)
                two_pi, c1, c2 = 2 * np.pi, 6.28125, 4059 / 2 ** 21
                big = 1.5 * 2 ** 23
                ts("kk", "th", 1 / two_pi, ALU.mult, big, ALU.add)
                ts("kk", "kk", big, ALU.subtract)
                for part in (c1, c2, two_pi - c1 - c2):
                    link(dve.scalar_tensor_tensor(out=vv["r"], in0=vv["kk"], scalar=-float(part),
                                                  in1=vv["th" if part == c1 else "r"], op0=ALU.mult, op1=ALU.add))
                ts("rc", "r", np.pi / 2, ALU.add)
                ts("m", "rc", np.pi, ALU.is_gt, -two_pi, ALU.mult)
                tt("rc", "rc", "m", ALU.add)
                for x in ("r", "rc"):
                    ts(x, x, 3.1415925, ALU.min, -3.1415925, ALU.max)
                dve.sem_inc(s.angles, 1)
                dve.wait_ge(s_act, 5)
                pr = lambda n: s.pr[:, n, :]
                pi = lambda n: s.pi[:, n, :]
                link(dve.memset(pr(0), 1.0))
                link(dve.memset(pi(0), 0.0))
                link(dve.tensor_tensor(pr(1), vv["mag"], vv["c"], ALU.mult))
                link(dve.tensor_tensor(pi(1), vv["mag"], vv["s"], ALU.mult))
                ts("am1", "c", 1.0, ALU.mult)
                link(dve.tensor_scalar(vv["am1"], pr(1), 1.0, None, ALU.subtract))
                tt("den", "ar", "ar", ALU.mult)
                tt("t1", "ai", "ai", ALU.mult)
                tt("den", "den", "t1", ALU.add)
                link(dve.reciprocal(vv["den"], vv["den"]))
                tt("t1", "am1", "ar", ALU.mult)
                link(dve.tensor_tensor(vv["t2"], pi(1), vv["ai"], ALU.mult))
                tt("t1", "t1", "t2", ALU.add)
                tt("wr", "t1", "den", ALU.mult)
                link(dve.tensor_tensor(vv["t1"], pi(1), vv["ar"], ALU.mult))
                tt("t2", "am1", "ai", ALU.mult)
                tt("t1", "t1", "t2", ALU.subtract)
                tt("wi", "t1", "den", ALU.mult)
                for n in range(3 + 7):
                    tt("t1", "c", "c", ALU.mult)
                    tt("t2", "s", "s", ALU.mult)
                    tt("m", "t1", "t2", ALU.add)
                    ts("m", "m", -0.5, ALU.mult, 1.5, ALU.add)
                    tt("c", "c", "m", ALU.mult)
                    tt("s", "s", "m", ALU.mult)
                    if n >= 3:
                        link(dve.tensor_copy(s.turns[:, n - 3, 0, :], vv["c"]))
                        link(dve.tensor_copy(s.turns[:, n - 3, 1, :], vv["s"]))
                    tt("t1", "c", "c", ALU.mult)
                    tt("t2", "s", "s", ALU.mult)
                    tt("s", "c", "s", ALU.mult)
                    ts("s", "s", 2.0, ALU.mult)
                    tt("c", "t1", "t2", ALU.subtract)
                for n in range(1, L):
                    link(dve.tensor_tensor(pr(n + 1), pr(n), pr(1), ALU.mult))
                    link(dve.tensor_tensor(vv["t1"], pi(n), pi(1), ALU.mult))
                    link(dve.tensor_tensor(pr(n + 1), pr(n + 1), vv["t1"], ALU.subtract))
                    link(dve.tensor_tensor(pi(n + 1), pr(n), pi(1), ALU.mult))
                    link(dve.tensor_tensor(vv["t1"], pi(n), pr(1), ALU.mult))
                    link(dve.tensor_tensor(pi(n + 1), pi(n + 1), vv["t1"], ALU.add))
                dve.wait_ge(s_b, 80)
                link(dve.tensor_scalar(b2[0:NS, :, :], b2[0:NS, :, :], -1.0, None, ALU.mult))
                wr, wi = (bc(v[n][:, :], [[1, GRP], [0, CG]]) for n in ("wr", "wi"))
                link(dve.tensor_tensor(s.wb1[:, :, :], b1[:, :, :], wr, ALU.mult))
                link(dve.tensor_tensor(tmp[:, :, :], b2[:, :, :], wi, ALU.mult))
                link(dve.tensor_tensor(s.wb1[:, :, :], s.wb1[:, :, :], tmp[:, :, :], ALU.add))
                link(dve.tensor_tensor(s.wb2[:, :, :], b2[:, :, :], wr, ALU.mult))
                link(dve.tensor_tensor(tmp[:, :, :], b1[:, :, :], wi, ALU.mult))
                link(dve.tensor_tensor(s.wb2[:, :, :], s.wb2[:, :, :], tmp[:, :, :], ALU.subtract))

            @block.scalar
            def _(act):
                act.wait_ge(s_b, 80)
                act.activation(v["dt"][:, :], v["logdt"][:, :], ACT.Exp).then_inc(s_act, 1)
                act.wait_ge(s.angles, 1)
                act.activation(v["mag"][:, :], v["x"][:, :], ACT.Exp).then_inc(s_act, 1)
                act.activation(s.mag8[:, :], v["x"][:, :], ACT.Exp, scale=float(L)).then_inc(s_act, 1)
                act.activation(v["s"][:, :], v["r"][:, :], ACT.Sin).then_inc(s_act, 1)
                act.activation(v["c"][:, :], v["rc"][:, :], ACT.Sin).then_inc(s_act, 1)


def stage_s5_quarter(k, s, qd, u):
    nc = k.nc
    g0 = qd * QG
    NU = NC + NB
    with ExitStack() as st:
        big = lambda name: k.sb(st, name, [P, QG, P])
        ur = k.sb(st, "u_by_step", [P, L, NC])
        U = k.sb(st, "U", [P, QG, NU])
        V, V2, Q, Q2 = big("V"), big("V2"), big("Q"), big("Q2")
        Pm, Pm2, cos, sin = big("Pm"), big("Pm2"), big("cos"), big("sin")
        t1, xr, G = big("t1"), big("xr"), big("G")
        km = k.sb(st, "kernels", [P, P])
        Tm = k.sb(st, "Tm", [P, L, P])
        Tg = k.sb(st, "Tg", [P, QG, P])
        ys = k.sb(st, "y_samples", [CG, QG, NB])
        yb = k.sb(st, "y_samples_back", [P, NB])
        s_Tg = k.sem("T_grouped")
        gcos, gsin, Y, yback = V, V2, xr, ur
        s_ur, s_uw, s_u0, s_u, s_dve, s_tz, s_v, s_q, s_qc, s_km, s_kmc, s_T = (k.sem(x) for x in (
            "u_by_step_ready", "u_written", "u_zeroed", "u_in", "s5q_dve", "T_zeroed", "V_ready", "Q_psum", "Q_ready",
            "kernels_psum", "kernels_ready", "T_in"))
        s_x, s_g, s_y, s_yc, s_yw, s_yb, s_ysp, s_ysc, s_hs = (k.sem(x) for x in (
            "X_ready", "G_ready", "Y_psum", "Y_out", "Y_written", "Y_back", "ys_psum", "ys_ready", "hs_ready"))
        gs = slice(g0, g0 + QG)
        power = lambda t, n, step: bass.AP(t[:, n, g0:g0 + 1].tensor, t[:, n, g0:g0 + 1].offset,
                                           [list(t[:, n, g0:g0 + 1].ap[0]), [1, QG], [step * GRP, L], [0, CG]])
        chan = lambda ap: bc(ap, [[CG, QG], [0, L], [1, CG]])
        wb1, wb2 = chan(s.wb1[:, g0:g0 + 1, 0:1]), chan(s.wb2[:, g0:g0 + 1, 0:1])
        c1, c2 = chan(s.c1[:, g0 * CG:g0 * CG + 1]), chan(s.c2[:, g0 * CG:g0 * CG + 1])
        four = lambda t: t[:, :, :].rearrange("p g (j c) -> p g j c", c=CG)
        with nc.Block() as block:
            @block.scalar
            def _(act):
                act.copy(ur[:, :, :], u[:, 0:T].rearrange("p (n j) -> p j n", j=L)).then_inc(s_ur, 1)
                for b in range(4):
                    act.wait_ge(s_q, b + 1)
                    dst = (Q, Q2)[b // 2][:, 4 * (b % 2):4 * (b % 2) + 4, :]
                    act.copy(dst, k.ps[:, b, :].rearrange("p (g m) -> p g m", g=4)).then_inc(s_qc, 1)
                act.wait_ge(s_km, 1)
                act.copy(km[:, :], k.ps[:, 4, 0:P]).then_inc(s_kmc, 1)
                act.wait_ge(s_T, 16 * 36)
                act.copy(Tg[:, :, :].rearrange("p g (j c) -> p g j c", c=CG),
                         Tm[:, :, :].rearrange("p j (g c) -> p g j c", c=CG)).then_inc(s_Tg, 1)
                for b in range(2):
                    act.wait_ge(s_y, b + 1)
                    act.copy(Y[:, 4 * b:4 * b + 4, :], k.ps[:, 5 + b, :].rearrange("p (g n) -> p g n", g=4)).then_inc(s_yc, 1)
                act.wait_ge(s_ysp, 1)
                act.copy(ys[:, :, :], k.ps[0:CG, 7, 0:QG * NB].rearrange("p (g b) -> p g b", b=NB)).then_inc(s_ysc, 1)

            @block.sync
            def _(sp):
                sp.wait_ge(s_ur, 1)
                sp.dma_start(k.d_u[:, 0:L * NC], ur[:, :, :].rearrange("p j n -> p (j n)")).then_inc(s_uw, 16)
                sp.dma_start(k.d_u[:, L * NC:], u[:, T:TA]).then_inc(s_uw, 16)
                sp.wait_ge(s_uw, 32)
                sp.wait_ge(s_u0, 1)
                steps = k.d_u[:, 0:L * NC].rearrange("(g c) (j n) -> c g j n", c=CG, j=L)
                for j in range(L):
                    sp.dma_start(U[j * CG:(j + 1) * CG, :, 0:NC], steps[:, :, j, :]).then_inc(s_u, 16)
                sp.dma_start(U[(L - 1) * CG:L * CG, :, NC:NU],
                             k.d_u[:, L * NC:].rearrange("(g c) b -> c g b", c=CG)).then_inc(s_u, 16)
                sp.wait_ge(s_kmc, 1)
                sp.wait_ge(s_tz, 1)
                for jp in range(L):
                    for j in range(jp, L):
                        r = (L - 1 - (j - jp)) * CG
                        sp.dma_start(Tm[jp * CG:(jp + 1) * CG, j, :], km[r:r + CG, :]).then_inc(s_T, 16)
                sp.wait_ge(s_yc, 2)
                sp.dma_start(k.d_y, Y[:, :, :].rearrange("p g n -> p (g n)")).then_inc(s_yw, 16)
                sp.wait_ge(s_ysc, 1)
                sp.dma_start(k.d_ys.rearrange("(g c) b -> c g b", c=CG), ys[:, :, :]).then_inc(s_yw, 16)
                sp.wait_ge(s_yw, 32)
                back = k.d_y.rearrange("(j c) (g n) -> c g j n", c=CG, g=QG)
                for g in range(QG):
                    sp.dma_start(yback[g * CG:(g + 1) * CG, :, :], back[:, g, :, :]).then_inc(s_yb, 16)
                sp.dma_start(yb[:, :], k.d_ys).then_inc(s_yb, 16)
                sp.wait_ge(s_yb, 16 * (QG + 1))
                sp.wait_ge(s_T, 16 * 36)

            @block.vector
            def _(dve):
                link = Chain(dve, s_dve)
                dve.memset(U[:, :, NC:NU], 0.0).then_inc(s_u0, 1)
                dve.memset(Tm[:, :, :], 0.0).then_inc(s_tz, 1)

                def combine(out, pa, xa, pb_, xb, op):
                    link(dve.tensor_tensor(four(out), pa, xa, ALU.mult))
                    link(dve.tensor_tensor(four(t1), pb_, xb, ALU.mult))
                    link(dve.tensor_tensor(four(out), four(out), four(t1), op))

                r7, i7 = power(s.pr, L - 1, -1), power(s.pi, L - 1, -1)
                combine(V, r7, wb1, i7, wb2, ALU.add)
                dve.sem_inc(s_v, 1)
                combine(V2, i7, wb1, r7, wb2, ALU.subtract)
                dve.sem_inc(s_v, 1)
                r1, i1 = power(s.pr, 1, 1), power(s.pi, 1, 1)
                combine(Pm, r1, c1, i1, c2, ALU.add)
                combine(Pm2, r1, c2, i1, c1, ALU.subtract)
                link(dve.memset(cos[:, :, 0:1], 1.0))
                link(dve.memset(sin[:, :, 0:1], 0.0))
                for level in range(7):
                    m = 2 ** level
                    cc, cs = (bc(s.turns[:, level, n, g0:g0 + 1], [[1, QG], [0, m]]) for n in (0, 1))
                    lo_c, lo_s, tmp = cos[:, :, 0:m], sin[:, :, 0:m], t1[:, :, 0:m]
                    hi_c, hi_s = cos[:, :, m:2 * m], sin[:, :, m:2 * m]
                    link(dve.tensor_tensor(hi_c, lo_c, cc, ALU.mult))
                    link(dve.tensor_tensor(tmp, lo_s, cs, ALU.mult))
                    link(dve.tensor_tensor(hi_c, hi_c, tmp, ALU.subtract))
                    link(dve.tensor_tensor(hi_s, lo_c, cs, ALU.mult))
                    link(dve.tensor_tensor(tmp, lo_s, cc, ALU.mult))
                    link(dve.tensor_tensor(hi_s, hi_s, tmp, ALU.add))
                dve.wait_ge(s_x, 1)
                for b in range(3):
                    n = min(3, QG - 3 * b)
                    src = k.ps[:, b, 0:n * NU].rearrange("p (g n) -> p g n", n=NU)
                    link(dve.tensor_tensor(xr[:, 3 * b:3 * b + n, :], src[:, :, 0:NC], cos[:, 3 * b:3 * b + n, :], ALU.mult))
                for b in range(2):
                    src = k.ps[:, 3 + b, :].rearrange("p (g n) -> p g n", n=NC)
                    link(dve.tensor_tensor(t1[:, 4 * b:4 * b + 4, :], src, sin[:, 4 * b:4 * b + 4, :], ALU.mult))
                link(dve.tensor_tensor(xr[:, :, :], xr[:, :, :], t1[:, :, :], ALU.add))
                for g in range(QG):
                    ins = dve.tensor_tensor_scan(out=G[:, g, :], data0=s.mag8[:, g0 + g:g0 + g + 1].to_broadcast([P, NC]),
                                                 data1=xr[:, g, :], initial=0.0, op0=ALU.mult, op1=ALU.add)
                link(ins)
                dve.tensor_tensor(gcos[:, :, :], G[:, :, :], cos[:, :, :], ALU.mult)
                dve.tensor_tensor(gsin[:, :, :], G[:, :, :], sin[:, :, :], ALU.mult).then_inc(s_g, 1)
                dve.wait_ge(s_g, 1)
                dve.tensor_copy(s.fin_c[:, gs], gcos[:, :, NC - 1])
                dve.tensor_copy(s.fin_s[:, gs], gsin[:, :, NC - 1])
                hn = s.hnew[:, :, gs]
                h1 = s.h1[:, :].rearrange("p (b g) -> p b g", g=GRP)[:, :, gs]
                h2 = s.h2[:, :].rearrange("p (b g) -> p b g", g=GRP)[:, :, gs]
                a_r, a_i = (bc(t[:, 1, g0:g0 + 1], [[0, NB], [1, QG]]) for t in (s.pr, s.pi))
                tmp = t1[:, :, 0:NB]
                link(dve.tensor_tensor(hn, h1, a_r, ALU.mult))
                link(dve.tensor_tensor(tmp, h2, a_i, ALU.mult))
                link(dve.tensor_tensor(hn, hn, tmp, ALU.add))
                for b in range(3):
                    n = min(3, QG - 3 * b)
                    src = k.ps[:, b, 0:n * NU].rearrange("p (g n) -> p n g", n=NU)[:, NC:NU, :]
                    part = s.hnew[:, :, g0 + 3 * b:g0 + 3 * b + n]
                    link(dve.tensor_tensor(part, part, src, ALU.add))
                dve.sem_inc(s_hs, 1)
                dve.wait_ge(s_yb, 16 * (QG + 1))
                d = k.cols[:, C_D + qd:C_D + qd + 1]
                up = u[:, 0:T].rearrange("p (n j) -> p n j", j=L)
                dve.scalar_tensor_tensor(out=up, in0=up, scalar=d, in1=yback[:, :, :].rearrange("p j n -> p n j"),
                                         op0=ALU.mult, op1=ALU.add)
                dve.scalar_tensor_tensor(out=u[:, T:TA], in0=u[:, T:TA], scalar=d, in1=yb[:, :],
                                         op0=ALU.mult, op1=ALU.add)

            @block.tensor
            def _(pe):
                for b in range(4):
                    pe.wait_ge(s_v, b // 2 + 1)
                    for g in range(4):
                        src = (V, V2)[b // 2][:, 4 * (b % 2) + g, :]
                        ins = pe.transpose(k.ps[:, b, g * P:(g + 1) * P], src, k.ident[:, :])
                    ins.then_inc(s_q, 1)
                for g in range(QG):
                    ins = pe.matmul(k.ps[:, 4, g * CG:(g + 1) * CG], V[:, g, :], s.c1[:, (g0 + g) * CG:(g0 + g + 1) * CG],
                                    start=True, stop=True)
                ins.then_inc(s_km, 1)
                pe.wait_ge(s_qc, 4)
                pe.wait_ge(s_kmc, 1)
                pe.wait_ge(s_u, 16 * (L + 1))
                for g in range(QG):
                    pe.matmul(k.ps[:, g // 3, (g % 3) * NU:(g % 3 + 1) * NU], Q[:, g, :], U[:, g, :], start=True, stop=True)
                for g in range(QG):
                    ins = pe.matmul(k.ps[:, 3 + g // 4, (g % 4) * NC:(g % 4 + 1) * NC], Q2[:, g, :], U[:, g, 0:NC],
                                    start=True, stop=True)
                ins.then_inc(s_x, 1)
                pe.wait_ge(s_Tg, 1)
                pe.wait_ge(s_g, 1)
                for g in range(QG):
                    out = k.ps[:, 5 + g // 4, (g % 4) * NC:(g % 4 + 1) * NC]
                    pe.matmul(out, Tg[:, g, :], U[:, g, 0:NC], start=True, stop=False)
                    pe.matmul(out[:, 1:NC], Pm[:, g, :], gcos[:, g, 0:NC - 1], start=False, stop=False)
                    ins = pe.matmul(out[:, 1:NC], Pm2[:, g, :], gsin[:, g, 0:NC - 1], start=False, stop=True)
                    if g % 4 == 3:
                        ins.then_inc(s_y, 1)
                pe.wait_ge(s_hs, 1)
                for g in range(QG):
                    ins = pe.matmul(k.ps[0:CG, 7, g * NB:(g + 1) * NB], s.c1[:, (g0 + g) * CG:(g0 + g + 1) * CG],
                                    s.hnew[:, :, g0 + g], start=True, stop=True)
                ins.then_inc(s_ysp, 1)


def stage_s5_states(k, s):
    nc, o = k.nc, k.o
    with ExitStack() as st:
        fp = k.sb(st, "fin_rows", [GRP, P])
        hs = k.sb(st, "hs_rows", [P, 2, P])
        s_tr, s_c, s_w = k.sem("fin_psum"), k.sem("fin_out"), k.sem("fin_stored")
        with nc.Block() as block:
            @block.tensor
            def _(pe):
                pe.matmul(k.ps[0:GRP, 0, 0:P], s.fin_c[:, :], k.ident[:, :], start=True, stop=False)
                pe.matmul(k.ps[0:GRP, 0, 0:P], s.fin_s[:, :], s.swap[:, :], start=False, stop=True)
                h = s.hnew[:, :, :].rearrange("p b g -> p (b g)")
                pe.transpose(k.ps[:, 1, 0:P], h[:, 0:P], k.ident[:, :])
                pe.transpose(k.ps[:, 1, P:2 * P], h[:, P:2 * P], k.ident[:, :]).then_inc(s_tr, 1)

            @block.vector
            def _(dve):
                dve.wait_ge(s_tr, 1)
                dve.tensor_copy(fp[:, :], k.ps[0:GRP, 0, 0:P])
                dve.tensor_copy(hs[:, :, :], k.ps[:, 1, 0:2 * P].rearrange("p (a c) -> p a c", a=2)).then_inc(s_c, 1)

            @block.sync
            def _(sp):
                sp.wait_ge(s_c, 1)
                for n, part in enumerate(("re", "im")):
                    cs = slice(n * NS, (n + 1) * NS)
                    sp.dma_start(o[f"s5_{part}_prompt"][0, 0], fp[:, cs]).then_inc(s_w, 16)
                    dst = o[f"s5_{part}_sample"][0].rearrange("b g p -> (b g) p").rearrange("(a r) p -> r a p", r=P)
                    sp.dma_start(dst, hs[:, :, cs]).then_inc(s_w, 16)
                sp.wait_ge(s_w, 64)


def s5(k, uT):
    nc = k.nc
    with ExitStack() as st:
        k.recycle()
        s = S5Tensors(k, st)
        stage_s5_params(k, s)
        for qd in range(4):
            stage_s5_quarter(k, s, qd, uT[:, qd, :])
        stage_s5_states(k, s)
        k.recycle()
    with ExitStack() as st:
        sig = k.sb(st, "sig", [P, 4, TA])
        with nc.Block() as block:
            @block.scalar
            def _(act):
                for m in range(4):
                    act.activation(uT[:, m, :], uT[:, m, :], ACT.Gelu_apprx_tanh)
        stage_linear(k, k.i["s5_w_glu"][0], 4, [(m * P, P) for m in range(4)],
                     lambda a, c: uT[:, a, c * CH:(c + 1) * CH],
                     lambda m, c, ps: nc.scalar.activation(sig[:, m, c * CH:(c + 1) * CH], ps, ACT.Sigmoid,
                                                           bias=k.cols[:, C_BGLU + m:C_BGLU + m + 1]), True)
        with nc.Block() as block:
            @block.vector
            def _(dve):
                for m in range(4):
                    dve.tensor_tensor(uT[:, m, :], uT[:, m, :], sig[:, m, :], ALU.mult)


def stage_gates(k, gT, gates):
    nc = k.nc
    with ExitStack() as st:
        gs = k.sb(st, "gates_rows", [NB, 24])
        s_tr, s_c, s_w = k.sem("gates_psum"), k.sem("gates_out"), k.sem("gates_moved")
        with nc.Block() as block:
            @block.tensor
            def _(pe):
                for t in range(TT):
                    pe.transpose(k.ps[:, 0, t * 24:(t + 1) * 24], gT[:, t * P:(t + 1) * P], k.ident[0:24, 0:24])
                pe.transpose(k.ps[0:NB, 0, 192:216], gT[:, T:TA], k.ident[0:24, 0:24]).then_inc(s_tr, 1)

            @block.vector
            def _(dve):
                dve.wait_ge(s_tr, 1)
                dve.tensor_copy(gates[:, :, :], k.ps[:, 0, 0:192].rearrange("p (t c) -> p t c", c=24))
                dve.tensor_copy(gs[:, :], k.ps[0:NB, 0, 192:216]).then_inc(s_c, 1)

            @block.sync
            def _(sp):
                sp.wait_ge(s_c, 1)
                sp.dma_start(k.d_gates, gs[:, :]).then_inc(s_w, 16)
                sp.wait_ge(s_w, 16)
                sp.dma_start(k.gate_s[:, :], k.d_gates.rearrange("b (h c) -> (b h) c", c=3)).then_inc(s_w, 16)
                sp.wait_ge(s_w, 32)


def stage_compress_prompt(k, w1s, w2, posb, kvT, kc, vc):
    nc, i = k.nc, k.i
    with ExitStack() as st:
        w1p = k.sb(st, "w1p", [P, 2, 16, P])
        hid = k.sb(st, "hidc", [HD, 4, 64])
        t1 = k.sb(st, "half1", [HD, 4, 64])
        s_w, s_u, s_t, s_hid, s_g, s_o = (k.sem(x) for x in (
            "w1_in", "u_psum", "half1_out", "hid_summed", "hidc_ready", "rows_psum"))
        loads = []
        for kv in range(2):
            w1 = i["nsa_cmp_w1"][0, kv]
            for r in range(2):
                half = w1[r * 1024:(r + 1) * 1024, :]
                loads.append((w1s[:, kv, :, r * HD:(r + 1) * HD], half.rearrange("(a p) h -> p a h", p=P)))
                for g in range(2):
                    loads.append((w1p[g * HD:(g + 1) * HD, kv, :, r * HD:(r + 1) * HD],
                                  half.rearrange("(s d) h -> d s h", d=HD)))
            loads.append((w2[:, kv, :], i["nsa_cmp_w2"][0, kv]))
        with nc.Block() as block:
            @block.sync
            def _(sp):
                for dst, src in loads:
                    sp.dma_start(dst, src).then_inc(s_w, 16)

            @block.tensor
            def _(pe):
                pe.wait_ge(s_w, 16 * len(loads))
                for kv in range(2):
                    for r in range(2):
                        for a in range(8):
                            c = C_POS + kv * 16 + r * 8 + a
                            ins = pe.matmul(k.ps[0:HD, 7, kv:kv + 1], w1s[:, kv, a, r * HD:(r + 1) * HD],
                                            k.cols[:, c:c + 1], start=(r == 0 and a == 0), stop=(r == 1 and a == 7))
                for x in range(4):
                    kv, g = x // 2, x % 2
                    gr = slice(g * HD, (g + 1) * HD)
                    for s in range(16):
                        ins = pe.matmul(k.ps[:, x, 0:64], w1p[gr, kv, s, :], kvT[gr, kv, s:T:16],
                                        start=(s == 0), stop=(s == 15))
                    ins.then_inc(s_u, 1)
                for x in range(4):
                    kv, g = x // 2, x % 2
                    pe.wait_ge(s_g, x + 1)
                    if kv == 0:
                        pe.matmul(k.ps[g * HD:(g + 1) * HD, 4, 0:NCK], w2[:, 0, :], hid[:, x, 0:NCK],
                                  start=True, stop=True)
                    else:
                        ins = pe.matmul(k.ps[0:NCK, 5, g * HD:(g + 1) * HD], hid[:, x, 0:NCK], w2[:, 1, :],
                                        start=True, stop=True)
                ins.then_inc(s_o, 1)

            @block.scalar
            def _(act):
                for x in range(4):
                    act.wait_ge(s_u, x + 1)
                    act.copy(t1[:, x, 0:NCK], k.ps[HD:P, x, 1:64]).then_inc(s_t, 1)
                for x in range(4):
                    act.wait_ge(s_hid, x + 1)
                    act.activation(hid[:, x, 0:NCK], hid[:, x, 0:NCK], ACT.Gelu_apprx_tanh,
                                   bias=posb[:, x // 2:x // 2 + 1]).then_inc(s_g, 1)

            @block.vector
            def _(dve):
                for x in range(4):
                    dve.wait_ge(s_t, x + 1)
                    if x == 0:
                        dve.tensor_copy(posb[:, :], k.ps[0:HD, 7, 0:2])
                    dve.tensor_tensor(hid[:, x, 0:NCK], k.ps[0:HD, x, 0:NCK], t1[:, x, 0:NCK], ALU.add).then_inc(s_hid, 1)
                dve.wait_ge(s_o, 1)
                dve.tensor_copy(kc[:, 0:NCK], k.ps[:, 4, 0:NCK])
                dve.tensor_copy(vc[0:NCK, :], k.ps[0:NCK, 5, 0:P])


def stage_sample_query(k, qT, qb):
    nc = k.nc
    s_z = k.sem("qb_zeroed")
    with nc.Block() as block:
        @block.vector
        def _(dve):
            dve.memset(qb[:, :, :], 0.0).then_inc(s_z, 1)
            dve.wait_ge(s_z, 1)
            for h in range(AH):
                g, base = h // 4, (h % 2) * HD
                first = qb[g * HD:g * HD + 1, 0, h:h + 1]
                dst = bass.AP(first.tensor, first.offset, [[NB * NB * AH, HD], [NB * AH + AH, NB]])
                dve.tensor_copy(dst, qT[base:base + HD, h // 2, T:TA])


class SampleSoftmax:

    def __init__(self, k, st, name):
        self.small = k.sb(st, name + "_small", [64, 4])
        self.s_max, self.s_exp = k.sem(name + "_max"), k.sem(name + "_exp")

    def maximum(self, dve, scores):
        dve.tensor_reduce(self.small[:, 0:1], scores, AX, ALU.max, negate=True).then_inc(self.s_max, 1)

    def exp(self, act, probs, scores):
        act.wait_ge(self.s_max, 1)
        act.activation(probs, scores, ACT.Exp, bias=self.small[:, 0:1], accum_out=self.small[:, 1:2]).then_inc(self.s_exp, 1)

    def normalise(self, dve, link, probs, gate):
        dve.wait_ge(self.s_exp, 1)
        link(dve.reciprocal(self.small[:, 2:3], self.small[:, 1:2]))
        if gate is not None:
            link(dve.tensor_tensor(self.small[:, 2:3], self.small[:, 2:3], gate, ALU.mult))
        link(dve.tensor_scalar(probs, probs, self.small[:, 2:3], None, ALU.mult))


def stage_window_sample(k, qb, oacc):
    nc, i = k.nc, k.i
    cache = i["cache_nsa_win"][0].rearrange("b t k g d -> b t (k g d)")
    new = k.o["nsa_win_sample"][0].rearrange("b t k g d -> b t (k g d)")
    with ExitStack() as st:
        kv = k.sb(st, "win_rows", [P, NB, 4, 4 * HD])
        kT = k.sb(st, "win_kT", [P, 2, 512])
        sc = k.sb(st, "win_scores", [64, 512])
        pT = k.sb(st, "win_pT", [P, 4, 64])
        sm = SampleSoftmax(k, st, "win")
        s_in, s_tr, s_kT, s_qk, s_dve, s_p, s_pTp, s_pT, s_o = (k.sem(x) for x in (
            "win_in", "win_tr", "win_kT_ready", "win_qk", "win_dve", "win_probs", "win_pT_psum", "win_pT_ready", "win_o"))
        with nc.Block() as block:
            @block.sync
            def _(sp):
                for b in range(NB):
                    sp.dma_start(kv[0:127, b, :, :].rearrange("p j c -> p (j c)"),
                                 cache[b, 1:509, :].rearrange("(p j) c -> p (j c)", j=4)).then_inc(s_in, 16)
                    sp.dma_start(kv[127:128, b, 0:3, :], cache[b:b + 1, 509:512, :]).then_inc(s_in, 16)
                    sp.dma_start(kv[127:128, b, 3, :], new[b:b + 1, 511, :]).then_inc(s_in, 16)

            @block.tensor
            def _(pe):
                pe.wait_ge(s_in, 48 * NB)
                for b in range(NB + 1):
                    if b < NB:
                        if b >= 2:
                            pe.wait_ge(s_kT, b - 1)
                        for j in range(4):
                            ins = pe.transpose(k.ps[:, b % 2, j * P:(j + 1) * P], kv[:, b, j, 0:P], k.ident[:, :])
                        ins.then_inc(s_tr, 1)
                    if b >= 1:
                        pe.wait_ge(s_kT, b)
                        pe.matmul(k.ps[0:64, 2, :], qb[:, b - 1, :], kT[:, (b - 1) % 2, :], start=(b == 1),
                                  stop=(b == NB)).then_inc(s_qk, 1)
                pe.wait_ge(s_p, 1)
                for j in range(4):
                    ins = pe.transpose(k.ps[:, 3, j * 64:(j + 1) * 64], sc[:, j * P:(j + 1) * P], k.ident[0:64, 0:64])
                ins.then_inc(s_pTp, 1)
                pe.wait_ge(s_pT, 1)
                for b in range(NB):
                    for g in range(G):
                        c0 = b * AH + g * 4
                        for j in range(4):
                            ins = pe.matmul(k.ps[0:HD, 4, c0:c0 + 4], kv[:, b, j, P + g * HD:P + (g + 1) * HD],
                                            pT[:, j, c0:c0 + 4], start=(j == 0), stop=(j == 3))
                ins.then_inc(s_o, 1)

            @block.scalar
            def _(act):
                sm.exp(act, sc[:, :], sc[:, :])

            @block.vector
            def _(dve):
                link = Chain(dve, s_dve)
                for b in range(NB):
                    dve.wait_ge(s_tr, b + 1)
                    if b >= 2:
                        dve.wait_ge(s_qk, b - 1)
                    dve.tensor_copy(kT[:, b % 2, :], k.ps[:, b % 2, :]).then_inc(s_kT, 1)
                dve.wait_ge(s_qk, NB)
                link(dve.tensor_tensor(sc[:, :], k.ps[0:64, 2, :], k.b_win[:, :], ALU.add))
                sm.maximum(dve, sc[:, :])
                sm.normalise(dve, link, sc[:, :], k.gate_s[:, 2:3])
                dve.sem_inc(s_p, 1)
                dve.wait_ge(s_pTp, 1)
                dve.tensor_copy(pT[:, :, :], k.ps[:, 3, 0:256].rearrange("p (j c) -> p j c", c=64)).then_inc(s_pT, 1)
                dve.wait_ge(s_o, 1)
                dve.tensor_copy(oacc[:, :], k.ps[0:HD, 4, 0:64])


def stage_index(k, idx):
    nc, i = k.nc, k.i
    with ExitStack() as st:
        pti = k.sb(st, "pages_int", [NB, NPAGE], I32)
        pt = k.sb(st, "pages", [NB, NPAGE])
        ptT = k.sb(st, "pagesT", [NPAGE + 1, NB])
        ex = k.sb(st, "expand", [NPAGE + 1, 2, P])
        s_in, s_c, s_t, s_tc, s_x, s_one = (k.sem(x) for x in (
            "pages_in", "pages_float", "pages_tr", "pagesT_ready", "idx_psum", "pagesT_ones"))
        with nc.Block() as block:
            @block.sync
            def _(sp):
                sp.dma_start(pti[:, :], i["page_table"]).then_inc(s_in, 16)
                sp.dma_start(ex[:, :, :], i["index_onehot"][0:NPAGE + 1, 0:2 * P].rearrange("a (h p) -> a h p", h=2)).then_inc(s_in, 16)

            @block.vector
            def _(dve):
                dve.memset(ptT[:, :], 1.0).then_inc(s_one, 1)
                dve.wait_ge(s_in, 32)
                dve.tensor_copy(pt[:, :], pti[:, :]).then_inc(s_c, 1)
                dve.wait_ge(s_t, 1)
                dve.wait_ge(s_one, 1)
                dve.tensor_copy(ptT[0:NPAGE, :], k.ps[0:NPAGE, 0, 0:NB]).then_inc(s_tc, 1)
                dve.wait_ge(s_x, 1)
                dve.tensor_copy(idx[:, :, :], k.ps[:, 1, 0:2 * NB].rearrange("p (h b) -> p h b", h=2))

            @block.tensor
            def _(pe):
                pe.wait_ge(s_c, 1)
                pe.transpose(k.ps[0:NPAGE, 0, 0:NB], pt[:, :], k.ident[0:NB, 0:NB]).then_inc(s_t, 1)
                pe.wait_ge(s_tc, 1)
                for h in range(2):
                    ins = pe.matmul(k.ps[:, 1, h * NB:(h + 1) * NB], ex[:, h, :], ptT[:, :], start=True, stop=True)
                ins.then_inc(s_x, 1)


def stage_compress_sample(k, idx, w1s, w2, posb, kc, vc):
    nc = k.nc
    table = k.i["cache_nsa_cmp"][0].rearrange("n (c s) k g d -> (n c) (s k g d)", s=16)
    units = [(b, h) for b in range(NB) for h in range(2)]
    with ExitStack() as st:
        X = k.sb(st, "chunks", [P, 3, 16 * 4 * HD])
        R = k.sb(st, "grouped", [P, 2, 2, 16 * HD])
        xT = k.sb(st, "chunksT", [P, 4, 4, P])
        hid = k.sb(st, "hids", [HD, 2, 4, 256])
        t1 = k.sb(st, "half1s", [HD, 2, 256])
        s_in = [k.sem(f"chunks_in{n}") for n in range(3)]
        s_r = [k.sem("keys_grouped"), k.sem("values_grouped")]
        s_tr, s_u, s_z, s_t, s_hid, s_g, s_w2, s_kv = (k.sem(x) for x in (
            "chunksT_psum", "us_psum", "hids_zeroed", "half1s_out", "hids_summed", "hids_ready", "w2_done", "kv_out"))
        s_xT = [k.sem("chunksT_act"), k.sem("chunksT_dve")]
        with nc.Block() as block:
            @block.gpsimd
            def _(pool):
                for u, (b, h) in enumerate(units):
                    if u >= 3:
                        pool.wait_ge(s_r[0], u - 2)
                        pool.wait_ge(s_r[1], u - 2)
                    pool.indirect_dma_start(X[:, u % 3, :], None, table,
                                            bass.IndirectOffsetOnAxis(ap=idx[:, h, b:b + 1], axis=0)).then_inc(s_in[u % 3], 16)

            def regroup(eng, kv, u):
                eng.wait_ge(s_in[u % 3], 16 * (u // 3 + 1))
                if u >= 1:
                    eng.wait_ge(s_tr, 8 * (u - 1) + 4 * kv + 4)
                src = X[:, u % 3, :].rearrange("p (s k g d) -> p k g s d", k=2, g=2, d=HD)[:, kv]
                copy = eng.tensor_copy if kv else eng.copy
                copy(R[:, kv, :, :].rearrange("p g (s d) -> p g s d", d=HD), src).then_inc(s_r[kv], 1)

            def copy_out(eng, par, u):
                for q in range(8 * u + par, 8 * u + 8, 2):
                    eng.wait_ge(s_tr, q + 1)
                    if q >= 4:
                        eng.wait_ge(s_u, q - 3)
                    copy = eng.tensor_copy if par else eng.copy
                    copy(xT[:, q % 4, :, :], k.ps[:, q % 2, :].rearrange("p (a n) -> p a n", a=4)).then_inc(s_xT[par], 1)

            @block.tensor
            def _(pe):
                def products(q):
                    u, x, half = q // 8, (q % 8) // 2, q % 2
                    b, h = units[u]
                    if h == 0 and half == 0 and b >= 1:
                        pe.wait_ge(s_hid, 4 * (b - 1) + x + 1)
                    pe.wait_ge(s_xT[q % 2], q // 2 + 1)
                    for a in range(4):
                        ins = pe.matmul(k.ps[:, 2 + x, h * P:(h + 1) * P], w1s[:, x // 2, 4 * half + a, :],
                                        xT[:, q % 4, a, :], start=(half == 0 and a == 0), stop=(half == 1 and a == 3))
                    ins.then_inc(s_u, 1)

                def second(b):
                    if b >= 1:
                        pe.wait_ge(s_kv, 2 * b)
                    for x in range(4):
                        kv, g = x // 2, x % 2
                        pe.wait_ge(s_g, 4 * b + x + 1)
                        if kv == 0:
                            ins = pe.matmul(k.ps[g * HD:(g + 1) * HD, 6, 0:256], w2[:, 0, :], hid[:, b % 2, x, :],
                                            start=True, stop=True)
                        else:
                            for h in range(2):
                                c0 = h * P + g * HD
                                ins = pe.matmul(k.ps[:, 7, c0:c0 + HD], hid[:, b % 2, x, h * P:(h + 1) * P], w2[:, 1, :],
                                                start=True, stop=True)
                        ins.then_inc(s_w2, 1)

                for q in range(8 * len(units) + 1):
                    if q < 8 * len(units):
                        u, x, half = q // 8, (q % 8) // 2, q % 2
                        pe.wait_ge(s_r[x // 2], u + 1)
                        if q >= 2:
                            pe.wait_ge(s_xT[q % 2], (q - 2) // 2 + 1)
                        for a in range(4):
                            c0 = (4 * half + a) * P
                            ins = pe.transpose(k.ps[:, q % 2, a * P:(a + 1) * P], R[:, x // 2, x % 2, c0:c0 + P], k.ident[:, :])
                        ins.then_inc(s_tr, 1)
                    if q >= 1:
                        products(q - 1)
                    if q % 16 == 8 and q >= 24:
                        second(q // 16 - 1)
                second(NB - 1)

            def hidden(eng, b, part):
                for x in range(4):
                    if part == "act":
                        eng.wait_ge(s_u, 16 * b + 8 + 2 * x + 2)
                        if 4 * b + x >= 2:
                            eng.wait_ge(s_hid, 4 * b + x - 1)
                        eng.copy(t1[:, x % 2, 0:255], k.ps[HD:P, 2 + x, 1:256]).then_inc(s_t, 1)
                    elif part == "dve":
                        eng.wait_ge(s_t, 4 * b + x + 1)
                        if b >= 2:
                            eng.wait_ge(s_w2, 4 * (b - 2) + x + 1)
                        eng.tensor_tensor(hid[:, b % 2, x, 0:255], k.ps[0:HD, 2 + x, 0:255], t1[:, x % 2, 0:255],
                                          ALU.add).then_inc(s_hid, 1)
                    else:
                        eng.wait_ge(s_hid, 4 * b + x + 1)
                        eng.activation(hid[:, b % 2, x, :], hid[:, b % 2, x, :], ACT.Gelu_apprx_tanh,
                                       bias=posb[:, x // 2:x // 2 + 1]).then_inc(s_g, 1)

            @block.scalar
            def _(act):
                act.wait_ge(s_z, 1)
                regroup(act, 0, 0)
                for u, (b, h) in enumerate(units):
                    copy_out(act, 0, u)
                    if u + 1 < len(units):
                        regroup(act, 0, u + 1)
                    if h == 1:
                        hidden(act, b, "act")
                        hidden(act, b, "gelu")

            @block.vector
            def _(dve):
                dve.memset(hid[:, :, :, 255:256], 0.0).then_inc(s_z, 1)
                dve.wait_ge(s_z, 1)

                def rows_out(b):
                    dve.wait_ge(s_w2, 4 * b + 4)
                    dve.tensor_copy(kc[:, b, :], k.ps[:, 6, 0:256]).then_inc(s_kv, 1)
                    dve.tensor_copy(vc[:, :, b, :], k.ps[:, 7, 0:256].rearrange("p (h c) -> p h c", h=2)).then_inc(s_kv, 1)

                regroup(dve, 1, 0)
                for u, (b, h) in enumerate(units):
                    if h == 1 and b >= 1:
                        rows_out(b - 1)
                    copy_out(dve, 1, u)
                    if u + 1 < len(units):
                        regroup(dve, 1, u + 1)
                    if h == 1:
                        hidden(dve, b, "dve")
                rows_out(NB - 1)


def stage_cmp_sample(k, qb, kc, vc, oacc, imp):
    nc = k.nc
    with ExitStack() as st:
        sc = k.sb(st, "cmp_scores", [64, 256])
        pr = k.sb(st, "cmp_probs", [64, 256])
        pT = k.sb(st, "cmp_pT", [P, 2, 2, 64])
        cover = k.sb(st, "cover", [P, 2, 64])
        gsum = k.sb(st, "group_sum", [64, 64])
        part = k.sb(st, "imp_part", [64, 64])
        sm = SampleSoftmax(k, st, "cmp")
        s_in, s_qk, s_dve, s_p, s_pTp, s_pT, s_o, s_ip, s_ic, s_im = (k.sem(x) for x in (
            "cover_in", "cmp_qk", "cmp_dve", "cmp_p", "cmp_pT_psum", "cmp_pT_ready", "cmp_o", "imp_psum", "imp_part_ready",
            "imp_sum"))
        with nc.Block() as block:
            @block.sync
            def _(sp):
                sp.dma_start(cover[:, :, :], k.i["index_onehot"][:, 384:512].rearrange("p (h s) -> p h s", h=2)).then_inc(s_in, 16)
                sp.dma_start(gsum[:, :], k.i["index_onehot"][0:64, 512:576]).then_inc(s_in, 16)

            @block.tensor
            def _(pe):
                for b in range(NB):
                    ins = pe.matmul(k.ps[0:64, 0, 0:NCS], qb[:, b, :], kc[:, b, 0:NCS], start=(b == 0), stop=(b == NB - 1))
                ins.then_inc(s_qk, 1)
                for n, src in enumerate((sc, pr)):
                    pe.wait_ge(s_p, n + 1)
                    for h in range(2):
                        ins = pe.transpose(k.ps[:, 1, (2 * n + h) * 64:(2 * n + h + 1) * 64], src[:, h * P:(h + 1) * P],
                                           k.ident[0:64, 0:64])
                ins.then_inc(s_pTp, 1)
                pe.wait_ge(s_pT, 1)
                pe.wait_ge(s_in, 32)
                for h in range(2):
                    ins = pe.matmul(k.ps[0:64, 2, 0:64], pT[:, 0, h, :], cover[:, h, :], start=(h == 0), stop=(h == 1))
                ins.then_inc(s_ip, 1)
                pe.wait_ge(s_ic, 1)
                pe.matmul(k.ps[0:64, 3, 0:64], gsum[:, :], part[:, :], start=True, stop=True).then_inc(s_im, 1)
                for b in range(NB):
                    for g in range(G):
                        c0 = b * AH + g * 4
                        for h in range(2):
                            ins = pe.matmul(k.ps[0:HD, 4, c0:c0 + 4], vc[:, h, b, g * HD:(g + 1) * HD],
                                            pT[:, 1, h, c0:c0 + 4], start=(h == 0), stop=(h == 1))
                ins.then_inc(s_o, 1)

            @block.scalar
            def _(act):
                sm.exp(act, sc[:, 0:NCS], k.ps[0:64, 0, 0:NCS])

            @block.vector
            def _(dve):
                link = Chain(dve, s_dve)
                link(dve.memset(sc[:, NCS:256], 0.0))
                dve.wait_ge(s_qk, 1)
                sm.maximum(dve, k.ps[0:64, 0, 0:NCS])
                sm.normalise(dve, link, sc[:, 0:NCS], None)
                dve.sem_inc(s_p, 1)
                link(dve.tensor_scalar(pr[:, :], sc[:, :], k.gate_s[:, 0:1], None, ALU.mult))
                dve.sem_inc(s_p, 1)
                dve.wait_ge(s_pTp, 1)
                dve.tensor_copy(pT[:, :, :, :], k.ps[:, 1, 0:256].rearrange("p (n h c) -> p n h c", n=2, h=2)).then_inc(s_pT, 1)
                dve.wait_ge(s_ip, 1)
                dve.tensor_copy(part[:, :], k.ps[0:64, 2, 0:64]).then_inc(s_ic, 1)
                dve.wait_ge(s_im, 1)
                link(dve.tensor_copy(imp[:, :], k.ps[0:64, 3, 0:64]))
                dve.tensor_scalar(imp[:, 0:64:63], imp[:, 0:64:63], 1000.0, None, ALU.add)
                dve.wait_ge(s_o, 1)
                dve.tensor_tensor(oacc[:, :], oacc[:, :], k.ps[0:HD, 4, 0:64], ALU.add)


def stage_select(k, imp, sidx, bias):
    nc, i = k.nc, k.i
    with ExitStack() as st:
        pti = k.sb(st, "ptb_int", [64, NPAGE], I32)
        pt = k.sb(st, "ptb", [64, NPAGE])
        top = k.sb(st, "top", [64, 16])
        left = k.sb(st, "left", [64, 64])
        tix = k.sb(st, "top_index", [64, 16], U32)
        pgi = k.sb(st, "page_int", [64, 2, 16], U32)
        blk = k.sb(st, "blockf", [64, 16])
        pg = k.sb(st, "page_par", [64, 2, 16])
        io_i = k.sb(st, "iota_int", [64, NPAGE], I32)
        io = k.sb(st, "iota_f", [64, NPAGE])
        hot = k.sb(st, "hot", [64, 16, NPAGE])
        base = k.sb(st, "base", [64, 16])
        e = k.sb(st, "is_near", [64, 2, 16])
        tmp = k.sb(st, "bias_tmp", [64, L, 16, 8])
        bT = k.sb(st, "baseT", [17, 64])
        ex = k.sb(st, "expand2", [17, P])
        s_in, s_io, s_dve, s_b, s_t, s_tc, s_x = (k.sem(x) for x in (
            "ptb_in", "iota_made", "sel_dve", "base_ready", "baseT_psum", "baseT_ready", "sidx_psum"))
        with nc.Block() as block:
            @block.sync
            def _(sp):
                for b in range(NB):
                    sp.dma_start(pti[b * AH:(b + 1) * AH, :], i["page_table"][b:b + 1, :].broadcast_to([AH, NPAGE])).then_inc(s_in, 16)
                sp.dma_start(ex[:, :], i["index_onehot"][0:17, 256:384]).then_inc(s_in, 16)

            @block.gpsimd
            def _(pool):
                pool.iota(io_i[:, :], pattern=[[1, NPAGE]], base=0, channel_multiplier=0).then_inc(s_io, 1)

            @block.vector
            def _(dve):
                link = Chain(dve, s_dve)
                link(dve.memset(bT[:, :], 1.0))
                link(dve.max(top[:, 0:8], imp[:, :]))
                link(dve.max_index(tix[:, 0:8], top[:, 0:8], imp[:, :]))
                link(dve.match_replace(left[:, :], top[:, 0:8], imp[:, :], NEG))
                link(dve.max(top[:, 8:16], left[:, :]))
                link(dve.max_index(tix[:, 8:16], top[:, 8:16], left[:, :]))
                link(dve.tensor_copy(blk[:, :], tix[:, :]))
                link(dve.tensor_scalar(pgi[:, 0, :], tix[:, :], 1, None, ALU.logical_shift_right))
                link(dve.tensor_scalar(pgi[:, 1, :], tix[:, :], 1, None, ALU.bitwise_and))
                link(dve.tensor_copy(pg[:, :, :], pgi[:, :, :]))
                dve.wait_ge(s_in, 16 * (NB + 1))
                dve.wait_ge(s_io, 1)
                link(dve.tensor_copy(pt[:, :], pti[:, :]))
                link(dve.tensor_copy(io[:, :], io_i[:, :]))
                link(dve.tensor_tensor(hot[:, :, :], bc(pg[:, 0, :], [[1, 16], [0, NPAGE]]), bc(io[:, :], [[0, 16], [1, NPAGE]]),
                                       ALU.is_equal))
                link(dve.tensor_tensor(hot[:, :, :], hot[:, :, :], bc(pt[:, :], [[0, 16], [1, NPAGE]]), ALU.mult))
                link(dve.tensor_reduce(base[:, :], hot[:, :, :], AX, ALU.add))
                link(dve.tensor_scalar(base[:, :], base[:, :], 16.0, None, ALU.mult))
                link(dve.scalar_tensor_tensor(out=base[:, :], in0=pg[:, 1, :], scalar=8.0, in1=base[:, :], op0=ALU.mult, op1=ALU.add))
                dve.sem_inc(s_b, 1)
                for n in range(2):
                    link(dve.tensor_scalar(e[:, n, :], blk[:, :], 62.0 + n, None, ALU.is_equal))
                for n in range(2):
                    near = bc(k.b_sel[:, n * 64:n * 64 + 1], [[8, L], [0, 16], [1, 8]])
                    which = bc(e[:, n, 0:1], [[0, L], [1, 16], [0, 8]])
                    link(dve.tensor_tensor((tmp, bias)[n][:, :, :, :], near, which, ALU.mult))
                link(dve.tensor_tensor(bias[:, :, :, :], bias[:, :, :, :], tmp[:, :, :, :], ALU.add))
                link(dve.memset(bias[:, :, 15, :], NEG))
                link(dve.tensor_copy(bias[:, 0, 15, 0:1], k.b_sel[:, 128:129]))
                dve.wait_ge(s_t, 1)
                dve.tensor_copy(bT[0:16, :], k.ps[0:16, 0, 0:64]).then_inc(s_tc, 1)
                dve.wait_ge(s_x, 1)
                dve.tensor_copy(sidx[:, :], k.ps[:, 1, 0:16])

            @block.tensor
            def _(pe):
                pe.wait_ge(s_b, 1)
                pe.transpose(k.ps[0:16, 0, 0:64], base[:, :], k.ident[0:64, 0:64]).then_inc(s_t, 1)
                pe.wait_ge(s_tc, 1)
                pe.matmul(k.ps[:, 1, 0:16], ex[:, :], bT[:, 0:64:4], start=True, stop=True).then_inc(s_x, 1)


def stage_sel_sample(k, qb, sidx, bias, oacc):
    nc = k.nc
    table = k.i["cache_nsa_sel"][0].rearrange("n (c s) k g d -> (n c) (s k g d)", s=8)
    new = kv_rows(k.o["nsa_sel_sample"])
    NX = 3
    n_u = 2 * NB
    with ExitStack() as st:
        X = k.sb(st, "sel_rows", [P, NX, 8, 4 * HD])
        V = k.sb(st, "sel_v", [P, n_u, 8, HD])
        kT = k.sb(st, "sel_kT", [P, 2, 1024])
        sc = k.sb(st, "sel_scores", [64, 1024])
        pT = k.sb(st, "sel_pT", [P, 8, 64])
        sm = SampleSoftmax(k, st, "sel")
        s_in = [k.sem(f"sel_in{n}") for n in range(NX)]
        s_new = [k.sem(f"sel_new{n}") for n in range(NX)]
        s_z, s_tr, s_kT, s_v, s_qk, s_dve, s_p, s_pTp, s_pT, s_o = (k.sem(x) for x in (
            "sel_zeroed", "sel_tr", "sel_kT_ready", "sel_v_ready", "sel_qk", "sel_dve", "sel_probs", "sel_pT_psum",
            "sel_pT_ready", "sel_o"))
        with nc.Block() as block:
            @block.gpsimd
            def _(pool):
                pool.wait_ge(s_z, 1)
                for u in range(n_u):
                    if u >= NX:
                        pool.wait_ge(s_tr, u - NX + 1)
                        pool.wait_ge(s_v, u - NX + 1)
                    pool.indirect_dma_start(X[0:120, u % NX, :, :].rearrange("p j c -> p (j c)"), None, table,
                                            bass.IndirectOffsetOnAxis(ap=sidx[0:120, u:u + 1], axis=0)).then_inc(s_in[u % NX], 16)

            @block.sync
            def _(sp):
                sp.wait_ge(s_z, 1)
                for u in range(n_u):
                    if u >= NX:
                        sp.wait_ge(s_tr, u - NX + 1)
                        sp.wait_ge(s_v, u - NX + 1)
                    sp.dma_start(X[120:121, u % NX, 0, :], new[u // 2:u // 2 + 1, :]).then_inc(s_new[u % NX], 16)

            @block.tensor
            def _(pe):
                def scores(b):
                    pe.wait_ge(s_kT, 2 * b + 2)
                    for c in range(2):
                        ins = pe.matmul(k.ps[0:64, 4 + c, :], qb[:, b, :], kT[:, b % 2, c * 512:(c + 1) * 512],
                                        start=(b == 0), stop=(b == NB - 1))
                    ins.then_inc(s_qk, 1)

                for u in range(n_u):
                    pe.wait_ge(s_in[u % NX], 16 * (u // NX + 1))
                    pe.wait_ge(s_new[u % NX], 16 * (u // NX + 1))
                    if u >= 2:
                        pe.wait_ge(s_kT, u - 1)
                    for j in range(8):
                        bank = 2 * (u % 2) + j // 4
                        ins = pe.transpose(k.ps[:, bank, (j % 4) * P:(j % 4 + 1) * P], X[:, u % NX, j, 0:P], k.ident[:, :])
                    ins.then_inc(s_tr, 1)
                    if u % 2 == 0 and u >= 2:
                        scores(u // 2 - 1)
                scores(NB - 1)
                pe.wait_ge(s_p, 1)
                for j in range(8):
                    ins = pe.transpose(k.ps[:, 6, j * 64:(j + 1) * 64], sc[:, j * P:(j + 1) * P], k.ident[0:64, 0:64])
                ins.then_inc(s_pTp, 1)
                pe.wait_ge(s_pT, 1)
                pe.wait_ge(s_v, n_u)
                for u in range(n_u):
                    for j in range(8):
                        ins = pe.matmul(k.ps[0:HD, 7, u * 4:u * 4 + 4], V[:, u, j, :], pT[:, j, u * 4:u * 4 + 4],
                                        start=(j == 0), stop=(j == 7))
                ins.then_inc(s_o, 1)

            @block.scalar
            def _(act):
                for u in range(n_u):
                    act.wait_ge(s_in[u % NX], 16 * (u // NX + 1))
                    act.wait_ge(s_new[u % NX], 16 * (u // NX + 1))
                    act.copy(V[:, u, :, :], X[:, u % NX, :, P + (u % 2) * HD:P + (u % 2 + 1) * HD]).then_inc(s_v, 1)
                sm.exp(act, sc[:, :], sc[:, :])

            @block.vector
            def _(dve):
                link = Chain(dve, s_dve)
                dve.memset(X[96:P, :, :, :], 0.0).then_inc(s_z, 1)
                for u in range(n_u):
                    b, g = u // 2, u % 2
                    dve.wait_ge(s_tr, u + 1)
                    if b >= 2:
                        dve.wait_ge(s_qk, b - 1)
                    dve.tensor_copy(kT[g * HD:(g + 1) * HD, b % 2, :],
                                    k.ps[g * HD:(g + 1) * HD, 2 * g:2 * g + 2, :].rearrange("p a c -> p (a c)")).then_inc(s_kT, 1)
                dve.wait_ge(s_qk, NB)
                link(dve.tensor_tensor(sc[:, :], k.ps[0:64, 4:6, :].rearrange("p a c -> p (a c)"),
                                       bias[:, :, :, :].rearrange("p j s c -> p (j s c)"), ALU.add))
                sm.maximum(dve, sc[:, :])
                sm.normalise(dve, link, sc[:, :], k.gate_s[:, 1:2])
                dve.sem_inc(s_p, 1)
                dve.wait_ge(s_pTp, 1)
                dve.tensor_copy(pT[:, :, :], k.ps[:, 6, :].rearrange("p (j c) -> p j c", c=64)).then_inc(s_pT, 1)
                dve.wait_ge(s_o, 1)
                dve.tensor_tensor(oacc[:, :], oacc[:, :], k.ps[0:HD, 7, 0:64], ALU.add)


def stage_place_sample(k, oacc, oT):
    nc = k.nc
    with nc.Block() as block:
        @block.vector
        def _(dve):
            for par in range(2):
                src = oacc[:, :].rearrange("p (b f r) -> p f b r", b=NB, r=2)[:, :, :, par]
                dve.tensor_copy(oT[par * HD:(par + 1) * HD, :, T:TA], src)


def kv_rows(ap):
    return ap.rearrange("l b t k g d -> (l b t) (k g d)")


def layer_a(k):
    nc = k.nc
    i, o = k.i, k.o
    with ExitStack() as st:
        uT = k.sb(st, "uT", [P, 4, TA])
        gT = k.sb(st, "gT", [24, TA])
        w1s = k.sb(st, "w1s", [P, 2, 8, P])
        w2 = k.sb(st, "w2c", [HD, 2, HD])
        posb = k.sb(st, "posb", [HD, 2])
        qb = k.sb(st, "qb", [P, NB, NB * AH])
        k.gate_s = k.sb(st, "gate_s", [64, 3])
        with ExitStack() as st1:
            qT = k.sb(st1, "qT", [P, 4, TA])
            kvT = k.sb(st1, "kvT", [P, 6, TA])
            with ExitStack() as st2:
                xn = k.sb(st2, "xn", [P, KD, TA])
                stage_norm(k, xn, C_MIX)
                tiles = [(m * P, P) for m in range(10)] + [(1280, 24)] + [(1304 + m * P, P) for m in range(4)]

                def put(m, c, ps):
                    cs = slice(c * CH, (c + 1) * CH)
                    if m < 4:
                        return nc.scalar.copy(qT[:, m, cs], ps)
                    if m < 10:
                        return nc.scalar.copy(kvT[:, m - 4, cs], ps)
                    if m == 10:
                        return nc.scalar.activation(gT[:, cs], ps, ACT.Sigmoid)
                    return nc.scalar.copy(uT[:, m - 11, cs], ps)

                stage_linear(k, i["a_w_in"][0], KD, tiles, lambda a, c: xn[:, a, c * CH:(c + 1) * CH], put, True)
            s5(k, uT)
            gq, gk = C_GAIN, C_GAIN + 1
            stage_head_norm(k, [(qT[:, n, :], gq, True) for n in range(4)]
                            + [(kvT[:, n, :], gk, False) for n in (0, 2, 4)])
            stage_sample_query(k, qT, qb)
            k.recycle()
            with ExitStack() as st2:
                oT_prompt = k.sb(st2, "oT_prompt", [P, 4, T])
                tok = k.sb(st2, "kvrows", [P, TT, 6, P])
                gates = k.sb(st2, "gates", [P, TT, 24])
                kc = k.sb(st2, "kc_prompt", [P, 64])
                vc = k.sb(st2, "vc_prompt", [64, P])
                kx = k.sb(st2, "kx", [P, 2, TA])
                kcx = k.sb(st2, "kcx", [P, 64])
                with ExitStack() as st3:
                    stok = k.sb(st3, "kvrows_s", [NB, 6, P])
                    stores = []
                    for br, name in enumerate(("cmp", "sel", "win")):
                        t0 = 4 if name == "win" else 0
                        dst = kv_rows(o[f"nsa_{name}_prompt"])
                        for t in range(t0, TT):
                            stores.append((dst[(t - t0) * P:(t - t0 + 1) * P, :], tok[:, t, 2 * br:2 * br + 2, :]))
                    win = o["nsa_win_sample"][0].rearrange("b t k g d -> b t (k g d)")
                    stores.append((kv_rows(o["nsa_cmp_sample"]), stok[:, 0:2, :]))
                    stores.append((kv_rows(o["nsa_sel_sample"]), stok[:, 2:4, :]))
                    stores.append((win[:, 511, :], stok[:, 4:6, :]))
                    stores.append((win[:, 0:511, :], i["cache_nsa_win"][0, :, 1:512].rearrange("b t k g d -> b t (k g d)")))
                    stage_rows(k, [kvT[:, n, :] for n in range(6)], tok, stok, stores)
                stage_gates(k, gT, gates)
                stage_compress_prompt(k, w1s, w2, posb, kvT, kc, vc)
                stage_head_norm(k, [(kc[:, 0:NCK], gk, False)])
                stage_swap(k, [(kx[:, 0, :], kvT[:, 2, :]), (kx[:, 1, :], kvT[:, 4, :]), (kcx[:, 0:NCK], kc[:, 0:NCK])])
                head = lambda g: slice(g * HD, (g + 1) * HD)
                branches = [
                    dict(kind="cmp", k=kc, kx=kcx, v=lambda t, g: vc[0:NCK, head(g)]),
                    dict(kind="sel", k=kvT[:, 2, :], kx=kx[:, 0, :], first=lambda q: 0,
                         v=lambda t, g: tok[:, t, 3, head(g)]),
                    dict(kind="win", k=kvT[:, 4, :], kx=kx[:, 1, :], first=lambda q: max(0, q - 4),
                         v=lambda t, g: tok[:, t, 5, head(g)])]
                k.recycle()
                stage_attend(k, qT, AH, branches, oT_prompt, gates)
                stage_move(k, [(k.d_o.rearrange("p (f t) -> p f t", f=4), oT_prompt[:, :, :])])
        oT = k.sb(st, "oT", [P, 4, TA])
        oacc = k.sb(st, "oacc", [HD, NB * AH])
        stage_move(k, [(oT[:, :, 0:T], k.d_o.rearrange("p (f t) -> p f t", f=4))])
        stage_window_sample(k, qb, oacc)
        k.recycle()
        with ExitStack() as st1:
            idx = k.sb(st1, "chunk_index", [P, 2, NB], U32)
            imp = k.sb(st1, "imp", [64, 64])
            sidx = k.sb(st1, "sel_index", [P, 16], U32)
            bias = k.sb(st1, "sel_bias", [64, L, 16, 8])
            stage_index(k, idx)
            with ExitStack() as st2:
                kc = k.sb(st2, "kc_sample", [P, NB, 256])
                vc = k.sb(st2, "vc_sample", [P, 2, NB, P])
                stage_compress_sample(k, idx, w1s, w2, posb, kc, vc)
                stage_head_norm(k, [(kc[:, :, :].rearrange("p b n -> p (b n)"), C_GAIN + 1, False)])
                stage_cmp_sample(k, qb, kc, vc, oacc, imp)
            stage_select(k, imp, sidx, bias)
            k.recycle()
            stage_sel_sample(k, qb, sidx, bias, oacc)
        stage_place_sample(k, oacc, oT)
        stage_residual(k, i["a_w_out"][0], KD,
                       lambda a, c: (oT[:, a, c * CH:(c + 1) * CH] if a < 4 else uT[:, a - 4, c * CH:(c + 1) * CH]))


def stage_move(k, moves):
    s_m = k.sem("moved")
    with k.nc.Block() as block:
        @block.sync
        def _(sp):
            for dst, src in moves:
                sp.dma_start(dst, src).then_inc(s_m, 16)
            sp.wait_ge(s_m, 16 * len(moves))


def build(nc, ins, outs):
    with ExitStack() as ctx:
        k = Core(nc, ctx, ins, outs)
        k.ident = k.sb(ctx, "ident", [P, P])
        k.ones = k.sb(ctx, "ones", [P, P])
        k.headones = k.sb(ctx, "headones", [P, P])
        k.eps = k.sb(ctx, "eps", [P, 1])
        k.cols = k.sb(ctx, "cols", [P, N_COLA + 2 * N_CW])
        k.tab = k.sb(ctx, "tab", [33, CHD])
        k.sink = k.sb(ctx, "sink", [P, 2, CHD])
        k.b_win = k.sb(ctx, "b_win", [64, 512])
        k.b_swa = k.sb(ctx, "b_swa", [P, P])
        k.b_sel = k.sb(ctx, "b_sel", [64, 129])
        k.hT = k.sb(ctx, "hT", [P, KD, TA])
        k.ps = ctx.enter_context(nc.psum_tensor("ps", [P, 8, 512], F32))
        k.d_toep = nc.dram_tensor("toeplitz", [CHD, P, 384], F32, kind="Internal").ap()
        k.d_gates = nc.dram_tensor("gates_s", [NB, 24], F32, kind="Internal").ap()
        k.d_o = nc.dram_tensor("o_prompt", [P, 4 * T], F32, kind="Internal").ap()
        k.d_u = nc.dram_tensor("s5_u", [P, L * NC + NB], F32, kind="Internal").ap()
        k.d_y = nc.dram_tensor("s5_y", [P, QG * NC], F32, kind="Internal").ap()
        k.d_ys = nc.dram_tensor("s5_ys", [P, NB], F32, kind="Internal").ap()
        s_eps = k.sem("eps_set")
        with nc.Block() as block:
            @block.vector
            def _(dve):
                dve.memset(k.eps[:, :], EPS).then_inc(s_eps, 1)
        stage_setup(k)
        layer_a(k)
        k.recycle()
        ffn(k, 0)
        k.recycle()
        layer_c(k)
        k.recycle()
        ffn(k, 1)
        stage_finish(k)


def bucket_onehot():
    def bucket(n):
        n = np.maximum(n, 0)
        nf = np.maximum(n, 16).astype(np.float32)
        large = 16 + (np.log(nf / np.float32(16)) / np.float32(np.log(8.0)) * np.float32(16)).astype(np.int32)
        return np.where(n < 16, n, np.minimum(large, 31))

    def cols(dist, relative_to_far, mask=None):
        m = np.zeros((33, dist.size), np.float32)
        m[bucket(dist), np.arange(dist.size)] = 1.0
        if relative_to_far:
            m[31] -= 1.0
        if mask is not None:
            m[:32, mask] = 0.0
            m[32, mask] = NEG
        return m

    d = 255 - np.arange(384)
    j, p = np.divmod(np.arange(512), 128)
    j8, p8 = np.divmod(np.arange(64), 8)
    pos = p8 * 8 + j8
    return np.concatenate([
        cols(d, True, d < 0),
        cols(511 - 4 * p - j, False),
        cols(127 - np.arange(128), False),
        cols(128 - pos, True), cols(64 - pos, True), cols(np.zeros(1, np.int64), True)], axis=1)


def index_onehot():
    m = np.zeros((128, 576), np.float32)
    p = np.arange(128)
    for half in range(2):
        m[half * 16 + p // 8, half * 128 + p] = 8.0
        m[32, half * 128 + p] = p % 8
    m[p // 8, 256 + p] = 1.0
    m[16, 256 + p] = p % 8
    for half in range(2):
        n = half * 128 + p[:, None]
        s = np.arange(64)[None, :]
        m[:, 384 + half * 64:448 + half * 64] = (16 * n < 64 * s + 64) & (16 * n + 31 >= 64 * s) & (n < NCS)
    h = np.arange(64)
    m[:64, 512:] = h[:, None] // 4 == h[None, :] // 4
    return m


_INS = ["x_prompt", "x_sample", "cache_nsa_cmp", "cache_nsa_sel", "cache_nsa_win", "state_s5_re", "state_s5_im",
        "cache_swa", "state_ffn_conv", "page_table", "rel_bias", "norm_mix", "norm_ffn", "a_w_in", "a_w_out",
        "nsa_q_gain", "nsa_k_gain", "nsa_cmp_pos", "nsa_cmp_w1", "nsa_cmp_w2", "s5_a_re", "s5_a_im", "s5_log_dt",
        "s5_b_re", "s5_b_im", "s5_c_re", "s5_c_im", "s5_d", "s5_w_glu", "s5_b_glu", "c_w_in", "c_w_out",
        "c_q_gain", "c_k_gain", "c_sinks", "ffn_w_up", "ffn_w_gate", "ffn_conv_w", "ffn_conv_b", "ffn_w_down"]
_OUTS = [("y_prompt", (1, T, D)), ("y_sample", (NB, 1, D)),
         ("nsa_cmp_prompt", (1, 1, T, 2, G, HD)), ("nsa_cmp_sample", (1, NB, 1, 2, G, HD)),
         ("nsa_sel_prompt", (1, 1, T, 2, G, HD)), ("nsa_sel_sample", (1, NB, 1, 2, G, HD)),
         ("nsa_win_prompt", (1, 1, 512, 2, G, HD)), ("nsa_win_sample", (1, NB, 512, 2, G, HD)),
         ("s5_re_prompt", (1, 1, GRP, NS)), ("s5_im_prompt", (1, 1, GRP, NS)),
         ("s5_re_sample", (1, NB, GRP, NS)), ("s5_im_sample", (1, NB, GRP, NS)),
         ("swa_prompt", (1, 1, 128, 2, 2, HD)), ("swa_sample", (1, NB, 128, 2, 2, HD)),
         ("ffn_conv_prompt", (2, 1, 2, DFF)), ("ffn_conv_sample", (2, NB, 2, DFF))]


def kernel(**inputs):
    import concourse.bacc as _bacc
    from concourse.bass_utils import run_bass_kernel_spmd as _run

    nc = _bacc.Bacc("TRN2", target_bir_lowering=False, num_devices=1)
    arrays, ins = {}, {}
    constants = {"bucket_onehot": bucket_onehot(), "index_onehot": index_onehot()}
    for name in _INS + list(constants):
        a = constants[name] if name in constants else np.ascontiguousarray(inputs[name])
        arrays[f"in_{name}_dram"] = a
        ins[name] = nc.dram_tensor(f"in_{name}_dram", a.shape, mybir.dt.from_np(a.dtype), kind="ExternalInput").ap()
    outs = {name: nc.dram_tensor(f"out_{name}", shape, F32, kind="ExternalOutput").ap() for name, shape in _OUTS}
    build(nc, ins, outs)
    r = _run(nc, [arrays], core_ids=[0])
    return tuple(r.results[0][f"out_{name}"] for name, _ in _OUTS)
```

```python
from contextlib import ExitStack

import numpy as np

import concourse.bass as bass
from concourse import mybir

F32 = mybir.dt.float32
F32R = mybir.dt.float32r
U32 = mybir.dt.uint32
I32 = mybir.dt.int32
ALU = mybir.AluOpType
ACT = mybir.ActivationFunctionType
AX = mybir.AxisListType.X

P = 128
D = 1024
KD = D // P
T = 1024
TT = T // P
NB = 8
TA = T + NB
NCH = 3
CH = TA // NCH
HD = 64
AH, G = 8, 2
CHD = 16
DFF = 2816
KF = DFF // P
PAST = 4096
PAGE = 128
NPAGE = PAST // PAGE
EPS = 1e-6
NEG = -1e30
FLOOR = -1e29
GRP, CG, NS = 32, 16, 64
L = 8
NC = T // L
QG = 8
NCK = T // 16 - 1
NCS = PAST // 16 - 1

C_MIX, C_FFN, C_D, C_BGLU, C_CB, C_GAIN, C_POS, C_CW = 0, 16, 32, 36, 40, 84, 88, 120
N_COLA = 120
N_CW = 3 * KF
O_TOEP, O_WIN, O_SWA, O_SEL = 0, 384, 896, 1024
N_OH = 1024 + 129


class Chain:

    def __init__(self, eng, sem):
        self.eng, self.sem, self.n = eng, sem, 0

    def __call__(self, ins):
        self.n += 1
        ins.then_inc(self.sem, 1)
        self.eng.wait_ge(self.sem, self.n)


class Core:

    def __init__(self, nc, ctx, ins, outs):
        self.nc, self.ctx, self.i, self.o = nc, ctx, ins, outs
        self.n, self.live = 0, []

    def sem(self, name):
        self.n += 1
        self.live.append(self.nc.alloc_semaphore(name=f"{name}_{self.n}"))
        return self.live[-1]

    def recycle(self):
        self.nc.clear_and_free_semaphores(self.live)
        self.nc.all_engine_barrier()
        self.live = []

    def sb(self, st, name, shape, dt=F32):
        self.n += 1
        return st.enter_context(self.nc.sbuf_tensor(f"{name}_{self.n}", shape, dt))


def bc(ap, dims):
    return bass.AP(ap.tensor, ap.offset, [list(ap.ap[0])] + [list(d) for d in dims])


def stage_setup(k):
    nc = k.nc
    with ExitStack() as st:
        rows = k.sb(st, "rows", [P, 3, P])
        xt = k.sb(st, "xt", [P, TT, D])
        xs = k.sb(st, "xs", [NB, D])
        oh = k.sb(st, "oh", [33, N_OH])
        tabs = k.sb(st, "tabs", [33, NB, AH])
        tabc = k.sb(st, "tabc", [33, NB, CHD])
        toep = k.sb(st, "toep", [P, 2, 384])
        s_zero, s_ident, s_tab1, s_rows, s_x, s_tab = (k.sem(n) for n in (
            "consts_zeroed", "ident_made", "tab_ones", "rows_in", "x_in", "tab_in"))
        s_tr, s_trc, s_rep, s_bias, s_biasc = (k.sem(n) for n in (
            "transposed", "transposed_out", "tab_repeated", "bias_made", "bias_out"))
        s_te, s_tw, s_bc, s_tb = (k.sem(n) for n in (
            "toep_made", "toep_written", "bcast_in", "toep_psum"))
        s_head = k.sem("headones_zeroed")
        s_trc = [s_trc, k.sem("transposed_out_act")]
        s_tw = [s_tw, k.sem("toep_written_odd")]
        i = k.i
        row_loads = [
            (rows[0:16, 0, :], i["norm_mix"].rearrange("l (a b) -> (l a) b", b=P)),
            (rows[16:32, 0, :], i["norm_ffn"].rearrange("l (a b) -> (l a) b", b=P)),
            (rows[32:36, 0, :], i["s5_d"].rearrange("l (a b) -> (l a) b", b=P)),
            (rows[36:40, 0, :], i["s5_b_glu"].rearrange("l (a b) -> (l a) b", b=P)),
            (rows[40:84, 0, :], i["ffn_conv_b"].rearrange("l (a b) -> (l a) b", b=P)),
            (rows[88:120, 0, :], i["nsa_cmp_pos"].rearrange("l k (a s) d -> (l k a) (s d)", s=2)),
            (rows[0:66, 1, :], i["ffn_conv_w"][0].rearrange("w (a b) -> (w a) b", b=P)),
            (rows[0:66, 2, :], i["ffn_conv_w"][1].rearrange("w (a b) -> (w a) b", b=P)),
        ]
        for n, name in enumerate(("nsa_q_gain", "nsa_k_gain", "c_q_gain", "c_k_gain")):
            for half in range(2):
                row_loads.append((rows[84 + n:85 + n, 0, half * HD:half * HD + HD], i[name]))
        n_jobs = 2 * KD + 1 + 3

        with nc.Block() as block:
            def copy_job(eng, j):
                src = k.ps[:, j % 4, :]
                copy = eng.tensor_copy if eng is nc.vector else eng.copy
                if j < 2 * KD:
                    copy(k.hT[:, j // 2, (j % 2) * 512:(j % 2) * 512 + 512], src).then_inc(s_trc[j % 2], 1)
                elif j == 2 * KD:
                    copy(k.hT[:, :, T:TA], src[:, 0:KD * NB].rearrange("p (f b) -> p f b", b=NB)).then_inc(s_trc[j % 2], 1)
                elif j == 2 * KD + 1:
                    copy(k.cols[:, 0:N_COLA], src[:, 0:N_COLA]).then_inc(s_trc[j % 2], 1)
                else:
                    c0 = C_CW + (j - 2 * KD - 2) * N_CW
                    copy(k.cols[:, c0:c0 + N_CW], src[:, 0:N_CW]).then_inc(s_trc[j % 2], 1)

            @block.gpsimd
            def _(pool):
                pool.memset(k.ident[:, :], 0.0).then_inc(s_zero, 1)
                pool.memset(k.ones[:, :], 1.0).then_inc(s_zero, 1)
                pool.memset(k.tab[:, :], 1.0).then_inc(s_tab1, 1)
                pool.wait_ge(s_zero, 2)
                pool.wait_ge(s_tab1, 1)
                pool.affine_select(out=k.ident[:, :], in_=k.ident[:, :], compare_op=ALU.not_equal, fill=1.0,
                                   base=0, pattern=[[-1, P]], channel_multiplier=1).then_inc(s_ident, 1)

            @block.sync
            def _(sp):
                for t in range(TT):
                    sp.dma_start(xt[:, t, :], i["x_prompt"][0, t * P:(t + 1) * P, :]).then_inc(s_x, 16)
                sp.dma_start(xs[:, :], i["x_sample"].rearrange("b s d -> (b s) d")).then_inc(s_x, 16)
                for h in range(CHD):
                    sp.wait_ge(s_te, h + 1)
                    sp.dma_start(k.d_toep[h], toep[:, h % 2, :]).then_inc(s_tw[h % 2], 16)
                for parity in range(2):
                    sp.wait_ge(s_tw[parity], 16 * CHD // 2)

            @block.scalar
            def _(act):
                act.wait_ge(s_tab1, 1)
                act.dma_start(k.tab[0:32, :], i["rel_bias"]).then_inc(s_tab, 16)
                act.dma_start(oh[:, :], i["bucket_onehot"]).then_inc(s_tab, 16)
                for dst, src in row_loads:
                    act.dma_start(dst, src).then_inc(s_rows, 16)
                act.dma_start(k.sink[:, 0, :], i["c_sinks"].broadcast_to([P, CHD])).then_inc(s_bc, 16)
                act.dma_start(k.sink[:, 1, :], i["rel_bias"][31:32, :].broadcast_to([P, CHD])).then_inc(s_bc, 16)
                act.wait_ge(s_bc, 32)
                for j in range(1, n_jobs, 2):
                    act.wait_ge(s_tr, j + 1)
                    copy_job(act, j)

            @block.vector
            def _(dve):
                dve.memset(k.headones[:, :], 0.0).then_inc(s_head, 1)
                dve.wait_ge(s_head, 1)
                dve.memset(k.headones[0:64, 0:64], 1.0)
                dve.memset(k.headones[64:128, 64:128], 1.0)
                dve.wait_ge(s_tab, 32)
                for b in range(NB):
                    dve.tensor_copy(tabs[:, b, :], k.tab[:, 0:AH]).then_inc(s_rep, 1)
                    dve.tensor_copy(tabc[:, b, :], k.tab[:, :]).then_inc(s_rep, 1)
                for j in range(0, n_jobs, 2):
                    dve.wait_ge(s_tr, j + 1)
                    copy_job(dve, j)
                for h in range(CHD):
                    dve.wait_ge(s_tb, h + 1)
                    if h >= 2:
                        dve.wait_ge(s_tw[h % 2], 16 * (h // 2))
                    dve.tensor_copy(toep[:, h % 2, :], k.ps[:, 4 + h % 2, 0:384]).then_inc(s_te, 1)
                dve.wait_ge(s_bias, 1)
                dve.tensor_copy(k.b_win[:, :], k.ps[0:64, 6, :])
                dve.wait_ge(s_bias, 2)
                dve.tensor_copy(k.b_swa[:, :], k.ps[:, 7, 0:P])
                dve.tensor_copy(k.b_sel[:, :], k.ps[0:64, 7, P:P + 129]).then_inc(s_biasc, 1)

            @block.tensor
            def _(pe):
                pe.wait_ge(s_ident, 1)
                pe.wait_ge(s_x, 16 * (TT + 1))
                for j in range(n_jobs):
                    if j >= 4:
                        pe.wait_ge(s_trc[j % 2], (j - 4) // 2 + 1)
                    bank = k.ps[:, j % 4, :]
                    if j < 2 * KD:
                        f = j // 2
                        for t in range(4):
                            ins = pe.transpose(bank[:, t * P:(t + 1) * P],
                                               xt[:, (j % 2) * 4 + t, f * P:(f + 1) * P], k.ident[:, :])
                    elif j == 2 * KD:
                        for f in range(KD):
                            ins = pe.transpose(bank[:, f * NB:(f + 1) * NB], xs[:, f * P:(f + 1) * P],
                                               k.ident[0:NB, 0:NB])
                    else:
                        if j == 2 * KD + 1:
                            pe.wait_ge(s_rows, 16 * len(row_loads))
                        n, w = j - 2 * KD - 1, (N_COLA, N_CW, N_CW)[j - 2 * KD - 1]
                        ins = pe.transpose(bank[:, 0:w], rows[0:w, n, :], k.ident[0:w, 0:w])
                    ins.then_inc(s_tr, 1)
                pe.wait_ge(s_tab, 32)
                pe.wait_ge(s_rep, 2 * NB)
                for h in range(CHD):
                    if h >= 2:
                        pe.wait_ge(s_te, h - 1)
                    pe.matmul(k.ps[:, 4 + h % 2, 0:384], k.tab[:, h:h + 1].to_broadcast([33, P]),
                              oh[:, O_TOEP:O_TOEP + 384], start=True, stop=True).then_inc(s_tb, 1)
                pe.matmul(k.ps[0:64, 6, :], tabs[:, :, :], oh[:, O_WIN:O_WIN + 512],
                          start=True, stop=True).then_inc(s_bias, 1)
                pe.matmul(k.ps[:, 7, 0:P], tabc[:, :, :], oh[:, O_SWA:O_SWA + P], start=True, stop=True)
                pe.matmul(k.ps[0:64, 7, P:P + 129], tabs[:, :, :], oh[:, O_SEL:O_SEL + 129],
                          start=True, stop=True).then_inc(s_bias, 1)


def stage_norm(k, xs, gain_col):
    nc = k.nc
    with ExitStack() as st:
        sq = k.sb(st, "sq", [P, 4, CH])
        root = k.sb(st, "root", [P, 2, CH])
        xn = k.sb(st, "xn", [P, 4, CH])
        s_sq, s_used, s_root, s_rec, s_xn, s_hi, s_lo = (k.sem(n) for n in (
            "squared", "square_used", "rooted", "reciprocal_ready", "normed", "norm_high", "norm_low"))
        spans = [(c, f) for c in range(NCH) for f in range(KD)]
        with nc.Block() as block:
            @block.scalar
            def _(act):
                def high(j):
                    c, f = spans[j]
                    act.wait_ge(s_xn, j + 1)
                    act.copy(xs.hi[:, f, c * CH:(c + 1) * CH], xn[:, j % 4, :]).then_inc(s_hi, 1)

                for j, (c, f) in enumerate(spans):
                    if j >= 4:
                        act.wait_ge(s_used, j - 3)
                    act.activation(sq[:, j % 4, :], k.hT[:, f, c * CH:(c + 1) * CH], ACT.Square).then_inc(s_sq, 1)
                    if f == KD - 1:
                        act.wait_ge(s_used, (c + 1) * KD)
                        if c >= 2:
                            act.wait_ge(s_xn, (c - 1) * KD)
                        act.activation(root[:, c % 2, :], k.ps[:, c, 0:CH], ACT.Sqrt, bias=k.eps[:, :],
                                       scale=1.0 / D).then_inc(s_root, 1)
                    if c >= 1:
                        high(j - KD)
                for j in range((NCH - 1) * KD, NCH * KD):
                    high(j)

            @block.tensor
            def _(pe):
                for j, (c, f) in enumerate(spans):
                    pe.wait_ge(s_sq, j + 1)
                    pe.matmul(k.ps[:, c, 0:CH], k.ones[:, :], sq[:, j % 4, :], start=(f == 0),
                              stop=(f == KD - 1)).then_inc(s_used, 1)

            @block.vector
            def _(dve):
                for j, (c, f) in enumerate(spans):
                    if f == 0:
                        dve.wait_ge(s_root, c + 1)
                        dve.reciprocal(root[:, c % 2, :], root[:, c % 2, :]).then_inc(s_rec, 1)
                        dve.wait_ge(s_rec, c + 1)
                    if j >= 4:
                        dve.wait_ge(s_lo, j - 3)
                    dve.scalar_tensor_tensor(
                        out=xn[:, j % 4, :], in0=k.hT[:, f, c * CH:(c + 1) * CH],
                        scalar=k.cols[:, gain_col + f:gain_col + f + 1], in1=root[:, c % 2, :],
                        op0=ALU.mult, op1=ALU.mult).then_inc(s_xn, 1)

            @block.gpsimd
            def _(pool):
                for j, (c, f) in enumerate(spans):
                    cs = slice(c * CH, (c + 1) * CH)
                    pool.wait_ge(s_hi, j + 1)
                    pool.tensor_tensor(xs.lo[:, f, cs], xn[:, j % 4, :], xs.hi[:, f, cs].bitcast(F32),
                                       ALU.subtract).then_inc(s_lo, 1)


class Split:

    def __init__(self, k, st, name, shape):
        self.hi = k.sb(st, name + "_hi", shape, F32R)
        self.lo = k.sb(st, name + "_lo", shape, F32R)


def stage_split(k, xs, tiles):
    nc = k.nc
    s_hi = k.sem("split_high")
    with nc.Block() as block:
        @block.scalar
        def _(act):
            for m, t in enumerate(tiles):
                act.copy(xs.hi[:, m, :], t).then_inc(s_hi, 1)

        @block.vector
        def _(dve):
            for m, t in enumerate(tiles):
                dve.wait_ge(s_hi, m + 1)
                dve.tensor_tensor(xs.lo[:, m, :], t, xs.hi[:, m, :].bitcast(F32), ALU.subtract)


def split_product(pe, psum, w_hi, w_lo, x_hi, x_lo, kt):
    for a in range(kt):
        for n, (w, x) in enumerate(((w_hi, x_hi), (w_hi, x_lo), (w_lo, x_hi))):
            ins = pe.matmul(psum, w(a), x(a), start=(a == 0 and n == 0), stop=(a == kt - 1 and n == 2))
    return ins


class WeightRing:

    def __init__(self, k, st, kt=KD):
        self.raw = k.sb(st, "w_raw", [P, 2, kt, P])
        self.parts = Split(k, st, "w", [P, 2, kt, P])
        self.s_in = [k.sem("weights_in0"), k.sem("weights_in1")]
        self.s_hi, self.s_lo, self.s_used = k.sem("weights_high"), k.sem("weights_low"), k.sem("weights_used")

    def load(self, sp, j, slot, turn, src, kt, width=P):
        sp.wait_ge(self.s_lo, j + 1)
        sp.dma_start(self.raw[:, slot, 0:kt, 0:width], src).then_inc(self.s_in[slot], 16)

    def high(self, act, j, slot, turn, kt, width=P):
        act.wait_ge(self.s_in[slot], turn * 16 + 16)
        act.wait_ge(self.s_used, j + 1)
        act.copy(self.parts.hi[:, slot, 0:kt, 0:width], self.raw[:, slot, 0:kt, 0:width]).then_inc(self.s_hi, 1)

    def low(self, pool, j, slot, kt, width=P):
        pool.wait_ge(self.s_hi, j + 1)
        pool.tensor_tensor(self.parts.lo[:, slot, 0:kt, 0:width], self.raw[:, slot, 0:kt, 0:width],
                           self.parts.hi[:, slot, 0:kt, 0:width].bitcast(F32), ALU.subtract).then_inc(self.s_lo, 1)

    def product(self, pe, psum, slot, xs, cols, kt, width=P):
        hi, lo = self.parts.hi, self.parts.lo
        return split_product(pe, psum, lambda a: hi[:, slot, a, 0:width], lambda a: lo[:, slot, a, 0:width],
                             lambda a: xs.hi[:, a, cols], lambda a: xs.lo[:, a, cols], kt)


def chunk(c):
    return slice(c * CH, (c + 1) * CH)


def stage_linear(k, w, kt, tiles, xs, put):
    nc = k.nc
    with ExitStack() as st:
        ring = WeightRing(k, st, kt)
        s_prod, s_out = k.sem("product_ready"), k.sem("product_out")
        n = len(tiles)
        with nc.Block() as block:
            @block.sync
            def _(sp):
                sp.sem_inc(ring.s_lo, 2)
                for m, (c0, width) in enumerate(tiles):
                    ring.load(sp, m, m % 2, m // 2, w[:, c0:c0 + width].rearrange("(a p) n -> p a n", p=P), kt, width)

            @block.gpsimd
            def _(pool):
                for m, (c0, width) in enumerate(tiles):
                    ring.low(pool, m, m % 2, kt, width)

            @block.tensor
            def _(pe):
                pe.sem_inc(ring.s_used, 2)
                for m, (c0, width) in enumerate(tiles):
                    pe.wait_ge(ring.s_lo, m + 3)
                    for c in range(NCH):
                        j = m * NCH + c
                        if j >= 6:
                            pe.wait_ge(s_out, j - 5)
                        ring.product(pe, k.ps[0:width, j % 6, 0:CH], m % 2, xs, chunk(c), kt, width).then_inc(s_prod, 1)
                    pe.wait_ge(s_prod, (m + 1) * NCH)
                    pe.sem_inc(ring.s_used, 1)

            @block.scalar
            def _(act):
                ring.high(act, 0, 0, 0, kt, tiles[0][1])
                for m, (c0, width) in enumerate(tiles):
                    if m + 1 < n:
                        ring.high(act, m + 1, (m + 1) % 2, (m + 1) // 2, kt, tiles[m + 1][1])
                    for c in range(NCH):
                        j = m * NCH + c
                        act.wait_ge(s_prod, j + 1)
                        put(m, c, k.ps[0:width, j % 6, 0:CH]).then_inc(s_out, 1)


def stage_residual(k, w, xs):
    nc = k.nc
    with ExitStack() as st:
        ring = WeightRing(k, st)
        s_prod, s_out = k.sem("sum_ready"), k.sem("sum_added")
        with nc.Block() as block:
            @block.sync
            def _(sp):
                sp.sem_inc(ring.s_lo, 2)
                with sp.Fori(0, KD // 2) as it:
                    for s in range(2):
                        m = it * 2 + s
                        ring.load(sp, m, s, it, w[:, bass.ds(m * P, P)].rearrange("(a p) n -> p a n", p=P), KD)

            @block.scalar
            def _(act):
                with act.Fori(0, KD // 2) as it:
                    for s in range(2):
                        ring.high(act, it * 2 + s, s, it, KD)

            @block.gpsimd
            def _(pool):
                with pool.Fori(0, KD // 2) as it:
                    for s in range(2):
                        ring.low(pool, it * 2 + s, s, KD)

            @block.tensor
            def _(pe):
                pe.sem_inc(s_out, 2 * NCH)
                pe.sem_inc(ring.s_used, 2)
                with pe.Fori(0, KD // 2) as it:
                    for s in range(2):
                        m = it * 2 + s
                        pe.wait_ge(ring.s_lo, m + 3)
                        for c in range(NCH):
                            pe.wait_ge(s_out, m * NCH + c + 1)
                            ring.product(pe, k.ps[:, 3 * s + c, 0:CH], s, xs, chunk(c), KD).then_inc(s_prod, 1)
                        pe.wait_ge(s_prod, m * NCH + NCH)
                        pe.sem_inc(ring.s_used, 1)

            @block.vector
            def _(dve):
                with dve.Fori(0, KD // 2) as it:
                    for s in range(2):
                        m = it * 2 + s
                        for c in range(NCH):
                            dve.wait_ge(s_prod, m * NCH + c + 1)
                            h = k.hT[:, bass.ds(m, 1), chunk(c)]
                            dve.tensor_tensor(h, h, k.ps[:, 3 * s + c:3 * s + c + 1, 0:CH], ALU.add).then_inc(s_out, 1)


def stage_ffn(k, layer, xs, stT, hlast):
    nc = k.nc
    wu, wg, wd = k.i["ffn_w_up"][layer], k.i["ffn_w_gate"][layer], k.i["ffn_w_down"][layer]
    cb, cw = C_CB + layer * KF, C_CW + layer * N_CW
    parts = [(0, 8), (8, 7), (15, 7)]
    base, jobs, downs = [], 0, []
    for f0, nf in parts:
        base.append(jobs)
        downs.append(jobs + 2 * nf)
        jobs += 2 * nf + KD
    with ExitStack() as st:
        ring = WeightRing(k, st)
        hid = Split(k, st, "hid", [P, 8, TA])
        hb = k.sb(st, "hbuf", [P, 2 + T + NB])
        z = k.sb(st, "conv", [P, TA])
        s_prod, s_h, s_conv, s_gelu, s_prd, s_hi, s_lo, s_step, s_out, s_free = (k.sem(x) for x in (
            "ffn_product", "h_out", "conv_ready", "gelu_ready", "hid_product", "hid_high", "hid_low",
            "conv_step", "down_added", "banks_free"))

        def loop(eng, p, body_up, body_down):
            f0, nf = parts[p]
            if body_up:
                with eng.Fori(0, nf) as it:
                    body_up(it, f0, base[p])
            if body_down:
                with eng.Fori(0, KD // 2) as it:
                    for s in range(2):
                        body_down(it, s, downs[p], nf)

        with nc.Block() as block:
            def rows(w, n, r0=0, nr=D):
                return w[r0:r0 + nr, bass.ds(n * P, P)].rearrange("(a p) n -> p a n", p=P)

            @block.sync
            def _(sp):
                sp.sem_inc(ring.s_lo, 2)
                for p, (f0, nf) in enumerate(parts):
                    def up(it, f0, j0):
                        ring.load(sp, it * 2 + j0, 0, None, rows(wu, it + f0), KD)
                        ring.load(sp, it * 2 + (j0 + 1), 1, None, rows(wg, it + f0), KD)

                    def down(it, s, j0, nf):
                        ring.load(sp, it * 2 + (j0 + s), s, None, rows(wd, it * 2 + s, f0 * P, nf * P), nf)

                    loop(sp, p, up, down)

            @block.gpsimd
            def _(pool):
                for p, (f0, nf) in enumerate(parts):
                    def up(it, f0, j0):
                        ring.low(pool, it * 2 + j0, 0, KD)
                        ring.low(pool, it * 2 + (j0 + 1), 1, KD)

                    loop(pool, p, up, lambda it, s, j0, nf: ring.low(pool, it * 2 + (j0 + s), s, nf))

            @block.tensor
            def _(pe):
                pe.sem_inc(ring.s_used, 2)
                pe.sem_inc(s_free, 2 * NCH)

                def job(j, slot, x, kt):
                    pe.wait_ge(ring.s_lo, j + 3)
                    for c in range(NCH):
                        pe.wait_ge(s_free, j * NCH + (c + 1))
                        ring.product(pe, k.ps[:, 3 * slot + c, 0:CH], slot, x, chunk(c), kt).then_inc(s_prod, 1)
                    pe.wait_ge(s_prod, j * NCH + NCH)
                    pe.sem_inc(ring.s_used, 1)

                for p, (f0, nf) in enumerate(parts):
                    def up(it, f0, j0):
                        job(it * 2 + j0, 0, xs, KD)
                        job(it * 2 + (j0 + 1), 1, xs, KD)

                    def down(it, s, j0, nf):
                        job(it * 2 + (j0 + s), s, hid, nf)

                    loop(pe, p, up, None)
                    pe.wait_ge(s_lo, f0 + nf + 1)
                    loop(pe, p, None, down)

            @block.scalar
            def _(act):
                for p, (f0, nf) in enumerate(parts):
                    j0, turn0 = base[p], base[p] // 2

                    def up(it, next_kt):
                        ring.high(act, it * 2 + (j0 + 1), 1, it + turn0, KD)
                        for c in range(NCH):
                            act.wait_ge(s_prod, it * 2 * NCH + (j0 * NCH + c + 1))
                            if c == 0:
                                act.wait_ge(s_conv, it + (f0 + 1))
                            act.copy(hb[:, 2 + c * CH:2 + (c + 1) * CH], k.ps[:, c, 0:CH]).then_inc(s_h, 1)
                        act.wait_ge(s_conv, it + (f0 + 2))
                        act.activation(z[:, :], z[:, :], ACT.Gelu_apprx_tanh).then_inc(s_gelu, 1)
                        ring.high(act, it * 2 + (j0 + 2), 0, it + (turn0 + 1), next_kt)
                        act.wait_ge(s_prd, it * NCH + (f0 * NCH + NCH))
                        act.copy(hid.hi[:, bass.ds(it, 1), :], z[:, :].unsqueeze(1)).then_inc(s_hi, 1)

                    ring.high(act, j0, 0, turn0, KD)
                    with act.Fori(0, nf - 1) as it:
                        up(it, KD)
                    up(nf - 1, nf)
                    j0 = downs[p]
                    ring.high(act, j0 + 1, 1, j0 // 2, nf)
                    with act.Fori(1, KD // 2) as it:
                        for s in range(2):
                            ring.high(act, it * 2 + (j0 + s), s, it + j0 // 2, nf)

            @block.vector
            def _(dve):
                dve.memset(hb[:, 0:2], 0.0).then_inc(s_conv, 1)
                dve.sem_inc(s_lo, 1)
                for p, (f0, nf) in enumerate(parts):
                    def up(it, f0, j0):
                        f = it + f0

                        def tap(j):
                            return k.cols[:, bass.ds(it + (cw + f0 + j * KF), 1)]

                        def prev(j):
                            return stT[:, bass.ds(f, 1), j:16:2].rearrange("p a b -> p (a b)")

                        hn, zp, zn = hb[:, 2 + T:2 + T + NB], z[:, 0:T], z[:, T:TA]
                        bias = k.cols[:, bass.ds(it + (cb + f0), 1)]
                        dve.wait_ge(s_h, it * NCH + (f0 * NCH + NCH))
                        dve.tensor_copy(hlast[:, bass.ds(f, 1), :], hb[:, T:T + 10].unsqueeze(1)).then_inc(s_free, NCH)
                        dve.wait_ge(s_lo, f + 1)
                        dve.tensor_scalar(zp, hb[:, 0:T], tap(0), bias, ALU.mult, ALU.add)
                        dve.tensor_scalar(zn, prev(0), tap(0), bias, ALU.mult, ALU.add).then_inc(s_step, 1)
                        dve.wait_ge(s_step, it * 2 + (2 * f0 + 1))
                        dve.scalar_tensor_tensor(out=zp, in0=hb[:, 1:T + 1], scalar=tap(1), in1=zp, op0=ALU.mult, op1=ALU.add)
                        dve.scalar_tensor_tensor(out=zn, in0=prev(1), scalar=tap(1), in1=zn, op0=ALU.mult,
                                                 op1=ALU.add).then_inc(s_step, 1)
                        dve.wait_ge(s_step, it * 2 + (2 * f0 + 2))
                        dve.scalar_tensor_tensor(out=zp, in0=hb[:, 2:T + 2], scalar=tap(2), in1=zp, op0=ALU.mult, op1=ALU.add)
                        dve.scalar_tensor_tensor(out=zn, in0=hn, scalar=tap(2), in1=zn, op0=ALU.mult,
                                                 op1=ALU.add).then_inc(s_conv, 1)
                        dve.wait_ge(s_gelu, f + 1)
                        for c in range(NCH):
                            dve.wait_ge(s_prod, it * 2 * NCH + (j0 * NCH + NCH + c + 1))
                            dve.tensor_tensor(z[:, chunk(c)], z[:, chunk(c)], k.ps[:, 3 + c, 0:CH], ALU.mult).then_inc(s_prd, 1)
                        dve.wait_ge(s_hi, f + 1)
                        dve.sem_inc(s_free, NCH)
                        dve.tensor_tensor(hid.lo[:, bass.ds(it, 1), :], z[:, :].unsqueeze(1),
                                          hid.hi[:, bass.ds(it, 1), :].bitcast(F32), ALU.subtract).then_inc(s_lo, 1)

                    def down(it, s, j0, nf):
                        j = it * 2 + (j0 + s)
                        for c in range(NCH):
                            dve.wait_ge(s_prod, j * NCH + (c + 1))
                            h = k.hT[:, bass.ds(it * 2 + s, 1), chunk(c)]
                            dve.tensor_tensor(h, h, k.ps[:, 3 * s + c:3 * s + c + 1, 0:CH], ALU.add).then_inc(s_free, 1)

                    loop(dve, p, up, down)


def ffn(k, layer):
    with ExitStack() as st:
        stT = k.sb(st, "stateT", [P, KF, 2 * NB])
        hlast = k.sb(st, "hlast", [P, KF, 10])
        stage_conv_state(k, layer, stT)
        with ExitStack() as st2:
            xs = Split(k, st2, "xf", [P, KD, TA])
            stage_norm(k, xs, C_FFN + layer * KD)
            stage_ffn(k, layer, xs, stT, hlast)
        stage_conv_rows(k, layer, hlast)


def stage_head_norm(k, tiles):
    nc = k.nc
    jobs = []
    for t, g, f in tiles:
        cols = t.shape[-1]
        step = min(cols, CH if cols == TA else 512)
        jobs += [(t[:, c:c + step], g, f, step) for c in range(0, cols, step)]
    n = len(jobs)
    with ExitStack() as st:
        sq = k.sb(st, "hsq", [P, 4, 512])
        root = k.sb(st, "hroot", [P, 4, 512])
        gain = k.sb(st, "hgain", [P, 2])
        s_sq, s_sum, s_root, s_rec, s_gain, s_done = (k.sem(x) for x in (
            "head_squared", "head_summed", "head_rooted", "head_reciprocal", "gain_scaled", "head_normed"))
        with nc.Block() as block:
            @block.scalar
            def _(act):
                for j in range(n + 2):
                    if j < n:
                        t, _, _, w = jobs[j]
                        if j >= 4:
                            act.wait_ge(s_sum, j - 3)
                        act.activation(sq[:, j % 4, 0:w], t, ACT.Square).then_inc(s_sq, 1)
                    if j >= 2:
                        act.wait_ge(s_sum, j - 1)
                        if j >= 6:
                            act.wait_ge(s_done, j - 5)
                        w = jobs[j - 2][3]
                        act.activation(root[:, (j - 2) % 4, 0:w], k.ps[:, (j - 2) % 4, 0:w], ACT.Sqrt,
                                       bias=k.eps[:, :], scale=1.0 / HD).then_inc(s_root, 1)

            @block.tensor
            def _(pe):
                for j in range(n):
                    pe.wait_ge(s_sq, j + 1)
                    if j >= 4:
                        pe.wait_ge(s_root, j - 3)
                    w = jobs[j][3]
                    pe.matmul(k.ps[:, j % 4, 0:w], k.headones[:, :], sq[:, j % 4, 0:w], start=True,
                              stop=True).then_inc(s_sum, 1)

            @block.vector
            def _(dve):
                g0 = tiles[0][1]
                dve.tensor_scalar(gain[:, :], k.cols[:, g0:g0 + 2], HD ** -0.5, None, ALU.mult).then_inc(s_gain, 1)
                dve.wait_ge(s_gain, 1)
                for j, (t, g, scaled, w) in enumerate(jobs):
                    dve.wait_ge(s_root, j + 1)
                    dve.reciprocal(root[:, j % 4, 0:w], root[:, j % 4, 0:w]).then_inc(s_rec, 1)
                    dve.wait_ge(s_rec, j + 1)
                    dve.scalar_tensor_tensor(
                        out=t, in0=t,
                        scalar=gain[:, 0:1] if scaled else k.cols[:, g:g + 1], in1=root[:, j % 4, 0:w],
                        op0=ALU.mult, op1=ALU.mult).then_inc(s_done, 1)


def stage_rows(k, kv, tok, stok, stores):
    nc = k.nc
    n_kv = len(kv)
    jobs = [(n, h) for n in range(n_kv) for h in range(2)] + [(n, 2) for n in range(n_kv)]
    with ExitStack() as st:
        s_tr, s_out, s_store = (k.sem(x) for x in ("rows_transposed", "rows_out", "rows_stored"))
        with nc.Block() as block:
            def take(eng, par):
                for j, (n, h) in enumerate(jobs):
                    if j % 2 != par:
                        continue
                    eng.wait_ge(s_tr, j + 1)
                    src = k.ps[:, j % 8, :]
                    copy = eng.copy if par else eng.tensor_copy
                    if h < 2:
                        copy(tok[:, 4 * h:4 * h + 4, n, :], src.rearrange("p (t f) -> p t f", t=4)).then_inc(s_out[par], 1)
                    else:
                        copy(stok[:, n, :], src[0:NB, 0:P]).then_inc(s_out[par], 1)

            s_out = [s_out, k.sem("rows_out_act")]

            @block.vector
            def _(dve):
                take(dve, 0)

            @block.scalar
            def _(act):
                take(act, 1)

            @block.tensor
            def _(pe):
                for j, (n, h) in enumerate(jobs):
                    if j >= 8:
                        pe.wait_ge(s_out[j % 2], (j - 8) // 2 + 1)
                    if h < 2:
                        for t in range(4):
                            c0 = (4 * h + t) * P
                            ins = pe.transpose(k.ps[:, j % 8, t * P:(t + 1) * P], kv[n][:, c0:c0 + P], k.ident[:, :])
                    else:
                        ins = pe.transpose(k.ps[0:NB, j % 8, 0:P], kv[n][:, T:TA], k.ident[:, :])
                    ins.then_inc(s_tr, 1)

            @block.sync
            def _(sp):
                sp.wait_ge(s_out[0], (len(jobs) + 1) // 2)
                sp.wait_ge(s_out[1], len(jobs) // 2)
                for dst, src in stores:
                    sp.dma_start(dst, src).then_inc(s_store, 16)
                sp.wait_ge(s_store, 16 * len(stores))


def stage_finish(k):
    nc = k.nc
    jobs = [(t, h) for t in range(TT + 1) for h in range(2)]
    with ExitStack() as st:
        out = k.sb(st, "yrows", [P, 3, D])
        s_tr, s_c0, s_c1, s_y = (k.sem(x) for x in ("y_transposed", "y_out_dve", "y_out_act", "y_stored0"))
        s_y = [s_y, k.sem("y_stored1"), k.sem("y_stored2")]
        with nc.Block() as block:
            def take(eng, par, sem):
                for t in range(TT + 1):
                    j = 2 * t + par
                    eng.wait_ge(s_tr, j + 1)
                    if t >= 3:
                        eng.wait_ge(s_y[t % 3], 16 * (t // 3))
                    n = P if t < TT else NB
                    copy = eng.copy if par else eng.tensor_copy
                    copy(out[0:n, t % 3, par * 512:par * 512 + 512], k.ps[0:n, j % 8, :]).then_inc(sem, 1)

            @block.vector
            def _(dve):
                take(dve, 0, s_c0)

            @block.scalar
            def _(act):
                take(act, 1, s_c1)

            @block.tensor
            def _(pe):
                for j, (t, h) in enumerate(jobs):
                    if j >= 8:
                        pe.wait_ge((s_c0, s_c1)[h], (j - 8) // 2 + 1)
                    n = P if t < TT else NB
                    for f in range(4):
                        ins = pe.transpose(k.ps[0:n, j % 8, f * P:(f + 1) * P],
                                           k.hT[:, 4 * h + f, t * P:t * P + n], k.ident[:, :])
                    ins.then_inc(s_tr, 1)

            @block.sync
            def _(sp):
                for t in range(TT + 1):
                    sp.wait_ge(s_c0, t + 1)
                    sp.wait_ge(s_c1, t + 1)
                    if t < TT:
                        sp.dma_start(k.o["y_prompt"][0, t * P:(t + 1) * P, :], out[:, t % 3, :]).then_inc(s_y[t % 3], 16)
                    else:
                        sp.dma_start(k.o["y_sample"].rearrange("b s d -> (b s) d"), out[0:NB, t % 3, :]).then_inc(s_y[t % 3], 16)
                for n in range(3):
                    sp.wait_ge(s_y[n], 16 * 3)


def stage_attend(k, qT, n_heads, branches, oT, gates):
    nc = k.nc
    per_group = n_heads // G
    tasks = [(i, h, b) for i in range(TT) for h in range(n_heads) for b in range(len(branches))]
    n = len(tasks)
    swa = branches[0]["kind"] == "swa"

    per_tile = n_heads * len(branches)
    per_unit = 8 * len(branches)

    def key_tiles(t):
        i, _, b = tasks[t]
        br = branches[b]
        return [0] if br["kind"] == "cmp" else list(range(br["first"](i), i + 1))

    def width(t):
        return NCK if branches[tasks[t][2]]["kind"] == "cmp" else P * len(key_tiles(t))

    steps, groups = [], []
    for t in range(n + 5):
        mine = []
        if 0 <= t - 3 < n:
            m = len(key_tiles(t - 3))
            mine = [(t - 3, g0, min(4, m - g0)) for g0 in range(0, m, 4)]
        steps.append(list(range(len(groups), len(groups) + len(mine))))
        groups += mine

    with ExitStack() as st:
        btab = k.sb(st, "btab", [P, n_heads, 2 * P])
        pbuf = k.sb(st, "probs", [P, 4, 2 * 512])
        pt = k.sb(st, "probsT", [P, 2, TT, P])
        negm = k.sb(st, "negmax", [P, 4])
        sums = k.sb(st, "sums", [P, 4])
        fac = k.sb(st, "factors", [P, 4, 2])
        esink = k.sb(st, "esink", [P, 4])
        nsink = k.sb(st, "nsink", [P, CHD])
        psink = k.sb(st, "psink", [P, CHD])
        farmask = k.sb(st, "farmask", [P, P])
        cmask = k.sb(st, "cmask", [P, TT, 64])
        s_btab, s_mask0, s_mask, s_sc, s_max, s_exp, s_tr, s_pv, s_o, s_dve, s_sink, s_esink, s_norm = (k.sem(x) for x in (
            "btab_in", "mask_zeroed", "masks_made", "scores_ready", "max_ready", "probs_ready", "probsT_psum",
            "values_done", "heads_out", "dve_step", "sink_ready", "esink_ready", "probs_scaled"))
        s_pt, s_qh, s_q = k.sem("probsT_ready"), k.sem("q_high"), k.sem("q_split")
        qs = k.sb(st, "q_split", [P, 2, n_heads, P], F32R)
        qh = k.sb(st, "q_high_odd", [P, n_heads // 2, P], F32R)

        def q_tile(i, odd):
            rows = slice(odd * HD, (odd + 1) * HD)
            return qT[rows, :, i * P:(i + 1) * P], lambda half: qs[half * HD:(half + 1) * HD, i % 2, odd::2, :]


        def scores(t, w=None):
            w = w or width(t)
            return k.ps[:, 2 * (t % 2):2 * (t % 2) + 2, :].rearrange("p a b -> p (a b)")[:, 0:w]

        with nc.Block() as block:
            @block.sync
            def _(sp):
                for h in range(n_heads):
                    src = bass.AP(k.d_toep.tensor, h * P * 384 + P - 1, [[383, P], [1, 2 * P]])
                    sp.dma_start(btab[:, h, :], src).then_inc(s_btab, 16)
                sp.wait_ge(s_btab, 16 * n_heads)

            @block.gpsimd
            def _(pool):
                pool.memset(farmask[:, :], 0.0).then_inc(s_mask0, 1)
                pool.memset(cmask[:, :, :], 0.0).then_inc(s_mask0, 1)
                pool.wait_ge(s_mask0, 2)
                pool.affine_select(out=farmask[:, :], in_=farmask[:, :], compare_op=ALU.is_gt, fill=NEG,
                                   base=0, pattern=[[1, P]], channel_multiplier=-1).then_inc(s_mask, 1)
                pool.affine_select(out=cmask[:, :, :], in_=cmask[:, :, :], compare_op=ALU.is_ge, fill=NEG,
                                   base=-31, pattern=[[P, TT], [-16, 64]], channel_multiplier=1).then_inc(s_mask, 1)
                pool.wait_ge(s_mask, 2)
                for i in range(TT):
                    pool.wait_ge(s_qh, 3 * i + 3)
                    for odd in range(2):
                        if i or odd:
                            pool.wait_ge(s_q, 2 * i + odd)
                        src, dst = q_tile(i, odd)
                        high = (qh[HD:P, :, :] if odd else dst(0)).bitcast(F32)
                        pool.tensor_tensor(dst(1), src, high, ALU.subtract).then_inc(s_q, 1)

            @block.tensor
            def _(pe):
                for t in range(n + 5):
                    if t < n:
                        i, h, b = tasks[t]
                        br = branches[b]
                        g = h // per_group
                        if t >= 2:
                            pe.wait_ge(s_exp, t - 1)
                        if t % per_tile == 0:
                            pe.wait_ge(s_q, 2 * i + 2)
                        w, c0 = width(t), key_tiles(t)[0] * P
                        w += w % 2
                        sc = scores(t, w)
                        for c in range(0, w, 512):
                            m = min(512, w - c)
                            for part in (br["k"].hi, br["k"].lo):
                                ins = pe.matmul(sc[:, c:c + m], qs[:, i % 2, h, :], part[:, g, c0 + c:c0 + c + m],
                                                start=(part is br["k"].hi), stop=(part is br["k"].lo))
                        ins.then_inc(s_sc, 1)
                    for gi in steps[t]:
                        task, a, m = groups[gi]
                        if gi >= 2:
                            pe.wait_ge(s_pt, gi - 1)
                        bank = k.ps[:, 4 + gi % 2, :]
                        pe.wait_ge(s_norm, task + 1)
                        kw = width(task)
                        for x in range(m):
                            lo, hi = (a + x) * P, min((a + x + 1) * P, kw)
                            ins = pe.transpose(bank[0:hi - lo, x * P:(x + 1) * P],
                                               pbuf[:, task % 4, lo:hi], k.ident[:, :])
                        ins.then_inc(s_tr, 1)
                    if 0 <= t - 4 < n:
                        u = t - 4
                        i, h, b = tasks[u]
                        g = h // per_group
                        pe.wait_ge(s_pt, steps[t - 1][-1] + 1)
                        unit = u // per_unit
                        if u % per_unit == 0 and unit >= 2:
                            pe.wait_ge(s_o, unit - 1)
                        kts = key_tiles(u)
                        out = k.ps[h % 2 * HD:(h % 2 + 1) * HD, 6 + unit % 2, h // 2 % 4 * P:(h // 2 % 4 + 1) * P]
                        for x, kti in enumerate(kts):
                            rows = NCK if width(u) == NCK else P
                            ins = pe.matmul(out, branches[b]["v"](kti, g), pt[0:rows, u % 2, x, :],
                                            start=(b == 0 and x == 0), stop=(b == len(branches) - 1 and x == len(kts) - 1))
                        ins.then_inc(s_pv, 1)

            @block.vector
            def _(dve):
                link = Chain(dve, s_dve)
                dve.wait_ge(s_mask, 2)
                dve.wait_ge(s_btab, 16 * n_heads)
                if swa:
                    link(dve.tensor_tensor(psink[:, :], k.sink[:, 0, :], k.sink[:, 1, :], ALU.subtract))
                    dve.tensor_scalar(nsink[:, :], psink[:, :], -1.0, None, ALU.mult).then_inc(s_sink, 1)
                    for h in range(n_heads):
                        ins = dve.tensor_tensor(btab[:, h, 0:P], btab[:, h, 0:P], farmask[:, :], ALU.add)
                    link(ins)
                    dve.wait_ge(s_sink, 1)
                done = link.n

                def mark(ins):
                    nonlocal done
                    done += 1
                    ins.then_inc(s_dve, 1)
                    return done

                for t in range(n + 2):
                    u = t - 2
                    if t < n:
                        i, h, b = tasks[t]
                        kind = branches[b]["kind"]
                        sc, w = scores(t), width(t)
                        dve.wait_ge(s_sc, t + 1)
                        if kind == "cmp":
                            biased = mark(dve.tensor_tensor(sc, sc, cmask[:, i, 0:NCK], ALU.add))
                        else:
                            near = min(w, 2 * P)
                            biased = mark(dve.tensor_tensor(sc[:, w - near:w], sc[:, w - near:w],
                                                            btab[:, h, 2 * P - near:2 * P], ALU.add))
                            if kind == "win" and i >= 4:
                                biased = mark(dve.tensor_tensor(sc[:, 0:P], sc[:, 0:P], farmask[:, :], ALU.add))
                    if u >= 0:
                        ui, _, ub = tasks[u]
                        f = fac[:, u % 4, :]
                        total = sums[:, u % 4:u % 4 + 1]
                        probs = pbuf[:, u % 4, 0:width(u)]
                        dve.wait_ge(s_exp, u + 1)
                        if swa:
                            dve.wait_ge(s_esink, u + 1)
                            summed = mark(dve.tensor_tensor(f[:, 0:1], total, esink[:, u % 4:u % 4 + 1], ALU.add))
                            total = f[:, 0:1]
                        elif branches[ub]["kind"] == "cmp":
                            summed = mark(dve.tensor_scalar(f[:, 0:1], total, 1e-30, None, ALU.max))
                            total = f[:, 0:1]
                        else:
                            summed = 0
                    if t < n:
                        m = negm[:, t % 4:t % 4 + 1]
                        dve.wait_ge(s_dve, biased)
                        if t >= 4:
                            dve.wait_ge(s_exp, t - 3)
                        if swa:
                            if t >= 4:
                                dve.wait_ge(s_esink, t - 3)
                        ins = dve.tensor_reduce(m, sc, AX, ALU.max, negate=True)
                        if kind == "cmp" or swa:
                            reduced = mark(ins)
                        else:
                            ins.then_inc(s_max, 1)
                    if u >= 0:
                        if summed:
                            dve.wait_ge(s_dve, summed)
                        inverse = mark(dve.reciprocal(f[:, 1:2], total))
                    if t < n and (kind == "cmp" or swa):
                        dve.wait_ge(s_dve, reduced)
                        if swa:
                            dve.tensor_tensor(m, m, nsink[:, h:h + 1], ALU.min).then_inc(s_max, 1)
                        else:
                            dve.tensor_scalar(m, m, -FLOOR, None, ALU.min).then_inc(s_max, 1)
                    if u >= 0:
                        dve.wait_ge(s_dve, inverse)
                        if gates is None:
                            ins = dve.tensor_scalar(probs, probs, f[:, 1:2], None, ALU.mult)
                        else:
                            ins = dve.tensor_scalar(probs, probs, f[:, 1:2], gates[:, ui, 3 * tasks[u][1] + ub:3 * tasks[u][1] + ub + 1],
                                                    ALU.mult, ALU.mult)
                        ins.then_inc(s_norm, 1)

            @block.scalar
            def _(act):
                def split_queries(i):
                    if i >= 1:
                        act.wait_ge(s_q, 2 * i)
                    if i >= 2:
                        act.wait_ge(s_sc, (i - 1) * per_tile)
                    (even, even_dst), (odd, odd_dst) = q_tile(i, 0), q_tile(i, 1)
                    act.copy(even_dst(0), even).then_inc(s_qh, 1)
                    act.copy(odd_dst(0), odd).then_inc(s_qh, 1)
                    act.copy(qh[HD:P, :, :], odd).then_inc(s_qh, 1)

                split_queries(0)
                for t in range(n + 5):
                    if t < n and t % per_tile == 4 and tasks[t][0] + 1 < TT:
                        split_queries(tasks[t][0] + 1)
                    for gi in steps[t]:
                        u, a, m = groups[gi]
                        act.wait_ge(s_tr, gi + 1)
                        bank = k.ps[:, 4 + gi % 2, :]
                        if width(u) == NCK:
                            dst, src = pt[0:NCK, u % 2, 0, :], bank[0:NCK, 0:P]
                        else:
                            dst, src = pt[:, u % 2, a:a + m, :].rearrange("p a b -> p (a b)"), bank[:, 0:m * P]
                        if u >= 2:
                            act.wait_ge(s_pv, u - 1)
                        act.copy(dst, src).then_inc(s_pt, 1)
                    if t < n:
                        act.wait_ge(s_max, t + 1)
                        if t >= 4:
                            act.wait_ge(s_tr, steps[t - 1][-1] + 1)
                        if t >= 4:
                            act.wait_ge(s_norm, t - 3)
                        c = t % 4
                        act.activation(pbuf[:, t % 4, 0:width(t)], scores(t), ACT.Exp, bias=negm[:, c:c + 1],
                                       accum_out=sums[:, c:c + 1]).then_inc(s_exp, 1)
                        if swa:
                            h = tasks[t][1]
                            if t == 0:
                                act.wait_ge(s_sink, 1)
                            act.activation(esink[:, c:c + 1], psink[:, h:h + 1], ACT.Exp,
                                           bias=negm[:, c:c + 1]).then_inc(s_esink, 1)
                    if t >= 5 and (t - 4) % per_unit == 0:
                        unit, (i, h, _) = (t - 5) // per_unit, tasks[t - 5]
                        act.wait_ge(s_pv, t - 4)
                        act.copy(oT[:, h // 8 * 4:h // 8 * 4 + 4, i * P:(i + 1) * P],
                                 k.ps[:, 6 + unit % 2, :].rearrange("p (f q) -> p f q", f=4)).then_inc(s_o, 1)


class KeySplit:

    def __init__(self, k, st, name, width):
        self.hi = k.sb(st, name + "_hi", [P, G, width], F32R)
        self.lo = k.sb(st, name + "_lo", [P, G, width], F32R)


def stage_split_keys(k, pairs):
    nc = k.nc
    s_hi = k.sem("keys_high")
    with nc.Block() as block:
        @block.scalar
        def _(act):
            for dst, src in pairs:
                w = src.shape[-1]
                for g in range(G):
                    for half in range(2):
                        act.copy(dst.hi[half * HD:(half + 1) * HD, g, 0:w], src[g * HD:(g + 1) * HD, :]).then_inc(s_hi, 1)

        @block.vector
        def _(dve):
            n = 0
            for dst, src in pairs:
                w, even = src.shape[-1], dst.hi.shape[-1]
                if w < even:
                    dve.memset(dst.hi[:, :, w:even].bitcast(F32), 0.0)
                    dve.memset(dst.lo[:, :, w:even].bitcast(F32), 0.0)
                for g in range(G):
                    rows = slice(g * HD, (g + 1) * HD)
                    n += 2
                    dve.wait_ge(s_hi, n)
                    for half in range(2):
                        dve.tensor_tensor(dst.lo[half * HD:(half + 1) * HD, g, 0:w], src[rows, :],
                                          dst.hi[rows, g, 0:w].bitcast(F32), ALU.subtract)


def stage_conv_state(k, layer, stT):
    nc = k.nc
    state, out = k.i["state_ffn_conv"][layer], k.o["ffn_conv_sample"][layer]
    with ExitStack() as st:
        rows = k.sb(st, "state_rows", [2 * NB, DFF])
        s_in, s_pass, s_tr = k.sem("state_in"), k.sem("state_passed"), k.sem("state_transposed")
        with nc.Block() as block:
            @block.sync
            def _(sp):
                sp.dma_start(rows[:, :], state.rearrange("b j f -> (b j) f")).then_inc(s_in, 16)
                sp.dma_start(out[:, 0, :], state[:, 1, :]).then_inc(s_pass, 16)
                sp.wait_ge(s_pass, 16)

            @block.tensor
            def _(pe):
                pe.wait_ge(s_in, 16)
                for f in range(KF):
                    ins = pe.transpose(k.ps[:, 0, f * 16:(f + 1) * 16], rows[:, f * P:(f + 1) * P], k.ident[0:16, 0:16])
                ins.then_inc(s_tr, 1)

            @block.vector
            def _(dve):
                dve.wait_ge(s_tr, 1)
                dve.tensor_copy(stT[:, :, :], k.ps[:, 0, 0:KF * 16].rearrange("p (f c) -> p f c", c=16))


def stage_conv_rows(k, layer, hlast):
    nc = k.nc
    with ExitStack() as st:
        rows = k.sb(st, "last_rows", [10, KF, P])
        s_tr, s_out, s_st = k.sem("last_transposed"), k.sem("last_out"), k.sem("last_stored")
        with nc.Block() as block:
            @block.tensor
            def _(pe):
                for f in range(KF):
                    ins = pe.transpose(k.ps[0:10, f // 4, (f % 4) * P:(f % 4 + 1) * P], hlast[:, f, :], k.ident[:, :])
                    if f % 4 == 3 or f == KF - 1:
                        ins.then_inc(s_tr, 1)

            @block.vector
            def _(dve):
                for b in range(-(-KF // 4)):
                    m = min(4, KF - 4 * b)
                    dve.wait_ge(s_tr, b + 1)
                    dve.tensor_copy(rows[:, 4 * b:4 * b + m, :],
                                    k.ps[0:10, b, 0:m * P].rearrange("r (f c) -> r f c", c=P)).then_inc(s_out, 1)

            @block.sync
            def _(sp):
                sp.wait_ge(s_out, -(-KF // 4))
                sp.dma_start(k.o["ffn_conv_prompt"][layer, 0], rows[0:2, :, :].rearrange("r f c -> r (f c)")).then_inc(s_st, 16)
                sp.dma_start(k.o["ffn_conv_sample"][layer, :, 1, :], rows[2:10, :, :].rearrange("r f c -> r (f c)")).then_inc(s_st, 16)
                sp.wait_ge(s_st, 32)


def layer_c(k):
    i = k.i
    with ExitStack() as outer:
        oT = k.sb(outer, "oT", [P, KD, TA])
        layer_c_mix(k, oT)
        os = Split(k, outer, "co", [P, KD, TA])
        stage_split(k, os, [oT[:, m, :] for m in range(KD)])
        stage_residual(k, i["c_w_out"][0], os)


def layer_c_mix(k, oT):
    nc = k.nc
    i, o = k.i, k.o
    with ExitStack() as st:
        qT = k.sb(st, "cqT", [P, KD, TA])
        kvT = k.sb(st, "ckvT", [P, 2, TA])
        with ExitStack() as st2:
            xs = Split(k, st2, "xc", [P, KD, TA])
            stage_norm(k, xs, C_MIX + KD)

            def put(m, c, ps):
                dst = qT[:, m, :] if m < KD else kvT[:, m - KD, :]
                return nc.scalar.copy(dst[:, chunk(c)], ps)

            stage_linear(k, i["c_w_in"][0], KD, [(m * P, P) for m in range(10)], xs, put)
        keys = KeySplit(k, st, "ck", T)
        tok = k.sb(st, "ckvrows", [P, TT, 2, P])
        stok = k.sb(st, "ckvrows_s", [NB, 2, P])
        stage_head_norm(k, [(qT[:, n, :], C_GAIN + 2, True) for n in range(KD)] + [(kvT[:, 0, :], C_GAIN + 3, False)])
        swa = o["swa_sample"][0].rearrange("b t k g d -> b t (k g d)")
        stage_rows(k, [kvT[:, n, :] for n in range(2)], tok, stok, [
            (kv_rows(o["swa_prompt"]), tok[:, TT - 1, :, :]),
            (swa[:, 127, :], stok[:, :, :]),
            (swa[:, 0:127, :], i["cache_swa"][0, :, 1:128].rearrange("b t k g d -> b t (k g d)"))])
        stage_split_keys(k, [(keys, kvT[:, 0, 0:T])])
        branch = dict(kind="swa", k=keys, first=lambda q: max(0, q - 1),
                      v=lambda t, g: tok[:, t, 1, g * HD:(g + 1) * HD])
        stage_attend(k, qT, CHD, [branch], oT, None)
        stage_swa_sample(k, qT, stok, oT)


def stage_swa_sample(k, qT, stok, oT):
    nc = k.nc
    i = k.i
    cache = i["cache_swa"][0].rearrange("b t k g d -> b t (k g d)")
    new = k.o["swa_sample"][0].rearrange("b t k g d -> b t (k g d)")
    with ExitStack() as st:
        kv = k.sb(st, "swa_rows", [P, NB, 4 * HD])
        qb = k.sb(st, "swa_q", [P, NB, NB * CHD])
        kT = k.sb(st, "swa_kT", [P, NB, P])
        pr = k.sb(st, "swa_p", [P, P])
        pT = k.sb(st, "swa_pT", [P, P])
        sc = k.sb(st, "swa_sc", [P, P])
        sm = k.sb(st, "swa_small", [P, 8])
        s_in, s_q0, s_q, s_tr, s_kT, s_sc, s_dve, s_act, s_pTp, s_pT, s_o, s_sink = (k.sem(x) for x in (
            "swa_in", "swa_q_zeroed", "swa_q_ready", "swa_transposed", "swa_kT_ready", "swa_scores", "swa_dve",
            "swa_exp", "swa_pT_psum", "swa_pT_ready", "swa_values", "swa_sink_in"))
        with nc.Block() as block:
            @block.sync
            def _(sp):
                sp.dma_start(kv[0:127, :, :], cache[:, 1:128, :].rearrange("b t c -> t b c")).then_inc(s_in, 16)
                sp.dma_start(kv[127:128, :, :], new[:, 127:128, :].rearrange("b t c -> t b c")).then_inc(s_in, 16)
                for b in range(NB):
                    sp.dma_start(sm[b * CHD:(b + 1) * CHD, 0:1], i["c_sinks"].rearrange("l h -> h l"),
                                 allow_slow_non_contiguous=True).then_inc(s_sink, 16)
                sp.wait_ge(s_sink, 16 * NB)

            @block.vector
            def _(dve):
                link = Chain(dve, s_dve)
                dve.memset(qb[:, :, :], 0.0).then_inc(s_q0, 1)
                dve.wait_ge(s_q0, 1)
                for h in range(CHD):
                    g, base = h // 8, (h % 2) * HD
                    dst = bass.AP(qb.ap().tensor, qb[g * HD:g * HD + 1, 0, h:h + 1].offset,
                                  [[NB * NB * CHD, HD], [NB * CHD + CHD, NB]])
                    ins = dve.tensor_copy(dst, qT[base:base + HD, h // 2, T:TA])
                ins.then_inc(s_q, 1)
                for b in range(2):
                    dve.wait_ge(s_tr, b + 1)
                    dve.tensor_copy(kT[:, 4 * b:4 * b + 4, :], k.ps[:, b, :].rearrange("p (b c) -> p b c", b=4)).then_inc(s_kT, 1)
                dve.wait_ge(s_sc, 1)
                link(dve.tensor_tensor(sc[:, :], k.ps[:, 2, 0:P], k.b_swa[:, :], ALU.add))
                link(dve.tensor_reduce(sm[:, 1:2], sc[:, :], AX, ALU.max))
                dve.wait_ge(s_sink, 16 * NB)
                link(dve.tensor_tensor(sm[:, 1:2], sm[:, 1:2], sm[:, 0:1], ALU.max))
                link(dve.tensor_scalar(sm[:, 2:3], sm[:, 1:2], -1.0, None, ALU.mult))
                dve.wait_ge(s_act, 2)
                link(dve.tensor_tensor(sm[:, 5:6], sm[:, 3:4], sm[:, 4:5], ALU.add))
                link(dve.reciprocal(sm[:, 6:7], sm[:, 5:6]))
                link(dve.tensor_scalar(pr[:, :], pr[:, :], sm[:, 6:7], None, ALU.mult))
                dve.wait_ge(s_pTp, 1)
                dve.tensor_copy(pT[:, :], k.ps[:, 3, 0:P]).then_inc(s_pT, 1)
                dve.wait_ge(s_o, 1)
                for par in range(2):
                    src = k.ps[0:HD, 4, 0:P].rearrange("p (b f r) -> p f b r", b=NB, r=2)[:, :, :, par]
                    dve.tensor_copy(oT[par * HD:(par + 1) * HD, :, T:TA], src)

            @block.scalar
            def _(act):
                act.wait_ge(s_dve, 4)
                act.activation(pr[:, :], sc[:, :], ACT.Exp, bias=sm[:, 2:3], accum_out=sm[:, 3:4]).then_inc(s_act, 1)
                act.activation(sm[:, 4:5], sm[:, 0:1], ACT.Exp, bias=sm[:, 2:3]).then_inc(s_act, 1)

            @block.tensor
            def _(pe):
                pe.wait_ge(s_in, 32)
                for b in range(NB):
                    ins = pe.transpose(k.ps[:, b // 4, (b % 4) * P:(b % 4 + 1) * P], kv[:, b, 0:P], k.ident[:, :])
                    if b % 4 == 3:
                        ins.then_inc(s_tr, 1)
                pe.wait_ge(s_q, 1)
                pe.wait_ge(s_kT, 2)
                for b in range(NB):
                    ins = pe.matmul(k.ps[:, 2, 0:P], qb[:, b, :], kT[:, b, :], start=(b == 0), stop=(b == NB - 1))
                ins.then_inc(s_sc, 1)
                pe.wait_ge(s_dve, 7)
                pe.transpose(k.ps[:, 3, 0:P], pr[:, :], k.ident[:, :]).then_inc(s_pTp, 1)
                pe.wait_ge(s_pT, 1)
                for b in range(NB):
                    for g in range(G):
                        c0 = b * CHD + g * 8
                        ins = pe.matmul(k.ps[0:HD, 4, c0:c0 + 8], kv[:, b, P + g * HD:P + (g + 1) * HD],
                                        pT[:, c0:c0 + 8], start=True, stop=True)
                ins.then_inc(s_o, 1)


class S5Tensors:

    def __init__(self, k, st):
        new = lambda name, *shape: k.sb(st, "s5_" + name, [P] + list(shape))
        self.angles = k.sem("angles_ready")
        self.c1, self.c2 = new("c1", GRP * CG), new("c2", GRP * CG)
        self.wb1, self.wb2 = new("wb1", GRP, CG), new("wb2", GRP, CG)
        self.h1, self.h2 = new("h1", 256), new("h2", 256)
        self.pr, self.pi = new("pr", L + 1, GRP), new("pi", L + 1, GRP)
        self.mag8 = new("mag8", GRP)
        self.turns = new("turns", 7, 2, GRP)
        self.fin_c, self.fin_s = new("fin_c", GRP), new("fin_s", GRP)
        self.hnew = new("hnew", NB, GRP)
        self.swap = new("swap", P)


def stage_s5_params(k, s):
    nc, i = k.nc, k.i
    with ExitStack() as st:
        ar_rows = k.sb(st, "ar_rows", [GRP, 2, P])
        c_rows = k.sb(st, "c_rows", [P, 2, 4, P])
        h_rows = k.sb(st, "h_rows", [P, 2, 2, P])
        b1 = k.sb(st, "b1", [P, GRP, CG])
        b2 = k.sb(st, "b2", [P, GRP, CG])
        tmp = k.sb(st, "wb_tmp", [P, GRP, CG])
        names = ("logdt dt ar ai x mag th kk r rc c s m den am1 wr wi t1 t2").split()
        v = {n: k.sb(st, "s5_" + n, [P, GRP]) for n in names}
        s_rows, s_b, s_tr, s_dve, s_act, s_sw0, s_sw = (k.sem(x) for x in (
            "s5_rows_in", "s5_b_in", "s5_transposed", "s5_dve", "s5_act", "swap_zeroed", "swap_made"))
        flat = lambda name, pat: i[name][0].rearrange(pat)
        row_loads = []
        for n, name in enumerate(("s5_a_re", "s5_a_im")):
            row_loads += [(ar_rows[:, n, half * NS:(half + 1) * NS], i[name][0]) for half in range(2)]
        for n, name in enumerate(("s5_c_re", "s5_c_im")):
            src = flat(name, "g c p -> (g c) p").rearrange("(a r) p -> r a p", r=P)
            row_loads += [(c_rows[:, 0, :, n * NS:(n + 1) * NS], src), (c_rows[:, 1, :, (1 - n) * NS:(2 - n) * NS], src)]
        for n, name in enumerate(("state_s5_re", "state_s5_im")):
            src = flat(name, "b g p -> (b g) p").rearrange("(a r) p -> r a p", r=P)
            row_loads += [(h_rows[:, 0, :, n * NS:(n + 1) * NS], src), (h_rows[:, 1, :, (1 - n) * NS:(2 - n) * NS], src)]
        with nc.Block() as block:
            @block.sync
            def _(sp):
                for dst, src in row_loads:
                    sp.dma_start(dst, src).then_inc(s_rows, 16)
                sp.dma_start(v["logdt"][:, :], i["s5_log_dt"].broadcast_to([P, GRP])).then_inc(s_b, 16)
                for n, name in enumerate(("s5_b_re", "s5_b_im")):
                    src = flat(name, "g p c -> p g c")
                    sp.dma_start(b1[n * NS:(n + 1) * NS, :, :], src).then_inc(s_b, 16)
                    sp.dma_start(b2[(1 - n) * NS:(2 - n) * NS, :, :], src).then_inc(s_b, 16)
                sp.wait_ge(s_b, 80)

            @block.gpsimd
            def _(pool):
                pool.memset(s.swap[:, :], 0.0).then_inc(s_sw0, 1)
                pool.wait_ge(s_sw0, 1)
                pool.affine_select(out=s.swap[:, :], in_=s.swap[:, :], compare_op=ALU.not_equal, fill=-1.0,
                                   base=-NS, pattern=[[-1, P]], channel_multiplier=1).then_inc(s_sw0, 1)
                pool.wait_ge(s_sw0, 2)
                pool.affine_select(out=s.swap[:, :], in_=s.swap[:, :], compare_op=ALU.not_equal, fill=1.0,
                                   base=NS, pattern=[[-1, P]], channel_multiplier=1).then_inc(s_sw, 1)

            @block.tensor
            def _(pe):
                pe.wait_ge(s_rows, 16 * len(row_loads))
                for n in range(2):
                    pe.transpose(k.ps[:, 0, n * GRP:(n + 1) * GRP], ar_rows[:, n, :], k.ident[0:GRP, 0:GRP])
                    for a in range(4):
                        pe.transpose(k.ps[:, 1 + n, a * P:(a + 1) * P], c_rows[:, n, a, :], k.ident[:, :])
                    for a in range(2):
                        ins = pe.transpose(k.ps[:, 3 + n, a * P:(a + 1) * P], h_rows[:, n, a, :], k.ident[:, :])
                ins.then_inc(s_tr, 1)

            @block.vector
            def _(dve):
                link = Chain(dve, s_dve)
                vv = {n: v[n][:, :] for n in names}
                tt = lambda o, a, b, op: link(dve.tensor_tensor(vv[o], vv[a], vv[b], op))
                ts = lambda o, a, x, op, y=None, op2=ALU.bypass: link(dve.tensor_scalar(vv[o], vv[a], x, y, op, op2))
                dve.wait_ge(s_tr, 1)
                link(dve.tensor_copy(vv["ar"], k.ps[:, 0, 0:GRP]))
                link(dve.tensor_copy(vv["ai"], k.ps[:, 0, GRP:2 * GRP]))
                link(dve.tensor_copy(s.c1[0:NS, :], k.ps[0:NS, 1, :]))
                link(dve.tensor_scalar(s.c1[NS:P, :], k.ps[NS:P, 1, :], -1.0, None, ALU.mult))
                link(dve.tensor_scalar(s.c2[:, :], k.ps[:, 2, :], -1.0, None, ALU.mult))
                link(dve.tensor_copy(s.h1[:, :], k.ps[:, 3, 0:256]))
                link(dve.tensor_scalar(s.h2[0:NS, :], k.ps[0:NS, 4, 0:256], -1.0, None, ALU.mult))
                link(dve.tensor_copy(s.h2[NS:P, :], k.ps[NS:P, 4, 0:256]))
                dve.wait_ge(s_act, 1)
                tt("x", "ar", "dt", ALU.mult)
                tt("th", "ai", "dt", ALU.mult)
                two_pi, c1, c2 = 2 * np.pi, 6.28125, 4059 / 2 ** 21
                big = 1.5 * 2 ** 23
                ts("kk", "th", 1 / two_pi, ALU.mult, big, ALU.add)
                ts("kk", "kk", big, ALU.subtract)
                for part in (c1, c2, two_pi - c1 - c2):
                    link(dve.scalar_tensor_tensor(out=vv["r"], in0=vv["kk"], scalar=-float(part),
                                                  in1=vv["th" if part == c1 else "r"], op0=ALU.mult, op1=ALU.add))
                ts("rc", "r", np.pi / 2, ALU.add)
                ts("m", "rc", np.pi, ALU.is_gt, -two_pi, ALU.mult)
                tt("rc", "rc", "m", ALU.add)
                for x in ("r", "rc"):
                    ts(x, x, 3.1415925, ALU.min, -3.1415925, ALU.max)
                dve.sem_inc(s.angles, 1)
                dve.wait_ge(s_act, 5)
                pr = lambda n: s.pr[:, n, :]
                pi = lambda n: s.pi[:, n, :]
                link(dve.memset(pr(0), 1.0))
                link(dve.memset(pi(0), 0.0))
                link(dve.tensor_tensor(pr(1), vv["mag"], vv["c"], ALU.mult))
                link(dve.tensor_tensor(pi(1), vv["mag"], vv["s"], ALU.mult))
                ts("am1", "c", 1.0, ALU.mult)
                link(dve.tensor_scalar(vv["am1"], pr(1), 1.0, None, ALU.subtract))
                tt("den", "ar", "ar", ALU.mult)
                tt("t1", "ai", "ai", ALU.mult)
                tt("den", "den", "t1", ALU.add)
                link(dve.reciprocal(vv["den"], vv["den"]))
                tt("t1", "am1", "ar", ALU.mult)
                link(dve.tensor_tensor(vv["t2"], pi(1), vv["ai"], ALU.mult))
                tt("t1", "t1", "t2", ALU.add)
                tt("wr", "t1", "den", ALU.mult)
                link(dve.tensor_tensor(vv["t1"], pi(1), vv["ar"], ALU.mult))
                tt("t2", "am1", "ai", ALU.mult)
                tt("t1", "t1", "t2", ALU.subtract)
                tt("wi", "t1", "den", ALU.mult)
                for n in range(3 + 7):
                    tt("t1", "c", "c", ALU.mult)
                    tt("t2", "s", "s", ALU.mult)
                    tt("m", "t1", "t2", ALU.add)
                    ts("m", "m", -0.5, ALU.mult, 1.5, ALU.add)
                    tt("c", "c", "m", ALU.mult)
                    tt("s", "s", "m", ALU.mult)
                    if n >= 3:
                        link(dve.tensor_copy(s.turns[:, n - 3, 0, :], vv["c"]))
                        link(dve.tensor_copy(s.turns[:, n - 3, 1, :], vv["s"]))
                    tt("t1", "c", "c", ALU.mult)
                    tt("t2", "s", "s", ALU.mult)
                    tt("s", "c", "s", ALU.mult)
                    ts("s", "s", 2.0, ALU.mult)
                    tt("c", "t1", "t2", ALU.subtract)
                for n in range(1, L):
                    link(dve.tensor_tensor(pr(n + 1), pr(n), pr(1), ALU.mult))
                    link(dve.tensor_tensor(vv["t1"], pi(n), pi(1), ALU.mult))
                    link(dve.tensor_tensor(pr(n + 1), pr(n + 1), vv["t1"], ALU.subtract))
                    link(dve.tensor_tensor(pi(n + 1), pr(n), pi(1), ALU.mult))
                    link(dve.tensor_tensor(vv["t1"], pi(n), pr(1), ALU.mult))
                    link(dve.tensor_tensor(pi(n + 1), pi(n + 1), vv["t1"], ALU.add))
                dve.wait_ge(s_b, 80)
                link(dve.tensor_scalar(b2[0:NS, :, :], b2[0:NS, :, :], -1.0, None, ALU.mult))
                wr, wi = (bc(v[n][:, :], [[1, GRP], [0, CG]]) for n in ("wr", "wi"))
                link(dve.tensor_tensor(s.wb1[:, :, :], b1[:, :, :], wr, ALU.mult))
                link(dve.tensor_tensor(tmp[:, :, :], b2[:, :, :], wi, ALU.mult))
                link(dve.tensor_tensor(s.wb1[:, :, :], s.wb1[:, :, :], tmp[:, :, :], ALU.add))
                link(dve.tensor_tensor(s.wb2[:, :, :], b2[:, :, :], wr, ALU.mult))
                link(dve.tensor_tensor(tmp[:, :, :], b1[:, :, :], wi, ALU.mult))
                link(dve.tensor_tensor(s.wb2[:, :, :], s.wb2[:, :, :], tmp[:, :, :], ALU.subtract))

            @block.scalar
            def _(act):
                act.wait_ge(s_b, 80)
                act.activation(v["dt"][:, :], v["logdt"][:, :], ACT.Exp).then_inc(s_act, 1)
                act.wait_ge(s.angles, 1)
                act.activation(v["mag"][:, :], v["x"][:, :], ACT.Exp).then_inc(s_act, 1)
                act.activation(s.mag8[:, :], v["x"][:, :], ACT.Exp, scale=float(L)).then_inc(s_act, 1)
                act.activation(v["s"][:, :], v["r"][:, :], ACT.Sin).then_inc(s_act, 1)
                act.activation(v["c"][:, :], v["rc"][:, :], ACT.Sin).then_inc(s_act, 1)


def stage_s5_quarter(k, s, qd, u):
    nc = k.nc
    g0 = qd * QG
    NU = NC + NB
    with ExitStack() as st:
        big = lambda name: k.sb(st, name, [P, QG, P])
        ur = k.sb(st, "u_by_step", [P, L, NC])
        U = k.sb(st, "U", [P, QG, NU])
        V, V2, Q, Q2 = big("V"), big("V2"), big("Q"), big("Q2")
        Pm, Pm2, cos, sin = big("Pm"), big("Pm2"), big("cos"), big("sin")
        t1, xr, G = big("t1"), big("xr"), big("G")
        km = k.sb(st, "kernels", [P, P])
        Tm = k.sb(st, "Tm", [P, L, P])
        Tg = k.sb(st, "Tg", [P, QG, P])
        ys = k.sb(st, "y_samples", [CG, QG, NB])
        yb = k.sb(st, "y_samples_back", [P, NB])
        s_Tg = k.sem("T_grouped")
        gcos, gsin, Y, yback = V, V2, xr, ur
        s_ur, s_uw, s_u0, s_u, s_dve, s_tz, s_v, s_q, s_qc, s_km, s_kmc, s_T = (k.sem(x) for x in (
            "u_by_step_ready", "u_written", "u_zeroed", "u_in", "s5q_dve", "T_zeroed", "V_ready", "Q_psum", "Q_ready",
            "kernels_psum", "kernels_ready", "T_in"))
        s_x, s_g, s_y, s_yc, s_yw, s_yb, s_ysp, s_ysc, s_hs = (k.sem(x) for x in (
            "X_ready", "G_ready", "Y_psum", "Y_out", "Y_written", "Y_back", "ys_psum", "ys_ready", "hs_ready"))
        gs = slice(g0, g0 + QG)
        power = lambda t, n, step: bass.AP(t[:, n, g0:g0 + 1].tensor, t[:, n, g0:g0 + 1].offset,
                                           [list(t[:, n, g0:g0 + 1].ap[0]), [1, QG], [step * GRP, L], [0, CG]])
        chan = lambda ap: bc(ap, [[CG, QG], [0, L], [1, CG]])
        wb1, wb2 = chan(s.wb1[:, g0:g0 + 1, 0:1]), chan(s.wb2[:, g0:g0 + 1, 0:1])
        c1, c2 = chan(s.c1[:, g0 * CG:g0 * CG + 1]), chan(s.c2[:, g0 * CG:g0 * CG + 1])
        four = lambda t: t[:, :, :].rearrange("p g (j c) -> p g j c", c=CG)
        with nc.Block() as block:
            @block.scalar
            def _(act):
                act.copy(ur[:, :, :], u[:, 0:T].rearrange("p (n j) -> p j n", j=L)).then_inc(s_ur, 1)
                for b in range(4):
                    act.wait_ge(s_q, b + 1)
                    dst = (Q, Q2)[b // 2][:, 4 * (b % 2):4 * (b % 2) + 4, :]
                    act.copy(dst, k.ps[:, b, :].rearrange("p (g m) -> p g m", g=4)).then_inc(s_qc, 1)
                act.wait_ge(s_km, 1)
                act.copy(km[:, :], k.ps[:, 4, 0:P]).then_inc(s_kmc, 1)
                act.wait_ge(s_T, 16 * 36)
                act.copy(Tg[:, :, :].rearrange("p g (j c) -> p g j c", c=CG),
                         Tm[:, :, :].rearrange("p j (g c) -> p g j c", c=CG)).then_inc(s_Tg, 1)
                for b in range(2):
                    act.wait_ge(s_y, b + 1)
                    act.copy(Y[:, 4 * b:4 * b + 4, :], k.ps[:, 5 + b, :].rearrange("p (g n) -> p g n", g=4)).then_inc(s_yc, 1)
                act.wait_ge(s_ysp, 1)
                act.copy(ys[:, :, :], k.ps[0:CG, 7, 0:QG * NB].rearrange("p (g b) -> p g b", b=NB)).then_inc(s_ysc, 1)

            @block.sync
            def _(sp):
                sp.wait_ge(s_ur, 1)
                sp.dma_start(k.d_u[:, 0:L * NC], ur[:, :, :].rearrange("p j n -> p (j n)")).then_inc(s_uw, 16)
                sp.dma_start(k.d_u[:, L * NC:], u[:, T:TA]).then_inc(s_uw, 16)
                sp.wait_ge(s_uw, 32)
                sp.wait_ge(s_u0, 1)
                steps = k.d_u[:, 0:L * NC].rearrange("(g c) (j n) -> c g j n", c=CG, j=L)
                for j in range(L):
                    sp.dma_start(U[j * CG:(j + 1) * CG, :, 0:NC], steps[:, :, j, :]).then_inc(s_u, 16)
                sp.dma_start(U[(L - 1) * CG:L * CG, :, NC:NU],
                             k.d_u[:, L * NC:].rearrange("(g c) b -> c g b", c=CG)).then_inc(s_u, 16)
                sp.wait_ge(s_kmc, 1)
                sp.wait_ge(s_tz, 1)
                for jp in range(L):
                    for j in range(jp, L):
                        r = (L - 1 - (j - jp)) * CG
                        sp.dma_start(Tm[jp * CG:(jp + 1) * CG, j, :], km[r:r + CG, :]).then_inc(s_T, 16)
                sp.wait_ge(s_yc, 2)
                sp.dma_start(k.d_y, Y[:, :, :].rearrange("p g n -> p (g n)")).then_inc(s_yw, 16)
                sp.wait_ge(s_ysc, 1)
                sp.dma_start(k.d_ys.rearrange("(g c) b -> c g b", c=CG), ys[:, :, :]).then_inc(s_yw, 16)
                sp.wait_ge(s_yw, 32)
                back = k.d_y.rearrange("(j c) (g n) -> c g j n", c=CG, g=QG)
                for g in range(QG):
                    sp.dma_start(yback[g * CG:(g + 1) * CG, :, :], back[:, g, :, :]).then_inc(s_yb, 16)
                sp.dma_start(yb[:, :], k.d_ys).then_inc(s_yb, 16)
                sp.wait_ge(s_yb, 16 * (QG + 1))
                sp.wait_ge(s_T, 16 * 36)

            @block.vector
            def _(dve):
                link = Chain(dve, s_dve)
                dve.memset(U[:, :, NC:NU], 0.0).then_inc(s_u0, 1)
                dve.memset(Tm[:, :, :], 0.0).then_inc(s_tz, 1)

                def combine(out, pa, xa, pb_, xb, op):
                    link(dve.tensor_tensor(four(out), pa, xa, ALU.mult))
                    link(dve.tensor_tensor(four(t1), pb_, xb, ALU.mult))
                    link(dve.tensor_tensor(four(out), four(out), four(t1), op))

                r7, i7 = power(s.pr, L - 1, -1), power(s.pi, L - 1, -1)
                combine(V, r7, wb1, i7, wb2, ALU.add)
                dve.sem_inc(s_v, 1)
                combine(V2, i7, wb1, r7, wb2, ALU.subtract)
                dve.sem_inc(s_v, 1)
                r1, i1 = power(s.pr, 1, 1), power(s.pi, 1, 1)
                combine(Pm, r1, c1, i1, c2, ALU.add)
                combine(Pm2, r1, c2, i1, c1, ALU.subtract)
                link(dve.memset(cos[:, :, 0:1], 1.0))
                link(dve.memset(sin[:, :, 0:1], 0.0))
                for level in range(7):
                    m = 2 ** level
                    cc, cs = (bc(s.turns[:, level, n, g0:g0 + 1], [[1, QG], [0, m]]) for n in (0, 1))
                    lo_c, lo_s, tmp = cos[:, :, 0:m], sin[:, :, 0:m], t1[:, :, 0:m]
                    hi_c, hi_s = cos[:, :, m:2 * m], sin[:, :, m:2 * m]
                    link(dve.tensor_tensor(hi_c, lo_c, cc, ALU.mult))
                    link(dve.tensor_tensor(tmp, lo_s, cs, ALU.mult))
                    link(dve.tensor_tensor(hi_c, hi_c, tmp, ALU.subtract))
                    link(dve.tensor_tensor(hi_s, lo_c, cs, ALU.mult))
                    link(dve.tensor_tensor(tmp, lo_s, cc, ALU.mult))
                    link(dve.tensor_tensor(hi_s, hi_s, tmp, ALU.add))
                dve.wait_ge(s_x, 1)
                for b in range(3):
                    n = min(3, QG - 3 * b)
                    src = k.ps[:, b, 0:n * NU].rearrange("p (g n) -> p g n", n=NU)
                    link(dve.tensor_tensor(xr[:, 3 * b:3 * b + n, :], src[:, :, 0:NC], cos[:, 3 * b:3 * b + n, :], ALU.mult))
                for b in range(2):
                    src = k.ps[:, 3 + b, :].rearrange("p (g n) -> p g n", n=NC)
                    link(dve.tensor_tensor(t1[:, 4 * b:4 * b + 4, :], src, sin[:, 4 * b:4 * b + 4, :], ALU.mult))
                link(dve.tensor_tensor(xr[:, :, :], xr[:, :, :], t1[:, :, :], ALU.add))
                for g in range(QG):
                    ins = dve.tensor_tensor_scan(out=G[:, g, :], data0=s.mag8[:, g0 + g:g0 + g + 1].to_broadcast([P, NC]),
                                                 data1=xr[:, g, :], initial=0.0, op0=ALU.mult, op1=ALU.add)
                link(ins)
                dve.tensor_tensor(gcos[:, :, :], G[:, :, :], cos[:, :, :], ALU.mult)
                dve.tensor_tensor(gsin[:, :, :], G[:, :, :], sin[:, :, :], ALU.mult).then_inc(s_g, 1)
                dve.wait_ge(s_g, 1)
                dve.tensor_copy(s.fin_c[:, gs], gcos[:, :, NC - 1])
                dve.tensor_copy(s.fin_s[:, gs], gsin[:, :, NC - 1])
                hn = s.hnew[:, :, gs]
                h1 = s.h1[:, :].rearrange("p (b g) -> p b g", g=GRP)[:, :, gs]
                h2 = s.h2[:, :].rearrange("p (b g) -> p b g", g=GRP)[:, :, gs]
                a_r, a_i = (bc(t[:, 1, g0:g0 + 1], [[0, NB], [1, QG]]) for t in (s.pr, s.pi))
                tmp = t1[:, :, 0:NB]
                link(dve.tensor_tensor(hn, h1, a_r, ALU.mult))
                link(dve.tensor_tensor(tmp, h2, a_i, ALU.mult))
                link(dve.tensor_tensor(hn, hn, tmp, ALU.add))
                for b in range(3):
                    n = min(3, QG - 3 * b)
                    src = k.ps[:, b, 0:n * NU].rearrange("p (g n) -> p n g", n=NU)[:, NC:NU, :]
                    part = s.hnew[:, :, g0 + 3 * b:g0 + 3 * b + n]
                    link(dve.tensor_tensor(part, part, src, ALU.add))
                dve.sem_inc(s_hs, 1)
                dve.wait_ge(s_yb, 16 * (QG + 1))
                d = k.cols[:, C_D + qd:C_D + qd + 1]
                up = u[:, 0:T].rearrange("p (n j) -> p n j", j=L)
                dve.scalar_tensor_tensor(out=up, in0=up, scalar=d, in1=yback[:, :, :].rearrange("p j n -> p n j"),
                                         op0=ALU.mult, op1=ALU.add)
                dve.scalar_tensor_tensor(out=u[:, T:TA], in0=u[:, T:TA], scalar=d, in1=yb[:, :],
                                         op0=ALU.mult, op1=ALU.add)

            @block.tensor
            def _(pe):
                for b in range(4):
                    pe.wait_ge(s_v, b // 2 + 1)
                    for g in range(4):
                        src = (V, V2)[b // 2][:, 4 * (b % 2) + g, :]
                        ins = pe.transpose(k.ps[:, b, g * P:(g + 1) * P], src, k.ident[:, :])
                    ins.then_inc(s_q, 1)
                for g in range(QG):
                    ins = pe.matmul(k.ps[:, 4, g * CG:(g + 1) * CG], V[:, g, :], s.c1[:, (g0 + g) * CG:(g0 + g + 1) * CG],
                                    start=True, stop=True)
                ins.then_inc(s_km, 1)
                pe.wait_ge(s_qc, 4)
                pe.wait_ge(s_kmc, 1)
                pe.wait_ge(s_u, 16 * (L + 1))
                for g in range(QG):
                    pe.matmul(k.ps[:, g // 3, (g % 3) * NU:(g % 3 + 1) * NU], Q[:, g, :], U[:, g, :], start=True, stop=True)
                for g in range(QG):
                    ins = pe.matmul(k.ps[:, 3 + g // 4, (g % 4) * NC:(g % 4 + 1) * NC], Q2[:, g, :], U[:, g, 0:NC],
                                    start=True, stop=True)
                ins.then_inc(s_x, 1)
                pe.wait_ge(s_Tg, 1)
                pe.wait_ge(s_g, 1)
                for g in range(QG):
                    out = k.ps[:, 5 + g // 4, (g % 4) * NC:(g % 4 + 1) * NC]
                    pe.matmul(out, Tg[:, g, :], U[:, g, 0:NC], start=True, stop=False)
                    pe.matmul(out[:, 1:NC], Pm[:, g, :], gcos[:, g, 0:NC - 1], start=False, stop=False)
                    ins = pe.matmul(out[:, 1:NC], Pm2[:, g, :], gsin[:, g, 0:NC - 1], start=False, stop=True)
                    if g % 4 == 3:
                        ins.then_inc(s_y, 1)
                pe.wait_ge(s_hs, 1)
                for g in range(QG):
                    ins = pe.matmul(k.ps[0:CG, 7, g * NB:(g + 1) * NB], s.c1[:, (g0 + g) * CG:(g0 + g + 1) * CG],
                                    s.hnew[:, :, g0 + g], start=True, stop=True)
                ins.then_inc(s_ysp, 1)


def stage_s5_states(k, s):
    nc, o = k.nc, k.o
    with ExitStack() as st:
        fp = k.sb(st, "fin_rows", [GRP, P])
        hs = k.sb(st, "hs_rows", [P, 2, P])
        s_tr, s_c, s_w = k.sem("fin_psum"), k.sem("fin_out"), k.sem("fin_stored")
        with nc.Block() as block:
            @block.tensor
            def _(pe):
                pe.matmul(k.ps[0:GRP, 0, 0:P], s.fin_c[:, :], k.ident[:, :], start=True, stop=False)
                pe.matmul(k.ps[0:GRP, 0, 0:P], s.fin_s[:, :], s.swap[:, :], start=False, stop=True)
                h = s.hnew[:, :, :].rearrange("p b g -> p (b g)")
                pe.transpose(k.ps[:, 1, 0:P], h[:, 0:P], k.ident[:, :])
                pe.transpose(k.ps[:, 1, P:2 * P], h[:, P:2 * P], k.ident[:, :]).then_inc(s_tr, 1)

            @block.vector
            def _(dve):
                dve.wait_ge(s_tr, 1)
                dve.tensor_copy(fp[:, :], k.ps[0:GRP, 0, 0:P])
                dve.tensor_copy(hs[:, :, :], k.ps[:, 1, 0:2 * P].rearrange("p (a c) -> p a c", a=2)).then_inc(s_c, 1)

            @block.sync
            def _(sp):
                sp.wait_ge(s_c, 1)
                for n, part in enumerate(("re", "im")):
                    cs = slice(n * NS, (n + 1) * NS)
                    sp.dma_start(o[f"s5_{part}_prompt"][0, 0], fp[:, cs]).then_inc(s_w, 16)
                    dst = o[f"s5_{part}_sample"][0].rearrange("b g p -> (b g) p").rearrange("(a r) p -> r a p", r=P)
                    sp.dma_start(dst, hs[:, :, cs]).then_inc(s_w, 16)
                sp.wait_ge(s_w, 64)


def s5(k, uT):
    nc = k.nc
    with ExitStack() as st:
        k.recycle()
        s = S5Tensors(k, st)
        stage_s5_params(k, s)
        for qd in range(4):
            stage_s5_quarter(k, s, qd, uT[:, qd, :])
        stage_s5_states(k, s)
        k.recycle()
    with ExitStack() as st:
        sig = k.sb(st, "sig", [P, 4, TA])
        with nc.Block() as block:
            @block.scalar
            def _(act):
                for m in range(4):
                    act.activation(uT[:, m, :], uT[:, m, :], ACT.Gelu_apprx_tanh)
        zs = Split(k, st, "glu_in", [P, 4, TA])
        stage_split(k, zs, [uT[:, m, :] for m in range(4)])
        stage_linear(k, k.i["s5_w_glu"][0], 4, [(m * P, P) for m in range(4)], zs,
                     lambda m, c, ps: nc.scalar.activation(sig[:, m, c * CH:(c + 1) * CH], ps, ACT.Sigmoid,
                                                           bias=k.cols[:, C_BGLU + m:C_BGLU + m + 1]))
        with nc.Block() as block:
            @block.vector
            def _(dve):
                for m in range(4):
                    dve.tensor_tensor(uT[:, m, :], uT[:, m, :], sig[:, m, :], ALU.mult)


def stage_gates(k, gT, gates):
    nc = k.nc
    with ExitStack() as st:
        gs = k.sb(st, "gates_rows", [NB, 24])
        s_tr, s_c, s_w = k.sem("gates_psum"), k.sem("gates_out"), k.sem("gates_moved")
        with nc.Block() as block:
            @block.tensor
            def _(pe):
                for t in range(TT):
                    pe.transpose(k.ps[:, 0, t * 24:(t + 1) * 24], gT[:, t * P:(t + 1) * P], k.ident[0:24, 0:24])
                pe.transpose(k.ps[0:NB, 0, 192:216], gT[:, T:TA], k.ident[0:24, 0:24]).then_inc(s_tr, 1)

            @block.vector
            def _(dve):
                dve.wait_ge(s_tr, 1)
                dve.tensor_copy(gates[:, :, :], k.ps[:, 0, 0:192].rearrange("p (t c) -> p t c", c=24))
                dve.tensor_copy(gs[:, :], k.ps[0:NB, 0, 192:216]).then_inc(s_c, 1)

            @block.sync
            def _(sp):
                sp.wait_ge(s_c, 1)
                sp.dma_start(k.d_gates, gs[:, :]).then_inc(s_w, 16)
                sp.wait_ge(s_w, 16)
                sp.dma_start(k.gate_s[:, :], k.d_gates.rearrange("b (h c) -> (b h) c", c=3)).then_inc(s_w, 16)
                sp.wait_ge(s_w, 32)


def stage_compress_prompt(k, w2, posb, kvT, kc, vc):
    nc, i = k.nc, k.i
    with ExitStack() as st:
        w1s = k.sb(st, "w1s", [P, 2, 8, P])
        w1p = k.sb(st, "w1p", [P, 2, 16, P])
        hid = k.sb(st, "hidc", [HD, 4, 64])
        t1 = k.sb(st, "half1", [HD, 4, 64])
        s_w, s_u, s_t, s_hid, s_g, s_o = (k.sem(x) for x in (
            "w1_in", "u_psum", "half1_out", "hid_summed", "hidc_ready", "rows_psum"))
        loads = []
        for kv in range(2):
            w1 = i["nsa_cmp_w1"][0, kv]
            for r in range(2):
                half = w1[r * 1024:(r + 1) * 1024, :]
                loads.append((w1s[:, kv, :, r * HD:(r + 1) * HD], half.rearrange("(a p) h -> p a h", p=P)))
                for g in range(2):
                    loads.append((w1p[g * HD:(g + 1) * HD, kv, :, r * HD:(r + 1) * HD],
                                  half.rearrange("(s d) h -> d s h", d=HD)))
            loads.append((w2[:, kv, :], i["nsa_cmp_w2"][0, kv]))
        with nc.Block() as block:
            @block.sync
            def _(sp):
                for dst, src in loads:
                    sp.dma_start(dst, src).then_inc(s_w, 16)

            @block.tensor
            def _(pe):
                pe.wait_ge(s_w, 16 * len(loads))
                for kv in range(2):
                    for r in range(2):
                        for a in range(8):
                            c = C_POS + kv * 16 + r * 8 + a
                            ins = pe.matmul(k.ps[0:HD, 7, kv:kv + 1], w1s[:, kv, a, r * HD:(r + 1) * HD],
                                            k.cols[:, c:c + 1], start=(r == 0 and a == 0), stop=(r == 1 and a == 7))
                for x in range(4):
                    kv, g = x // 2, x % 2
                    gr = slice(g * HD, (g + 1) * HD)
                    for s in range(16):
                        ins = pe.matmul(k.ps[:, x, 0:64], w1p[gr, kv, s, :], kvT[gr, kv, s:T:16],
                                        start=(s == 0), stop=(s == 15))
                    ins.then_inc(s_u, 1)
                for x in range(4):
                    kv, g = x // 2, x % 2
                    pe.wait_ge(s_g, x + 1)
                    if kv == 0:
                        pe.matmul(k.ps[g * HD:(g + 1) * HD, 4, 0:NCK], w2[:, 0, :], hid[:, x, 0:NCK],
                                  start=True, stop=True)
                    else:
                        ins = pe.matmul(k.ps[0:NCK, 5, g * HD:(g + 1) * HD], hid[:, x, 0:NCK], w2[:, 1, :],
                                        start=True, stop=True)
                ins.then_inc(s_o, 1)

            @block.scalar
            def _(act):
                for x in range(4):
                    act.wait_ge(s_u, x + 1)
                    act.copy(t1[:, x, 0:NCK], k.ps[HD:P, x, 1:64]).then_inc(s_t, 1)
                for x in range(4):
                    act.wait_ge(s_hid, x + 1)
                    act.activation(hid[:, x, 0:NCK], hid[:, x, 0:NCK], ACT.Gelu_apprx_tanh,
                                   bias=posb[:, x // 2:x // 2 + 1]).then_inc(s_g, 1)

            @block.vector
            def _(dve):
                for x in range(4):
                    dve.wait_ge(s_t, x + 1)
                    if x == 0:
                        dve.tensor_copy(posb[:, :], k.ps[0:HD, 7, 0:2])
                    dve.tensor_tensor(hid[:, x, 0:NCK], k.ps[0:HD, x, 0:NCK], t1[:, x, 0:NCK], ALU.add).then_inc(s_hid, 1)
                dve.wait_ge(s_o, 1)
                dve.tensor_copy(kc[:, 0:NCK], k.ps[:, 4, 0:NCK])
                dve.tensor_copy(vc[0:NCK, :], k.ps[0:NCK, 5, 0:P])


def stage_sample_query(k, qT, qb):
    nc = k.nc
    s_z = k.sem("qb_zeroed")
    with nc.Block() as block:
        @block.vector
        def _(dve):
            dve.memset(qb[:, :, :], 0.0).then_inc(s_z, 1)
            dve.wait_ge(s_z, 1)
            for h in range(AH):
                g, base = h // 4, (h % 2) * HD
                first = qb[g * HD:g * HD + 1, 0, h:h + 1]
                dst = bass.AP(first.tensor, first.offset, [[NB * NB * AH, HD], [NB * AH + AH, NB]])
                dve.tensor_copy(dst, qT[base:base + HD, h // 2, T:TA])


class SampleSoftmax:

    def __init__(self, k, st, name):
        self.small = k.sb(st, name + "_small", [64, 4])
        self.s_max, self.s_exp = k.sem(name + "_max"), k.sem(name + "_exp")

    def maximum(self, dve, scores):
        dve.tensor_reduce(self.small[:, 0:1], scores, AX, ALU.max, negate=True).then_inc(self.s_max, 1)

    def exp(self, act, probs, scores):
        act.wait_ge(self.s_max, 1)
        act.activation(probs, scores, ACT.Exp, bias=self.small[:, 0:1], accum_out=self.small[:, 1:2]).then_inc(self.s_exp, 1)

    def normalise(self, dve, link, probs, gate):
        dve.wait_ge(self.s_exp, 1)
        link(dve.reciprocal(self.small[:, 2:3], self.small[:, 1:2]))
        if gate is not None:
            link(dve.tensor_tensor(self.small[:, 2:3], self.small[:, 2:3], gate, ALU.mult))
        link(dve.tensor_scalar(probs, probs, self.small[:, 2:3], None, ALU.mult))


def stage_window_sample(k, qb, oacc):
    nc, i = k.nc, k.i
    cache = i["cache_nsa_win"][0].rearrange("b t k g d -> b t (k g d)")
    new = k.o["nsa_win_sample"][0].rearrange("b t k g d -> b t (k g d)")
    with ExitStack() as st:
        kv = k.sb(st, "win_rows", [P, NB, 4, 4 * HD])
        kT = k.sb(st, "win_kT", [P, 2, 512])
        sc = k.sb(st, "win_scores", [64, 512])
        pT = k.sb(st, "win_pT", [P, 4, 64])
        sm = SampleSoftmax(k, st, "win")
        s_in, s_tr, s_kT, s_qk, s_dve, s_p, s_pTp, s_pT, s_o = (k.sem(x) for x in (
            "win_in", "win_tr", "win_kT_ready", "win_qk", "win_dve", "win_probs", "win_pT_psum", "win_pT_ready", "win_o"))
        with nc.Block() as block:
            @block.sync
            def _(sp):
                for b in range(NB):
                    sp.dma_start(kv[0:127, b, :, :].rearrange("p j c -> p (j c)"),
                                 cache[b, 1:509, :].rearrange("(p j) c -> p (j c)", j=4)).then_inc(s_in, 16)
                    sp.dma_start(kv[127:128, b, 0:3, :], cache[b:b + 1, 509:512, :]).then_inc(s_in, 16)
                    sp.dma_start(kv[127:128, b, 3, :], new[b:b + 1, 511, :]).then_inc(s_in, 16)

            @block.tensor
            def _(pe):
                pe.wait_ge(s_in, 48 * NB)
                for b in range(NB + 1):
                    if b < NB:
                        if b >= 2:
                            pe.wait_ge(s_kT, b - 1)
                        for j in range(4):
                            ins = pe.transpose(k.ps[:, b % 2, j * P:(j + 1) * P], kv[:, b, j, 0:P], k.ident[:, :])
                        ins.then_inc(s_tr, 1)
                    if b >= 1:
                        pe.wait_ge(s_kT, b)
                        pe.matmul(k.ps[0:64, 2, :], qb[:, b - 1, :], kT[:, (b - 1) % 2, :], start=(b == 1),
                                  stop=(b == NB)).then_inc(s_qk, 1)
                pe.wait_ge(s_p, 1)
                for j in range(4):
                    ins = pe.transpose(k.ps[:, 3, j * 64:(j + 1) * 64], sc[:, j * P:(j + 1) * P], k.ident[0:64, 0:64])
                ins.then_inc(s_pTp, 1)
                pe.wait_ge(s_pT, 1)
                for b in range(NB):
                    for g in range(G):
                        c0 = b * AH + g * 4
                        for j in range(4):
                            ins = pe.matmul(k.ps[0:HD, 4, c0:c0 + 4], kv[:, b, j, P + g * HD:P + (g + 1) * HD],
                                            pT[:, j, c0:c0 + 4], start=(j == 0), stop=(j == 3))
                ins.then_inc(s_o, 1)

            @block.scalar
            def _(act):
                sm.exp(act, sc[:, :], sc[:, :])

            @block.vector
            def _(dve):
                link = Chain(dve, s_dve)
                for b in range(NB):
                    dve.wait_ge(s_tr, b + 1)
                    if b >= 2:
                        dve.wait_ge(s_qk, b - 1)
                    dve.tensor_copy(kT[:, b % 2, :], k.ps[:, b % 2, :]).then_inc(s_kT, 1)
                dve.wait_ge(s_qk, NB)
                link(dve.tensor_tensor(sc[:, :], k.ps[0:64, 2, :], k.b_win[:, :], ALU.add))
                sm.maximum(dve, sc[:, :])
                sm.normalise(dve, link, sc[:, :], k.gate_s[:, 2:3])
                dve.sem_inc(s_p, 1)
                dve.wait_ge(s_pTp, 1)
                dve.tensor_copy(pT[:, :, :], k.ps[:, 3, 0:256].rearrange("p (j c) -> p j c", c=64)).then_inc(s_pT, 1)
                dve.wait_ge(s_o, 1)
                dve.tensor_copy(oacc[:, :], k.ps[0:HD, 4, 0:64])


def stage_index(k, idx):
    nc, i = k.nc, k.i
    with ExitStack() as st:
        pti = k.sb(st, "pages_int", [NB, NPAGE], I32)
        pt = k.sb(st, "pages", [NB, NPAGE])
        ptT = k.sb(st, "pagesT", [NPAGE + 1, NB])
        ex = k.sb(st, "expand", [NPAGE + 1, 2, P])
        s_in, s_c, s_t, s_tc, s_x, s_one = (k.sem(x) for x in (
            "pages_in", "pages_float", "pages_tr", "pagesT_ready", "idx_psum", "pagesT_ones"))
        with nc.Block() as block:
            @block.sync
            def _(sp):
                sp.dma_start(pti[:, :], i["page_table"]).then_inc(s_in, 16)
                sp.dma_start(ex[:, :, :], i["index_onehot"][0:NPAGE + 1, 0:2 * P].rearrange("a (h p) -> a h p", h=2)).then_inc(s_in, 16)

            @block.vector
            def _(dve):
                dve.memset(ptT[:, :], 1.0).then_inc(s_one, 1)
                dve.wait_ge(s_in, 32)
                dve.tensor_copy(pt[:, :], pti[:, :]).then_inc(s_c, 1)
                dve.wait_ge(s_t, 1)
                dve.wait_ge(s_one, 1)
                dve.tensor_copy(ptT[0:NPAGE, :], k.ps[0:NPAGE, 0, 0:NB]).then_inc(s_tc, 1)
                dve.wait_ge(s_x, 1)
                dve.tensor_copy(idx[:, :, :], k.ps[:, 1, 0:2 * NB].rearrange("p (h b) -> p h b", h=2))

            @block.tensor
            def _(pe):
                pe.wait_ge(s_c, 1)
                pe.transpose(k.ps[0:NPAGE, 0, 0:NB], pt[:, :], k.ident[0:NB, 0:NB]).then_inc(s_t, 1)
                pe.wait_ge(s_tc, 1)
                for h in range(2):
                    ins = pe.matmul(k.ps[:, 1, h * NB:(h + 1) * NB], ex[:, h, :], ptT[:, :], start=True, stop=True)
                ins.then_inc(s_x, 1)


def stage_compress_sample(k, idx, w2, posb, kc, vc):
    nc = k.nc
    table = k.i["cache_nsa_cmp"][0].rearrange("n (c s) k g d -> (n c) (s k g d)", s=16)
    units = [(b, h) for b in range(NB) for h in range(2)]
    with ExitStack() as st:
        w1s = k.sb(st, "w1s", [P, 2, 8, P])
        X = k.sb(st, "chunks", [P, 3, 16 * 4 * HD])
        R = k.sb(st, "grouped", [P, 2, 2, 16 * HD])
        xT = k.sb(st, "chunksT", [P, 4, 4, P])
        hid = k.sb(st, "hids", [HD, 2, 4, 256])
        t1 = k.sb(st, "half1s", [HD, 2, 256])
        s_in = [k.sem(f"chunks_in{n}") for n in range(3)]
        s_r = [k.sem("keys_grouped"), k.sem("values_grouped")]
        s_tr, s_u, s_z, s_t, s_hid, s_g, s_w2, s_kv = (k.sem(x) for x in (
            "chunksT_psum", "us_psum", "hids_zeroed", "half1s_out", "hids_summed", "hids_ready", "w2_done", "kv_out"))
        s_xT = [k.sem("chunksT_act"), k.sem("chunksT_dve")]
        s_w1 = k.sem("w1s_in")
        with nc.Block() as block:
            @block.sync
            def _(sp):
                for kv in range(2):
                    for r in range(2):
                        sp.dma_start(w1s[:, kv, :, r * HD:(r + 1) * HD],
                                     k.i["nsa_cmp_w1"][0, kv, r * 1024:(r + 1) * 1024, :].rearrange(
                                         "(a p) h -> p a h", p=P)).then_inc(s_w1, 16)

            @block.gpsimd
            def _(pool):
                for u, (b, h) in enumerate(units):
                    if u >= 3:
                        pool.wait_ge(s_r[0], u - 2)
                        pool.wait_ge(s_r[1], u - 2)
                    pool.indirect_dma_start(X[:, u % 3, :], None, table,
                                            bass.IndirectOffsetOnAxis(ap=idx[:, h, b:b + 1], axis=0)).then_inc(s_in[u % 3], 16)

            def regroup(eng, kv, u):
                eng.wait_ge(s_in[u % 3], 16 * (u // 3 + 1))
                if u >= 1:
                    eng.wait_ge(s_tr, 8 * (u - 1) + 4 * kv + 4)
                src = X[:, u % 3, :].rearrange("p (s k g d) -> p k g s d", k=2, g=2, d=HD)[:, kv]
                copy = eng.tensor_copy if kv else eng.copy
                copy(R[:, kv, :, :].rearrange("p g (s d) -> p g s d", d=HD), src).then_inc(s_r[kv], 1)

            def copy_out(eng, par, u):
                for q in range(8 * u + par, 8 * u + 8, 2):
                    eng.wait_ge(s_tr, q + 1)
                    if q >= 4:
                        eng.wait_ge(s_u, q - 3)
                    copy = eng.tensor_copy if par else eng.copy
                    copy(xT[:, q % 4, :, :], k.ps[:, q % 2, :].rearrange("p (a n) -> p a n", a=4)).then_inc(s_xT[par], 1)

            @block.tensor
            def _(pe):
                pe.wait_ge(s_w1, 16 * 4)

                def products(q):
                    u, x, half = q // 8, (q % 8) // 2, q % 2
                    b, h = units[u]
                    if h == 0 and half == 0 and b >= 1:
                        pe.wait_ge(s_hid, 4 * (b - 1) + x + 1)
                    pe.wait_ge(s_xT[q % 2], q // 2 + 1)
                    for a in range(4):
                        ins = pe.matmul(k.ps[:, 2 + x, h * P:(h + 1) * P], w1s[:, x // 2, 4 * half + a, :],
                                        xT[:, q % 4, a, :], start=(half == 0 and a == 0), stop=(half == 1 and a == 3))
                    ins.then_inc(s_u, 1)

                def second(b):
                    if b >= 1:
                        pe.wait_ge(s_kv, 2 * b)
                    for x in range(4):
                        kv, g = x // 2, x % 2
                        pe.wait_ge(s_g, 4 * b + x + 1)
                        if kv == 0:
                            ins = pe.matmul(k.ps[g * HD:(g + 1) * HD, 6, 0:256], w2[:, 0, :], hid[:, b % 2, x, :],
                                            start=True, stop=True)
                        else:
                            for h in range(2):
                                c0 = h * P + g * HD
                                ins = pe.matmul(k.ps[:, 7, c0:c0 + HD], hid[:, b % 2, x, h * P:(h + 1) * P], w2[:, 1, :],
                                                start=True, stop=True)
                        ins.then_inc(s_w2, 1)

                for q in range(8 * len(units) + 1):
                    if q < 8 * len(units):
                        u, x, half = q // 8, (q % 8) // 2, q % 2
                        pe.wait_ge(s_r[x // 2], u + 1)
                        if q >= 2:
                            pe.wait_ge(s_xT[q % 2], (q - 2) // 2 + 1)
                        for a in range(4):
                            c0 = (4 * half + a) * P
                            ins = pe.transpose(k.ps[:, q % 2, a * P:(a + 1) * P], R[:, x // 2, x % 2, c0:c0 + P], k.ident[:, :])
                        ins.then_inc(s_tr, 1)
                    if q >= 1:
                        products(q - 1)
                    if q % 16 == 8 and q >= 24:
                        second(q // 16 - 1)
                second(NB - 1)

            def hidden(eng, b, part):
                for x in range(4):
                    if part == "act":
                        eng.wait_ge(s_u, 16 * b + 8 + 2 * x + 2)
                        if 4 * b + x >= 2:
                            eng.wait_ge(s_hid, 4 * b + x - 1)
                        eng.copy(t1[:, x % 2, 0:255], k.ps[HD:P, 2 + x, 1:256]).then_inc(s_t, 1)
                    elif part == "dve":
                        eng.wait_ge(s_t, 4 * b + x + 1)
                        if b >= 2:
                            eng.wait_ge(s_w2, 4 * (b - 2) + x + 1)
                        eng.tensor_tensor(hid[:, b % 2, x, 0:255], k.ps[0:HD, 2 + x, 0:255], t1[:, x % 2, 0:255],
                                          ALU.add).then_inc(s_hid, 1)
                    else:
                        eng.wait_ge(s_hid, 4 * b + x + 1)
                        eng.activation(hid[:, b % 2, x, :], hid[:, b % 2, x, :], ACT.Gelu_apprx_tanh,
                                       bias=posb[:, x // 2:x // 2 + 1]).then_inc(s_g, 1)

            @block.scalar
            def _(act):
                act.wait_ge(s_z, 1)
                regroup(act, 0, 0)
                for u, (b, h) in enumerate(units):
                    copy_out(act, 0, u)
                    if u + 1 < len(units):
                        regroup(act, 0, u + 1)
                    if h == 1:
                        hidden(act, b, "act")
                        hidden(act, b, "gelu")

            @block.vector
            def _(dve):
                dve.memset(hid[:, :, :, 255:256], 0.0).then_inc(s_z, 1)
                dve.wait_ge(s_z, 1)

                def rows_out(b):
                    dve.wait_ge(s_w2, 4 * b + 4)
                    dve.tensor_copy(kc[:, b, :], k.ps[:, 6, 0:256]).then_inc(s_kv, 1)
                    dve.tensor_copy(vc[:, :, b, :], k.ps[:, 7, 0:256].rearrange("p (h c) -> p h c", h=2)).then_inc(s_kv, 1)

                regroup(dve, 1, 0)
                for u, (b, h) in enumerate(units):
                    if h == 1 and b >= 1:
                        rows_out(b - 1)
                    copy_out(dve, 1, u)
                    if u + 1 < len(units):
                        regroup(dve, 1, u + 1)
                    if h == 1:
                        hidden(dve, b, "dve")
                rows_out(NB - 1)


def stage_cmp_sample(k, qb, kc, vc, oacc, imp):
    nc = k.nc
    with ExitStack() as st:
        sc = k.sb(st, "cmp_scores", [64, 256])
        pr = k.sb(st, "cmp_probs", [64, 256])
        pT = k.sb(st, "cmp_pT", [P, 2, 2, 64])
        cover = k.sb(st, "cover", [P, 2, 64])
        gsum = k.sb(st, "group_sum", [64, 64])
        part = k.sb(st, "imp_part", [64, 64])
        sm = SampleSoftmax(k, st, "cmp")
        s_in, s_qk, s_dve, s_p, s_pTp, s_pT, s_o, s_ip, s_ic, s_im = (k.sem(x) for x in (
            "cover_in", "cmp_qk", "cmp_dve", "cmp_p", "cmp_pT_psum", "cmp_pT_ready", "cmp_o", "imp_psum", "imp_part_ready",
            "imp_sum"))
        with nc.Block() as block:
            @block.sync
            def _(sp):
                sp.dma_start(cover[:, :, :], k.i["index_onehot"][:, 384:512].rearrange("p (h s) -> p h s", h=2)).then_inc(s_in, 16)
                sp.dma_start(gsum[:, :], k.i["index_onehot"][0:64, 512:576]).then_inc(s_in, 16)

            @block.tensor
            def _(pe):
                for b in range(NB):
                    ins = pe.matmul(k.ps[0:64, 0, 0:NCS], qb[:, b, :], kc[:, b, 0:NCS], start=(b == 0), stop=(b == NB - 1))
                ins.then_inc(s_qk, 1)
                for n, src in enumerate((sc, pr)):
                    pe.wait_ge(s_p, n + 1)
                    for h in range(2):
                        ins = pe.transpose(k.ps[:, 1, (2 * n + h) * 64:(2 * n + h + 1) * 64], src[:, h * P:(h + 1) * P],
                                           k.ident[0:64, 0:64])
                ins.then_inc(s_pTp, 1)
                pe.wait_ge(s_pT, 1)
                pe.wait_ge(s_in, 32)
                for h in range(2):
                    ins = pe.matmul(k.ps[0:64, 2, 0:64], pT[:, 0, h, :], cover[:, h, :], start=(h == 0), stop=(h == 1))
                ins.then_inc(s_ip, 1)
                pe.wait_ge(s_ic, 1)
                pe.matmul(k.ps[0:64, 3, 0:64], gsum[:, :], part[:, :], start=True, stop=True).then_inc(s_im, 1)
                for b in range(NB):
                    for g in range(G):
                        c0 = b * AH + g * 4
                        for h in range(2):
                            ins = pe.matmul(k.ps[0:HD, 4, c0:c0 + 4], vc[:, h, b, g * HD:(g + 1) * HD],
                                            pT[:, 1, h, c0:c0 + 4], start=(h == 0), stop=(h == 1))
                ins.then_inc(s_o, 1)

            @block.scalar
            def _(act):
                sm.exp(act, sc[:, 0:NCS], k.ps[0:64, 0, 0:NCS])

            @block.vector
            def _(dve):
                link = Chain(dve, s_dve)
                link(dve.memset(sc[:, NCS:256], 0.0))
                dve.wait_ge(s_qk, 1)
                sm.maximum(dve, k.ps[0:64, 0, 0:NCS])
                sm.normalise(dve, link, sc[:, 0:NCS], None)
                dve.sem_inc(s_p, 1)
                link(dve.tensor_scalar(pr[:, :], sc[:, :], k.gate_s[:, 0:1], None, ALU.mult))
                dve.sem_inc(s_p, 1)
                dve.wait_ge(s_pTp, 1)
                dve.tensor_copy(pT[:, :, :, :], k.ps[:, 1, 0:256].rearrange("p (n h c) -> p n h c", n=2, h=2)).then_inc(s_pT, 1)
                dve.wait_ge(s_ip, 1)
                dve.tensor_copy(part[:, :], k.ps[0:64, 2, 0:64]).then_inc(s_ic, 1)
                dve.wait_ge(s_im, 1)
                link(dve.tensor_copy(imp[:, :], k.ps[0:64, 3, 0:64]))
                dve.tensor_scalar(imp[:, 0:64:63], imp[:, 0:64:63], 1000.0, None, ALU.add)
                dve.wait_ge(s_o, 1)
                dve.tensor_tensor(oacc[:, :], oacc[:, :], k.ps[0:HD, 4, 0:64], ALU.add)


def stage_select(k, imp, sidx, bias):
    nc, i = k.nc, k.i
    with ExitStack() as st:
        pti = k.sb(st, "ptb_int", [64, NPAGE], I32)
        pt = k.sb(st, "ptb", [64, NPAGE])
        top = k.sb(st, "top", [64, 16])
        left = k.sb(st, "left", [64, 64])
        tix = k.sb(st, "top_index", [64, 16], U32)
        pgi = k.sb(st, "page_int", [64, 2, 16], U32)
        blk = k.sb(st, "blockf", [64, 16])
        pg = k.sb(st, "page_par", [64, 2, 16])
        io_i = k.sb(st, "iota_int", [64, NPAGE], I32)
        io = k.sb(st, "iota_f", [64, NPAGE])
        hot = k.sb(st, "hot", [64, 16, NPAGE])
        base = k.sb(st, "base", [64, 16])
        e = k.sb(st, "is_near", [64, 2, 16])
        tmp = k.sb(st, "bias_tmp", [64, L, 16, 8])
        bT = k.sb(st, "baseT", [17, 64])
        ex = k.sb(st, "expand2", [17, P])
        s_in, s_io, s_dve, s_b, s_t, s_tc, s_x = (k.sem(x) for x in (
            "ptb_in", "iota_made", "sel_dve", "base_ready", "baseT_psum", "baseT_ready", "sidx_psum"))
        with nc.Block() as block:
            @block.sync
            def _(sp):
                for b in range(NB):
                    sp.dma_start(pti[b * AH:(b + 1) * AH, :], i["page_table"][b:b + 1, :].broadcast_to([AH, NPAGE])).then_inc(s_in, 16)
                sp.dma_start(ex[:, :], i["index_onehot"][0:17, 256:384]).then_inc(s_in, 16)

            @block.gpsimd
            def _(pool):
                pool.iota(io_i[:, :], pattern=[[1, NPAGE]], base=0, channel_multiplier=0).then_inc(s_io, 1)

            @block.vector
            def _(dve):
                link = Chain(dve, s_dve)
                link(dve.memset(bT[:, :], 1.0))
                link(dve.max(top[:, 0:8], imp[:, :]))
                link(dve.max_index(tix[:, 0:8], top[:, 0:8], imp[:, :]))
                link(dve.match_replace(left[:, :], top[:, 0:8], imp[:, :], NEG))
                link(dve.max(top[:, 8:16], left[:, :]))
                link(dve.max_index(tix[:, 8:16], top[:, 8:16], left[:, :]))
                link(dve.tensor_copy(blk[:, :], tix[:, :]))
                link(dve.tensor_scalar(pgi[:, 0, :], tix[:, :], 1, None, ALU.logical_shift_right))
                link(dve.tensor_scalar(pgi[:, 1, :], tix[:, :], 1, None, ALU.bitwise_and))
                link(dve.tensor_copy(pg[:, :, :], pgi[:, :, :]))
                dve.wait_ge(s_in, 16 * (NB + 1))
                dve.wait_ge(s_io, 1)
                link(dve.tensor_copy(pt[:, :], pti[:, :]))
                link(dve.tensor_copy(io[:, :], io_i[:, :]))
                link(dve.tensor_tensor(hot[:, :, :], bc(pg[:, 0, :], [[1, 16], [0, NPAGE]]), bc(io[:, :], [[0, 16], [1, NPAGE]]),
                                       ALU.is_equal))
                link(dve.tensor_tensor(hot[:, :, :], hot[:, :, :], bc(pt[:, :], [[0, 16], [1, NPAGE]]), ALU.mult))
                link(dve.tensor_reduce(base[:, :], hot[:, :, :], AX, ALU.add))
                link(dve.tensor_scalar(base[:, :], base[:, :], 16.0, None, ALU.mult))
                link(dve.scalar_tensor_tensor(out=base[:, :], in0=pg[:, 1, :], scalar=8.0, in1=base[:, :], op0=ALU.mult, op1=ALU.add))
                dve.sem_inc(s_b, 1)
                for n in range(2):
                    link(dve.tensor_scalar(e[:, n, :], blk[:, :], 62.0 + n, None, ALU.is_equal))
                for n in range(2):
                    near = bc(k.b_sel[:, n * 64:n * 64 + 1], [[8, L], [0, 16], [1, 8]])
                    which = bc(e[:, n, 0:1], [[0, L], [1, 16], [0, 8]])
                    link(dve.tensor_tensor((tmp, bias)[n][:, :, :, :], near, which, ALU.mult))
                link(dve.tensor_tensor(bias[:, :, :, :], bias[:, :, :, :], tmp[:, :, :, :], ALU.add))
                link(dve.memset(bias[:, :, 15, :], NEG))
                link(dve.tensor_copy(bias[:, 0, 15, 0:1], k.b_sel[:, 128:129]))
                dve.wait_ge(s_t, 1)
                dve.tensor_copy(bT[0:16, :], k.ps[0:16, 0, 0:64]).then_inc(s_tc, 1)
                dve.wait_ge(s_x, 1)
                dve.tensor_copy(sidx[:, :], k.ps[:, 1, 0:16])

            @block.tensor
            def _(pe):
                pe.wait_ge(s_b, 1)
                pe.transpose(k.ps[0:16, 0, 0:64], base[:, :], k.ident[0:64, 0:64]).then_inc(s_t, 1)
                pe.wait_ge(s_tc, 1)
                pe.matmul(k.ps[:, 1, 0:16], ex[:, :], bT[:, 0:64:4], start=True, stop=True).then_inc(s_x, 1)


def stage_sel_sample(k, qb, sidx, bias, oacc):
    nc = k.nc
    table = k.i["cache_nsa_sel"][0].rearrange("n (c s) k g d -> (n c) (s k g d)", s=8)
    new = kv_rows(k.o["nsa_sel_sample"])
    NX = 3
    n_u = 2 * NB
    with ExitStack() as st:
        X = k.sb(st, "sel_rows", [P, NX, 8, 4 * HD])
        V = k.sb(st, "sel_v", [P, n_u, 8, HD])
        kT = k.sb(st, "sel_kT", [P, 2, 1024])
        sc = k.sb(st, "sel_scores", [64, 1024])
        pT = k.sb(st, "sel_pT", [P, 8, 64])
        sm = SampleSoftmax(k, st, "sel")
        s_in = [k.sem(f"sel_in{n}") for n in range(NX)]
        s_new = [k.sem(f"sel_new{n}") for n in range(NX)]
        s_z, s_tr, s_kT, s_v, s_qk, s_dve, s_p, s_pTp, s_pT, s_o = (k.sem(x) for x in (
            "sel_zeroed", "sel_tr", "sel_kT_ready", "sel_v_ready", "sel_qk", "sel_dve", "sel_probs", "sel_pT_psum",
            "sel_pT_ready", "sel_o"))
        with nc.Block() as block:
            @block.gpsimd
            def _(pool):
                pool.wait_ge(s_z, 1)
                for u in range(n_u):
                    if u >= NX:
                        pool.wait_ge(s_tr, u - NX + 1)
                        pool.wait_ge(s_v, u - NX + 1)
                    pool.indirect_dma_start(X[0:120, u % NX, :, :].rearrange("p j c -> p (j c)"), None, table,
                                            bass.IndirectOffsetOnAxis(ap=sidx[0:120, u:u + 1], axis=0)).then_inc(s_in[u % NX], 16)

            @block.sync
            def _(sp):
                sp.wait_ge(s_z, 1)
                for u in range(n_u):
                    if u >= NX:
                        sp.wait_ge(s_tr, u - NX + 1)
                        sp.wait_ge(s_v, u - NX + 1)
                    sp.dma_start(X[120:121, u % NX, 0, :], new[u // 2:u // 2 + 1, :]).then_inc(s_new[u % NX], 16)

            @block.tensor
            def _(pe):
                def scores(b):
                    pe.wait_ge(s_kT, 2 * b + 2)
                    for c in range(2):
                        ins = pe.matmul(k.ps[0:64, 4 + c, :], qb[:, b, :], kT[:, b % 2, c * 512:(c + 1) * 512],
                                        start=(b == 0), stop=(b == NB - 1))
                    ins.then_inc(s_qk, 1)

                for u in range(n_u):
                    pe.wait_ge(s_in[u % NX], 16 * (u // NX + 1))
                    pe.wait_ge(s_new[u % NX], 16 * (u // NX + 1))
                    if u >= 2:
                        pe.wait_ge(s_kT, u - 1)
                    for j in range(8):
                        bank = 2 * (u % 2) + j // 4
                        ins = pe.transpose(k.ps[:, bank, (j % 4) * P:(j % 4 + 1) * P], X[:, u % NX, j, 0:P], k.ident[:, :])
                    ins.then_inc(s_tr, 1)
                    if u % 2 == 0 and u >= 2:
                        scores(u // 2 - 1)
                scores(NB - 1)
                pe.wait_ge(s_p, 1)
                for j in range(8):
                    ins = pe.transpose(k.ps[:, 6, j * 64:(j + 1) * 64], sc[:, j * P:(j + 1) * P], k.ident[0:64, 0:64])
                ins.then_inc(s_pTp, 1)
                pe.wait_ge(s_pT, 1)
                pe.wait_ge(s_v, n_u)
                for u in range(n_u):
                    for j in range(8):
                        ins = pe.matmul(k.ps[0:HD, 7, u * 4:u * 4 + 4], V[:, u, j, :], pT[:, j, u * 4:u * 4 + 4],
                                        start=(j == 0), stop=(j == 7))
                ins.then_inc(s_o, 1)

            @block.scalar
            def _(act):
                for u in range(n_u):
                    act.wait_ge(s_in[u % NX], 16 * (u // NX + 1))
                    act.wait_ge(s_new[u % NX], 16 * (u // NX + 1))
                    act.copy(V[:, u, :, :], X[:, u % NX, :, P + (u % 2) * HD:P + (u % 2 + 1) * HD]).then_inc(s_v, 1)
                sm.exp(act, sc[:, :], sc[:, :])

            @block.vector
            def _(dve):
                link = Chain(dve, s_dve)
                dve.memset(X[96:P, :, :, :], 0.0).then_inc(s_z, 1)
                for u in range(n_u):
                    b, g = u // 2, u % 2
                    dve.wait_ge(s_tr, u + 1)
                    if b >= 2:
                        dve.wait_ge(s_qk, b - 1)
                    dve.tensor_copy(kT[g * HD:(g + 1) * HD, b % 2, :],
                                    k.ps[g * HD:(g + 1) * HD, 2 * g:2 * g + 2, :].rearrange("p a c -> p (a c)")).then_inc(s_kT, 1)
                dve.wait_ge(s_qk, NB)
                link(dve.tensor_tensor(sc[:, :], k.ps[0:64, 4:6, :].rearrange("p a c -> p (a c)"),
                                       bias[:, :, :, :].rearrange("p j s c -> p (j s c)"), ALU.add))
                sm.maximum(dve, sc[:, :])
                sm.normalise(dve, link, sc[:, :], k.gate_s[:, 1:2])
                dve.sem_inc(s_p, 1)
                dve.wait_ge(s_pTp, 1)
                dve.tensor_copy(pT[:, :, :], k.ps[:, 6, :].rearrange("p (j c) -> p j c", c=64)).then_inc(s_pT, 1)
                dve.wait_ge(s_o, 1)
                dve.tensor_tensor(oacc[:, :], oacc[:, :], k.ps[0:HD, 7, 0:64], ALU.add)


def stage_place_sample(k, oacc, oT):
    nc = k.nc
    with nc.Block() as block:
        @block.vector
        def _(dve):
            for par in range(2):
                src = oacc[:, :].rearrange("p (b f r) -> p f b r", b=NB, r=2)[:, :, :, par]
                dve.tensor_copy(oT[par * HD:(par + 1) * HD, :, T:TA], src)


def kv_rows(ap):
    return ap.rearrange("l b t k g d -> (l b t) (k g d)")


def layer_a(k):
    nc = k.nc
    i, o = k.i, k.o
    with ExitStack() as st:
        uT = k.sb(st, "uT", [P, 4, TA])
        gT = k.sb(st, "gT", [24, TA])
        w2 = k.sb(st, "w2c", [HD, 2, HD])
        posb = k.sb(st, "posb", [HD, 2])
        qb = k.sb(st, "qb", [P, NB, NB * AH])
        k.gate_s = k.sb(st, "gate_s", [64, 3])
        with ExitStack() as st1:
            qT = k.sb(st1, "qT", [P, 4, TA])
            kvT = k.sb(st1, "kvT", [P, 6, TA])
            with ExitStack() as st2:
                xs = Split(k, st2, "xa", [P, KD, TA])
                stage_norm(k, xs, C_MIX)
                tiles = [(m * P, P) for m in range(10)] + [(1280, 24)] + [(1304 + m * P, P) for m in range(4)]

                def put(m, c, ps):
                    cs = slice(c * CH, (c + 1) * CH)
                    if m < 4:
                        return nc.scalar.copy(qT[:, m, cs], ps)
                    if m < 10:
                        return nc.scalar.copy(kvT[:, m - 4, cs], ps)
                    if m == 10:
                        return nc.scalar.activation(gT[:, cs], ps, ACT.Sigmoid)
                    return nc.scalar.copy(uT[:, m - 11, cs], ps)

                stage_linear(k, i["a_w_in"][0], KD, tiles, xs, put)
            s5(k, uT)
            gq, gk = C_GAIN, C_GAIN + 1
            stage_head_norm(k, [(qT[:, n, :], gq, True) for n in range(4)]
                            + [(kvT[:, n, :], gk, False) for n in (0, 2, 4)])
            stage_sample_query(k, qT, qb)
            k.recycle()
            with ExitStack() as st2:
                tok = k.sb(st2, "kvrows", [P, TT, 6, P])
                gates = k.sb(st2, "gates", [P, TT, 24])
                kc = k.sb(st2, "kc_prompt", [P, 64])
                vc = k.sb(st2, "vc_prompt", [64, P])
                keys = [KeySplit(k, st2, name, width) for name, width in (("k_cmp", 64), ("k_sel", T), ("k_win", T))]
                with ExitStack() as st3:
                    stok = k.sb(st3, "kvrows_s", [NB, 6, P])
                    stores = []
                    for br, name in enumerate(("cmp", "sel", "win")):
                        t0 = 4 if name == "win" else 0
                        dst = kv_rows(o[f"nsa_{name}_prompt"])
                        for t in range(t0, TT):
                            stores.append((dst[(t - t0) * P:(t - t0 + 1) * P, :], tok[:, t, 2 * br:2 * br + 2, :]))
                    win = o["nsa_win_sample"][0].rearrange("b t k g d -> b t (k g d)")
                    stores.append((kv_rows(o["nsa_cmp_sample"]), stok[:, 0:2, :]))
                    stores.append((kv_rows(o["nsa_sel_sample"]), stok[:, 2:4, :]))
                    stores.append((win[:, 511, :], stok[:, 4:6, :]))
                    stores.append((win[:, 0:511, :], i["cache_nsa_win"][0, :, 1:512].rearrange("b t k g d -> b t (k g d)")))
                    stage_rows(k, [kvT[:, n, :] for n in range(6)], tok, stok, stores)
                stage_gates(k, gT, gates)
                stage_compress_prompt(k, w2, posb, kvT, kc, vc)
                stage_head_norm(k, [(kc[:, 0:NCK], gk, False)])
                stage_split_keys(k, [(keys[0], kc[:, 0:NCK]), (keys[1], kvT[:, 2, 0:T]), (keys[2], kvT[:, 4, 0:T])])
                head = lambda g: slice(g * HD, (g + 1) * HD)
                branches = [
                    dict(kind="cmp", k=keys[0], v=lambda t, g: vc[0:NCK, head(g)]),
                    dict(kind="sel", k=keys[1], first=lambda q: 0,
                         v=lambda t, g: tok[:, t, 3, head(g)]),
                    dict(kind="win", k=keys[2], first=lambda q: max(0, q - 4),
                         v=lambda t, g: tok[:, t, 5, head(g)])]
                k.recycle()
                stage_attend(k, qT, AH, branches, qT, gates)
                stage_move(k, [(k.d_o.rearrange("p (f t) -> p f t", f=4), qT[:, :, 0:T])])
        oT = k.sb(st, "oT", [P, 4, TA])
        oacc = k.sb(st, "oacc", [HD, NB * AH])
        stage_move(k, [(oT[:, :, 0:T], k.d_o.rearrange("p (f t) -> p f t", f=4))])
        stage_window_sample(k, qb, oacc)
        k.recycle()
        with ExitStack() as st1:
            idx = k.sb(st1, "chunk_index", [P, 2, NB], U32)
            imp = k.sb(st1, "imp", [64, 64])
            sidx = k.sb(st1, "sel_index", [P, 16], U32)
            bias = k.sb(st1, "sel_bias", [64, L, 16, 8])
            stage_index(k, idx)
            with ExitStack() as st2:
                kc = k.sb(st2, "kc_sample", [P, NB, 256])
                vc = k.sb(st2, "vc_sample", [P, 2, NB, P])
                stage_compress_sample(k, idx, w2, posb, kc, vc)
                stage_head_norm(k, [(kc[:, :, :].rearrange("p b n -> p (b n)"), C_GAIN + 1, False)])
                stage_cmp_sample(k, qb, kc, vc, oacc, imp)
            stage_select(k, imp, sidx, bias)
            k.recycle()
            stage_sel_sample(k, qb, sidx, bias, oacc)
        stage_place_sample(k, oacc, oT)
        os = Split(k, st, "ao", [P, KD, TA])
        stage_split(k, os, [oT[:, m, :] for m in range(4)] + [uT[:, m, :] for m in range(4)])
        stage_residual(k, i["a_w_out"][0], os)


def stage_move(k, moves):
    s_m = k.sem("moved")
    with k.nc.Block() as block:
        @block.sync
        def _(sp):
            for dst, src in moves:
                sp.dma_start(dst, src).then_inc(s_m, 16)
            sp.wait_ge(s_m, 16 * len(moves))


def build(nc, ins, outs):
    with ExitStack() as ctx:
        k = Core(nc, ctx, ins, outs)
        k.ident = k.sb(ctx, "ident", [P, P])
        k.ones = k.sb(ctx, "ones", [P, P])
        k.headones = k.sb(ctx, "headones", [P, P])
        k.eps = k.sb(ctx, "eps", [P, 1])
        k.cols = k.sb(ctx, "cols", [P, N_COLA + 2 * N_CW])
        k.tab = k.sb(ctx, "tab", [33, CHD])
        k.sink = k.sb(ctx, "sink", [P, 2, CHD])
        k.b_win = k.sb(ctx, "b_win", [64, 512])
        k.b_swa = k.sb(ctx, "b_swa", [P, P])
        k.b_sel = k.sb(ctx, "b_sel", [64, 129])
        k.hT = k.sb(ctx, "hT", [P, KD, TA])
        k.ps = ctx.enter_context(nc.psum_tensor("ps", [P, 8, 512], F32))
        k.d_toep = nc.dram_tensor("toeplitz", [CHD, P, 384], F32, kind="Internal").ap()
        k.d_gates = nc.dram_tensor("gates_s", [NB, 24], F32, kind="Internal").ap()
        k.d_o = nc.dram_tensor("o_prompt", [P, 4 * T], F32, kind="Internal").ap()
        k.d_u = nc.dram_tensor("s5_u", [P, L * NC + NB], F32, kind="Internal").ap()
        k.d_y = nc.dram_tensor("s5_y", [P, QG * NC], F32, kind="Internal").ap()
        k.d_ys = nc.dram_tensor("s5_ys", [P, NB], F32, kind="Internal").ap()
        s_eps = k.sem("eps_set")
        with nc.Block() as block:
            @block.vector
            def _(dve):
                dve.memset(k.eps[:, :], EPS).then_inc(s_eps, 1)
        stage_setup(k)
        layer_a(k)
        k.recycle()
        ffn(k, 0)
        k.recycle()
        layer_c(k)
        k.recycle()
        ffn(k, 1)
        stage_finish(k)


def bucket_onehot():
    def bucket(n):
        n = np.maximum(n, 0)
        nf = np.maximum(n, 16).astype(np.float32)
        large = 16 + (np.log(nf / np.float32(16)) / np.float32(np.log(8.0)) * np.float32(16)).astype(np.int32)
        return np.where(n < 16, n, np.minimum(large, 31))

    def cols(dist, relative_to_far, mask=None):
        m = np.zeros((33, dist.size), np.float32)
        m[bucket(dist), np.arange(dist.size)] = 1.0
        if relative_to_far:
            m[31] -= 1.0
        if mask is not None:
            m[:32, mask] = 0.0
            m[32, mask] = NEG
        return m

    d = 255 - np.arange(384)
    j, p = np.divmod(np.arange(512), 128)
    j8, p8 = np.divmod(np.arange(64), 8)
    pos = p8 * 8 + j8
    return np.concatenate([
        cols(d, True, d < 0),
        cols(511 - 4 * p - j, False),
        cols(127 - np.arange(128), False),
        cols(128 - pos, True), cols(64 - pos, True), cols(np.zeros(1, np.int64), True)], axis=1)


def index_onehot():
    m = np.zeros((128, 576), np.float32)
    p = np.arange(128)
    for half in range(2):
        m[half * 16 + p // 8, half * 128 + p] = 8.0
        m[32, half * 128 + p] = p % 8
    m[p // 8, 256 + p] = 1.0
    m[16, 256 + p] = p % 8
    for half in range(2):
        n = half * 128 + p[:, None]
        s = np.arange(64)[None, :]
        m[:, 384 + half * 64:448 + half * 64] = (16 * n < 64 * s + 64) & (16 * n + 31 >= 64 * s) & (n < NCS)
    h = np.arange(64)
    m[:64, 512:] = h[:, None] // 4 == h[None, :] // 4
    return m


_INS = ["x_prompt", "x_sample", "cache_nsa_cmp", "cache_nsa_sel", "cache_nsa_win", "state_s5_re", "state_s5_im",
        "cache_swa", "state_ffn_conv", "page_table", "rel_bias", "norm_mix", "norm_ffn", "a_w_in", "a_w_out",
        "nsa_q_gain", "nsa_k_gain", "nsa_cmp_pos", "nsa_cmp_w1", "nsa_cmp_w2", "s5_a_re", "s5_a_im", "s5_log_dt",
        "s5_b_re", "s5_b_im", "s5_c_re", "s5_c_im", "s5_d", "s5_w_glu", "s5_b_glu", "c_w_in", "c_w_out",
        "c_q_gain", "c_k_gain", "c_sinks", "ffn_w_up", "ffn_w_gate", "ffn_conv_w", "ffn_conv_b", "ffn_w_down"]
_OUTS = [("y_prompt", (1, T, D)), ("y_sample", (NB, 1, D)),
         ("nsa_cmp_prompt", (1, 1, T, 2, G, HD)), ("nsa_cmp_sample", (1, NB, 1, 2, G, HD)),
         ("nsa_sel_prompt", (1, 1, T, 2, G, HD)), ("nsa_sel_sample", (1, NB, 1, 2, G, HD)),
         ("nsa_win_prompt", (1, 1, 512, 2, G, HD)), ("nsa_win_sample", (1, NB, 512, 2, G, HD)),
         ("s5_re_prompt", (1, 1, GRP, NS)), ("s5_im_prompt", (1, 1, GRP, NS)),
         ("s5_re_sample", (1, NB, GRP, NS)), ("s5_im_sample", (1, NB, GRP, NS)),
         ("swa_prompt", (1, 1, 128, 2, 2, HD)), ("swa_sample", (1, NB, 128, 2, 2, HD)),
         ("ffn_conv_prompt", (2, 1, 2, DFF)), ("ffn_conv_sample", (2, NB, 2, DFF))]


def kernel(**inputs):
    import concourse.bacc as _bacc
    from concourse.bass_utils import run_bass_kernel_spmd as _run

    nc = _bacc.Bacc("TRN2", target_bir_lowering=False, num_devices=1)
    arrays, ins = {}, {}
    constants = {"bucket_onehot": bucket_onehot(), "index_onehot": index_onehot()}
    for name in _INS + list(constants):
        a = constants[name] if name in constants else np.ascontiguousarray(inputs[name])
        arrays[f"in_{name}_dram"] = a
        ins[name] = nc.dram_tensor(f"in_{name}_dram", a.shape, mybir.dt.from_np(a.dtype), kind="ExternalInput").ap()
    outs = {name: nc.dram_tensor(f"out_{name}", shape, F32, kind="ExternalOutput").ap() for name, shape in _OUTS}
    build(nc, ins, outs)
    r = _run(nc, [arrays], core_ids=[0])
    return tuple(r.results[0][f"out_{name}"] for name, _ in _OUTS)
```
